# Optimizing a Trainium2 kernel written in Bass

```python
import jax, jax.numpy as jnp
from jax import lax
import numpy as np

D_MODEL = 1024
BATCH = 1
SEQ = 256
DEPTH = 1
DEC_BATCH = 8
DEC_SEQ = 4
PAST_LEN = 2048
PAGE_SIZE = 128

GDN_HEADS = 8
GDN_DK = 128
GDN_DV = 128
GDN_CONV = 4
GDN_CHUNK = 64
QK_W = GDN_HEADS * GDN_DK
V_W = GDN_HEADS * GDN_DV
QKV_W = 2 * QK_W + V_W
CONF_DIM = D_MODEL
CONF_WIDTH = 31
MEM_LEN = 256
XA_HEADS = 4
XA_DH = D_MODEL // XA_HEADS
N_EXPERTS = 32
TOP_K = 4
D_FF = D_MODEL
SWIGLU_ALPHA = 1.702
SWIGLU_LIMIT = 7.0
SPLITS = (QKV_W, QKV_W + V_W, QKV_W + V_W + GDN_HEADS, QKV_W + V_W + 2 * GDN_HEADS,
          QKV_W + V_W + 2 * GDN_HEADS + 2 * CONF_DIM)
N_IN = SPLITS[-1] + 2 * D_MODEL

kernel_name = "hybrid_gdn_conformer_memxattn_moe_step"

def rms_norm(x, g, eps=1e-6):
    xf = x.astype(jnp.float32)
    y = xf * lax.rsqrt(jnp.mean(xf * xf, axis=-1, keepdims=True) + eps)
    return (y * g.astype(jnp.float32)).astype(x.dtype)

def layer_norm(x, g, b, eps=1e-5):
    xf = x.astype(jnp.float32)
    mu = jnp.mean(xf, axis=-1, keepdims=True)
    xc = xf - mu
    var = jnp.mean(xc * xc, axis=-1, keepdims=True)
    return (xc * lax.rsqrt(var + eps) * g.astype(jnp.float32) + b.astype(jnp.float32)).astype(x.dtype)

def l2_normalize(x, eps=1e-6):
    return x * lax.rsqrt(jnp.sum(x * x, axis=-1, keepdims=True) + eps)

def causal_dwconv(x, buf, w):
    ext = jnp.concatenate([buf.astype(x.dtype), x], axis=1)
    y = lax.conv_general_dilated(ext, w[:, None, :].astype(x.dtype), window_strides=(1,), padding="VALID",
                                 dimension_numbers=("NWC", "WIO", "NWC"), feature_group_count=x.shape[-1])
    return y, ext[:, -(w.shape[0] - 1):]

def gated_delta_chunked(q, k, v, g, beta, s0):
    bsz, t_len, n_h, _ = q.shape
    d_v = v.shape[-1]
    c = min(GDN_CHUNK, t_len)
    n_c = -(-t_len // c)
    pad = n_c * c - t_len
    if pad:
        padw = lambda a: jnp.pad(a, [(0, 0), (0, pad)] + [(0, 0)] * (a.ndim - 2))
        q, k, v, g, beta = padw(q), padw(k), padw(v), padw(g), padw(beta)

    def blocks(a):
        return jnp.moveaxis(a.reshape((bsz, n_c, c) + a.shape[2:]), 3, 1)

    q, k, v, g, beta = blocks(q), blocks(k), blocks(v), blocks(g), blocks(beta)
    gc = jnp.cumsum(g, axis=-1)
    incl = jnp.tril(jnp.ones((c, c), dtype=bool))
    strict = jnp.tril(jnp.ones((c, c), dtype=bool), -1)
    diff = gc[..., :, None] - gc[..., None, :]
    decay = jnp.where(incl, jnp.exp(jnp.where(incl, diff, 0.0)), 0.0)
    kb = k * beta[..., None]
    m = jnp.where(strict, jnp.einsum("bhncd,bhnsd->bhncs", kb, k) * decay, 0.0)
    a_mat = m + jnp.eye(c, dtype=m.dtype)
    rhs = jnp.concatenate([v * beta[..., None], kb * jnp.exp(gc)[..., None]], axis=-1)
    sol = lax.linalg.triangular_solve(a_mat, rhs, left_side=True, lower=True, unit_diagonal=True)
    u, w = sol[..., :d_v], sol[..., d_v:]
    p_intra = jnp.einsum("bhncd,bhnsd->bhncs", q, k) * decay

    def step(s, xs):
        qc, kc, uc, wc, gcc, pc = xs
        v_new = uc - jnp.einsum("bhcd,bhde->bhce", wc, s)
        o = (jnp.einsum("bhcd,bhde->bhce", qc * jnp.exp(gcc)[..., None], s)
             + jnp.einsum("bhcs,bhse->bhce", pc, v_new))
        g_last = gcc[..., -1]
        s = (s * jnp.exp(g_last)[..., None, None]
             + jnp.einsum("bhcd,bhce->bhde", kc * jnp.exp(g_last[..., None] - gcc)[..., None], v_new))
        return s, o

    xs = tuple(jnp.moveaxis(a, 2, 0) for a in (q, k, u, w, gc, p_intra))
    s_fin, o = lax.scan(step, s0, xs)
    o = jnp.moveaxis(jnp.moveaxis(o, 0, 2), 1, 3).reshape(bsz, n_c * c, n_h, d_v)[:, :t_len]
    return o, s_fin

def mixer(h, gdn_buf, s0, conf_buf, w_in, gdn_conv_w, gdn_a_log, gdn_dt_bias, gdn_norm, gdn_o,
          conf_conv_w, conf_conv_b, conf_ln_g, conf_ln_b, conf_pw2, conf_pw2_b, w_out):
    bsz, t_len, _ = h.shape
    f32 = jnp.float32
    proj = h @ w_in
    qkv, z, a, b, glu, gates = jnp.split(proj, SPLITS, axis=-1)
    qkv, gdn_buf_new = causal_dwconv(qkv, gdn_buf, gdn_conv_w)
    qkv = jax.nn.silu(qkv).astype(f32)
    q, k, v = jnp.split(qkv, (QK_W, 2 * QK_W), axis=-1)
    q = l2_normalize(q.reshape(bsz, t_len, GDN_HEADS, GDN_DK)) * (GDN_DK ** -0.5)
    k = l2_normalize(k.reshape(bsz, t_len, GDN_HEADS, GDN_DK))
    v = v.reshape(bsz, t_len, GDN_HEADS, GDN_DV)
    beta = jax.nn.sigmoid(b.astype(f32))
    g = -jnp.exp(gdn_a_log.astype(f32)) * jax.nn.softplus(a.astype(f32) + gdn_dt_bias.astype(f32))
    o, s_new = gated_delta_chunked(q, k, v, g, beta, s0.astype(f32))
    o = rms_norm(o, gdn_norm) * jax.nn.silu(z.astype(f32).reshape(bsz, t_len, GDN_HEADS, GDN_DV))
    y_a = o.reshape(bsz, t_len, V_W).astype(h.dtype) @ gdn_o
    glu_a, glu_b = jnp.split(glu, 2, axis=-1)
    cv = glu_a * jax.nn.sigmoid(glu_b)
    cv, conf_buf_new = causal_dwconv(cv, conf_buf, conf_conv_w)
    cv = layer_norm(cv + conf_conv_b, conf_ln_g, conf_ln_b)
    y_b = jax.nn.silu(cv) @ conf_pw2 + conf_pw2_b
    g_a, g_b = jnp.split(gates, 2, axis=-1)
    y = (jax.nn.sigmoid(g_a) * y_a + jax.nn.sigmoid(g_b) * y_b) @ w_out
    return y, gdn_buf_new.astype(gdn_buf.dtype), s_new.astype(s0.dtype), conf_buf_new.astype(conf_buf.dtype)

def mem_kv(mem, norm_mem, xa_kv):
    m = rms_norm(mem, norm_mem)
    kk, vv = jnp.split(m @ xa_kv, 2, axis=-1)
    shp = mem.shape[:2] + (XA_HEADS, XA_DH)
    return kk.reshape(shp), vv.reshape(shp)

def cross_attn(h, mk, mv, xa_q, xa_o):
    bsz, t_len, _ = h.shape
    q = (h @ xa_q).reshape(bsz, t_len, XA_HEADS, XA_DH)
    s = jnp.einsum("bthd,bmhd->bhtm", q, mk.astype(h.dtype)).astype(jnp.float32) * (XA_DH ** -0.5)
    p = jax.nn.softmax(s, axis=-1).astype(h.dtype)
    o = jnp.einsum("bhtm,bmhd->bthd", p, mv.astype(h.dtype)).reshape(bsz, t_len, XA_HEADS * XA_DH)
    return o @ xa_o

def clamped_swiglu(x_glu, x_lin):
    x_glu = jnp.minimum(x_glu, SWIGLU_LIMIT)
    x_lin = jnp.clip(x_lin, -SWIGLU_LIMIT, SWIGLU_LIMIT)
    return x_glu * jax.nn.sigmoid(SWIGLU_ALPHA * x_glu) * (x_lin + 1.0)

def moe(h, router_w, router_b, moe_w1, moe_b1, moe_w2, moe_b2):
    bsz, t_len, d = h.shape
    xt = h.reshape(-1, d)
    logits = (xt @ router_w + router_b).astype(jnp.float32)
    top_v, top_i = lax.top_k(logits, TOP_K)
    gate = jax.nn.softmax(top_v, axis=-1)
    combine = jnp.sum(jax.nn.one_hot(top_i, N_EXPERTS, dtype=jnp.float32) * gate[..., None], axis=1)
    out = jnp.zeros((xt.shape[0], d), jnp.float32)
    for e in range(N_EXPERTS):
        hid = xt @ moe_w1[e] + moe_b1[e]
        act = clamped_swiglu(hid[:, :D_FF], hid[:, D_FF:])
        out = out + combine[:, e:e + 1] * (act @ moe_w2[e] + moe_b2[e]).astype(jnp.float32)
    return out.astype(h.dtype).reshape(bsz, t_len, d)

def setup_inputs(seed: int = 0) -> dict:
    key = jax.random.key(seed)
    ks = iter(jax.random.split(key, 64))
    f32 = jnp.float32
    L = DEPTH

    def normal(shape, scale):
        return scale * jax.random.normal(next(ks), shape, f32)

    def gain(shape):
        return 1.0 + 0.02 * jax.random.normal(next(ks), shape, f32)

    inp = {}
    inp["x_prompt"] = normal((BATCH, SEQ, D_MODEL), 1.0)
    inp["x_sample"] = normal((DEC_BATCH, DEC_SEQ, D_MODEL), 1.0)
    inp["mem_prompt"] = normal((BATCH, MEM_LEN, D_MODEL), 1.0)
    inp["state_gdn"] = normal((L, DEC_BATCH, GDN_HEADS, GDN_DK, GDN_DV), 0.1)
    inp["state_gdn_conv"] = normal((L, DEC_BATCH, GDN_CONV - 1, QKV_W), 1.0)
    inp["state_conf_conv"] = normal((L, DEC_BATCH, CONF_WIDTH - 1, CONF_DIM), 1.0)
    inp["cache_mem_k"] = normal((L, DEC_BATCH, MEM_LEN, XA_HEADS, XA_DH), 1.0)
    inp["cache_mem_v"] = normal((L, DEC_BATCH, MEM_LEN, XA_HEADS, XA_DH), 1.0)
    inp["norm_mix"] = gain((L, D_MODEL))
    inp["w_in"] = normal((L, D_MODEL, N_IN), D_MODEL ** -0.5)
    inp["gdn_conv_w"] = normal((L, GDN_CONV, QKV_W), GDN_CONV ** -0.5)
    inp["gdn_a_log"] = jnp.log(jax.random.uniform(next(ks), (L, GDN_HEADS), f32, 1.0, 16.0))
    dt = jax.random.uniform(next(ks), (L, GDN_HEADS), f32, 0.001, 0.1)
    inp["gdn_dt_bias"] = dt + jnp.log(-jnp.expm1(-dt))
    inp["gdn_norm"] = gain((L, GDN_DV))
    inp["gdn_o"] = normal((L, V_W, D_MODEL), V_W ** -0.5)
    inp["conf_conv_w"] = normal((L, CONF_WIDTH, CONF_DIM), CONF_WIDTH ** -0.5)
    inp["conf_conv_b"] = normal((L, CONF_DIM), 0.02)
    inp["conf_ln_g"] = gain((L, CONF_DIM))
    inp["conf_ln_b"] = normal((L, CONF_DIM), 0.02)
    inp["conf_pw2"] = normal((L, CONF_DIM, D_MODEL), CONF_DIM ** -0.5)
    inp["conf_pw2_b"] = normal((L, D_MODEL), 0.02)
    inp["w_out"] = normal((L, D_MODEL, D_MODEL), D_MODEL ** -0.5)
    inp["norm_xa"] = gain((L, D_MODEL))
    inp["norm_mem"] = gain((L, D_MODEL))
    inp["xa_q"] = normal((L, D_MODEL, XA_HEADS * XA_DH), D_MODEL ** -0.5)
    inp["xa_kv"] = normal((L, D_MODEL, 2 * XA_HEADS * XA_DH), D_MODEL ** -0.5)
    inp["xa_o"] = normal((L, XA_HEADS * XA_DH, D_MODEL), (XA_HEADS * XA_DH) ** -0.5)
    inp["norm_ffn"] = gain((L, D_MODEL))
    inp["router_w"] = normal((L, D_MODEL, N_EXPERTS), D_MODEL ** -0.5)
    inp["router_b"] = normal((L, N_EXPERTS), 0.01)
    inp["moe_w1"] = normal((L, N_EXPERTS, D_MODEL, 2 * D_FF), D_MODEL ** -0.5)
    inp["moe_b1"] = normal((L, N_EXPERTS, 2 * D_FF), 0.01)
    inp["moe_w2"] = normal((L, N_EXPERTS, D_FF, D_MODEL), D_FF ** -0.5)
    inp["moe_b2"] = normal((L, N_EXPERTS, D_MODEL), 0.01)
    inp["norm_final"] = gain((D_MODEL,))
    return inp

def reference(x_prompt, x_sample, mem_prompt, state_gdn, state_gdn_conv, state_conf_conv, cache_mem_k, cache_mem_v,
              norm_mix, w_in, gdn_conv_w, gdn_a_log, gdn_dt_bias, gdn_norm, gdn_o, conf_conv_w, conf_conv_b,
              conf_ln_g, conf_ln_b, conf_pw2, conf_pw2_b, w_out, norm_xa, norm_mem, xa_q, xa_kv, xa_o,
              norm_ffn, router_w, router_b, moe_w1, moe_b1, moe_w2, moe_b2, norm_final):

    def block(x, mk, mv, gbuf, s, cbuf, l):
        h = rms_norm(x, norm_mix[l])
        y, gbuf, s, cbuf = mixer(h, gbuf, s, cbuf, w_in[l], gdn_conv_w[l], gdn_a_log[l], gdn_dt_bias[l],
                                 gdn_norm[l], gdn_o[l], conf_conv_w[l], conf_conv_b[l], conf_ln_g[l],
                                 conf_ln_b[l], conf_pw2[l], conf_pw2_b[l], w_out[l])
        x = x + y
        x = x + cross_attn(rms_norm(x, norm_xa[l]), mk, mv, xa_q[l], xa_o[l])
        x = x + moe(rms_norm(x, norm_ffn[l]), router_w[l], router_b[l], moe_w1[l], moe_b1[l], moe_w2[l], moe_b2[l])
        return x, gbuf, s, cbuf

    bp = x_prompt.shape[0]
    xp, xs = x_prompt, x_sample
    p_gdn, p_gconv, p_cconv, p_mk, p_mv = [], [], [], [], []
    s_gdn, s_gconv, s_cconv = [], [], []
    for l in range(DEPTH):
        mk_p, mv_p = mem_kv(mem_prompt, norm_mem[l], xa_kv[l])
        gbuf0 = jnp.zeros((bp, GDN_CONV - 1, QKV_W), xp.dtype)
        s0 = jnp.zeros((bp, GDN_HEADS, GDN_DK, GDN_DV), xp.dtype)
        cbuf0 = jnp.zeros((bp, CONF_WIDTH - 1, CONF_DIM), xp.dtype)
        xp, gp, sp, cp = block(xp, mk_p, mv_p, gbuf0, s0, cbuf0, l)
        p_gdn.append(sp); p_gconv.append(gp); p_cconv.append(cp); p_mk.append(mk_p); p_mv.append(mv_p)
        xs, gs, ss, cs = block(xs, cache_mem_k[l], cache_mem_v[l], state_gdn_conv[l], state_gdn[l],
                               state_conf_conv[l], l)
        s_gdn.append(ss); s_gconv.append(gs); s_cconv.append(cs)
    y_prompt = rms_norm(xp, norm_final)
    y_sample = rms_norm(xs, norm_final)
    return (y_prompt, y_sample, jnp.stack(p_gdn), jnp.stack(p_gconv), jnp.stack(p_cconv), jnp.stack(p_mk),
            jnp.stack(p_mv), jnp.stack(s_gdn), jnp.stack(s_gconv), jnp.stack(s_cconv))


_drawn_inputs = setup_inputs


def setup_inputs(seed=0):
    import zlib

    import numpy as np

    out = dict(_drawn_inputs(seed))
    spreads = {}
    factors = {'conf_ln_b': 3.094,
     'norm_xa': 8.0,
     'norm_mem': 2.92,
     'moe_b1': 8.0,
     'moe_b2': 8.0,
     'norm_final': 2.85}
    for name, (base, spread) in spreads.items():
        noise = np.random.default_rng([zlib.crc32(name.encode()), seed]).standard_normal(out[name].shape)
        drawn = base * np.exp(spread * noise) if base else spread * noise
        out[name] = __import__('jax').numpy.asarray(drawn.astype(out[name].dtype))
    for name, factor in factors.items():
        out[name] = (out[name] * factor).astype(out[name].dtype)
    return out
```

```python
from contextlib import ExitStack

import concourse.bass as bass
from concourse import mybir

F32 = mybir.dt.float32
I32 = mybir.dt.int32
BF16 = mybir.dt.bfloat16
ALU = mybir.AluOpType
ACT = mybir.ActivationFunctionType
AX = mybir.AxisListType.X

P = 128
D = 1024
KC = D // P
SEQ, NB, DT = 256, 8, 4
NS = NB * DT
T = SEQ + NS
TT = (T + P - 1) // P
TROWS = [P, P, NS]
H = 8
GC = 4
QC = 3 * H
GM = GC - 1
GLEN = GM + SEQ + NB * (GM + DT)
CW = 31
CM = CW - 1
CLEN = CM + SEQ + NB * (CM + DT)
ML = 256
XH, XC = 4, 2
E, TOPK = 32, 4
FC = D // P
CAP = 64
LEVELS = 7
RING = 12
PCOL = 256
EPI = 12


def build(nc, d):
    with ExitStack() as ctx:
        def sb(name, shape, dt=F32):
            return ctx.enter_context(nc.sbuf_tensor(name, shape, dt))

        def sem(name):
            return ctx.enter_context(nc.semaphore(name))

        bank = [ctx.enter_context(nc.psum_tensor(f"bank{i}", [P, 512], F32)) for i in range(8)]

        ident = sb("ident", [P, P])
        ones = sb("ones", [P, P])
        level_mask = sb("level_mask", [P, LEVELS, P])
        causal = sb("causal", [P, 2, P])
        batch_of = sb("batch_of", [NS, NB])
        last_of = sb("last_of", [NS, NS])
        slot_id = sb("slot_id", [P, CAP])
        slot_int = sb("slot_int", [P, CAP], I32)
        NPT = 10
        prm = sb("prm", [P, NPT * P])
        abias = sb("abias", [P, 2, H])
        rbias = sb("rbias", [P, E])
        w_ab = sb("w_ab", [P, KC, 2 * H])
        w_router = sb("w_router", [P, KC, E])

        ring = sb("ring", [P, RING, 2048])
        xT = sb("xT", [P, KC, T])
        hT = sb("hT", [P, KC, T])
        arena = sb("arena", [P, 19200])
        SC = sb("SC", [P, 3, T])
        sg = sb("sg", [P, 2, T])
        rounds = sb("rounds", [1, 2, E], I32)

        A_QKV, A_Z = 0, QC * GLEN
        A_CV = A_Z + KC * T
        A_SA = A_CV + KC * CLEN
        A_SB = A_SA + KC * T
        assert A_SB + KC * T <= 19200

        def at(off, *shape):
            n = 1
            for s in shape:
                n *= s
            v = arena[:, off:off + n]
            if len(shape) == 2:
                return v.rearrange("p (a b) -> p a b", a=shape[0])
            if len(shape) == 3:
                return v.rearrange("p (a b c) -> p a b c", a=shape[0], b=shape[1])
            return v

        qkv = at(A_QKV, QC, GLEN)
        zs = at(A_Z, KC, T)
        cvx = at(A_CV, KC, CLEN)
        gate_a = at(A_SA, KC, T)
        gate_b = at(A_SB, KC, T)
        st_x = at(A_QKV, TT, D)
        st_conf = at(A_Z, 2, D)
        st_gdn = at(A_SA, QC * P)
        st_par = at(A_SA + QC * P, NPT, P)
        assert QC * P + NPT * P <= 2 * KC * T

        VEC = {}
        for n, name in enumerate(["norm_mix", "norm_xa", "norm_mem", "norm_ffn", "norm_final",
                                  "conf_conv_b", "conf_ln_g", "conf_ln_b", "conf_pw2_b"]):
            VEC[name] = 8 * n
        VEC["gdn_norm"] = 72
        GW, CWO, B1O, B2O = P, 2 * P, 4 * P, 8 * P

        def vec(name, k):
            return prm[:, VEC[name] + k:VEC[name] + k + 1]

        def gdn_w(j, c):
            return prm[:, GW + QC * j + c:GW + QC * j + c + 1]

        def conf_w(j, c):
            r = KC * j + c
            r = r if r < 124 else r + 4
            return prm[:, CWO + r:CWO + r + 1]

        def cols(w, j):
            return w[0].rearrange("(k p) n -> p k n", p=P)[:, :, PCOL * j:PCOL * (j + 1)]

        def cols_at(w, c0):
            return w[0].rearrange("(k p) n -> p k n", p=P)[:, :, c0:c0 + PCOL]

        NQKV, NV = QC * P, H * P
        C_Z, C_A = NQKV, NQKV + NV
        C_GLU = C_A + 2 * H
        C_GATE = C_GLU + 2 * D
        W = d["w_in"]
        pieces = []
        for j in range(4):
            pieces += [cols_at(W, C_GLU + PCOL * j), cols_at(W, C_GLU + D + PCOL * j)]
        pieces += [cols(W, j) for j in range(NQKV // PCOL)]
        pieces += [cols_at(W, C_Z + PCOL * j) for j in range(4)]
        pieces += [cols_at(W, C_GATE + PCOL * j) for j in range(8)]
        for name in ("conf_pw2", "gdn_o", "w_out"):
            pieces += [cols(d[name], j) for j in range(4)]
        pieces += [cols(d["xa_kv"], j) for j in range(8)]
        pieces += [cols(d["xa_q"], j) for j in range(4)]
        for name in ("cache_mem_k", "cache_mem_v"):
            for b in range(NB):
                pieces.append(d[name][0, b].rearrange("(m p) h e -> p m (h e)", p=P))
        pieces += [cols(d["xa_o"], j) for j in range(4)]
        PRE = len(pieces)

        def dense(n):
            return ring[:, n % RING, :].rearrange("p (k n) -> p k n", k=KC)

        def wide(n):
            return ring[:, n % RING, :].rearrange("p (k n) -> p k n", k=2)

        w_here = [sem(f"w_here{i}") for i in range(RING)]
        w_free = sem("w_free")

        ld_x, ld_par, ld_conf, ld_gdn, ld_small = [sem(f"ld_{n}") for n in ("x", "par", "conf", "gdn", "small")]
        ld_mem, ld_state, masks_made, pads_made, tr_done, proj_done = [
            sem(n) for n in ["ld_mem", "ld_state", "masks_made", "pads_made", "tr_done", "proj_done"]]
        sq_made, sq_used, root_in, root_made, norm_made, act_self = [
            sem(n) for n in ["sq_made", "sq_used", "root_in", "root_made", "norm_made", "act_self"]]
        dve_self, pool_self, sig_made, acc_made, ab_done, ab_dve = [
            sem(n) for n in ["dve_self", "pool_self", "sig_made", "acc_made", "ab_done", "ab_dve"]]
        ab_act, g_pe, g_dve, g_act, g_pool, st_out = [
            sem(n) for n in ["ab_act", "g_pe", "g_dve", "g_act", "g_pool", "st_out"]]
        stores, conf_tail_made, gdn_tail_made, conf_s_made, conf_made, conv_made = [
            sem(n) for n in ["stores", "conf_tail_made", "gdn_tail_made", "conf_s_made", "conf_made", "conv_made"]]
        mean_done, mean_read, centred, scaled, silu_made, st_conf_rows = [
            sem(n) for n in ["mean_done", "mean_read", "centred", "scaled", "silu_made", "st_conf_rows"]]
        st_gdn_rows, l2_read, l2_root, gl_made, banks_clear, gc_done = [
            sem(n) for n in ["st_gdn_rows", "l2_read", "l2_root", "gl_made", "banks_clear", "gc_done"]]
        gc_read, unit_made, o_made, scores_done, max_made, exp_made = [
            sem(n) for n in ["gc_read", "unit_made", "o_made", "scores_done", "max_made", "exp_made"]]
        probs_made, pt_done, pt_made, xo_done, xo_made, s_scores = [
            sem(n) for n in ["probs_made", "pt_done", "pt_made", "xo_done", "xo_made", "s_scores"]]
        sT_made, v_used, logits_done, chosen_made, counts_done, rounds_made = [
            sem(n) for n in ["sT_made", "v_used", "logits_done", "chosen_made", "counts_done", "rounds_made"]]
        p_made, pg_made, xg_done, xg_evac, gate_made, sigm_made = [
            sem(n) for n in ["p_made", "pg_made", "xg_done", "xg_evac", "gate_made", "sigm_made"]]
        act_made, ysb_made, yt_done, ytok_evac, cg_done, cg_evac = [
            sem(n) for n in ["act_made", "ysb_made", "yt_done", "ytok_evac", "cg_done", "cg_evac"]]
        scat_done, scat_add, ex_self, ex_pe, ex_dve, ex_actv = [
            sem(n) for n in ["scat_done", "scat_add", "ex_self", "ex_pe", "ex_dve", "ex_actv"]]
        lo_made, hi_made, gates_made, gates_T_done, gates_T_made, b2_done = [
            sem(n) for n in ["lo_made", "hi_made", "gates_made", "gates_T_done", "gates_T_made", "b2_done"]]
        b2_added, ld_b2, xlo_evac, yhi_evac, ylo_made, cgl_made = [
            sem(n) for n in ["b2_added", "ld_b2", "xlo_evac", "yhi_evac", "ylo_made", "cgl_made"]]
        tr_free = [sem(f"tr_free{i}") for i in range(2)]
        proj_free = [sem(f"proj_free{i}") for i in range(4)]

        def chain(eng, s):
            n = {}

            def link(ins, signal=None, value=None):
                to = s if signal is None else signal
                n[to.name] = n.get(to.name, 0) + 1
                ins.then_inc(to, 1)
                eng.wait_ge(to, n[to.name] if value is None else value)
            return link

        in_jobs = []
        for t in range(TT):
            for half in range(2):
                r = TROWS[t]
                in_jobs.append(("x", [(st_x[0:r, t, P * (4 * half + i):P * (4 * half + i + 1)], r) for i in range(4)],
                                xT[:, 4 * half:4 * half + 4, P * t:P * t + r], (4, r)))
        PAR_ROWS = [73, 96, 124, 124] + [128] * 6
        for i, r in enumerate(PAR_ROWS):
            in_jobs.append(("par", [(st_par[0:r, i, :], r)], prm[:, P * i:P * i + r], None))
        conf_hist = cvx[:, :, CM + SEQ:CLEN].rearrange("p c (b s) -> p c b s", s=CM + DT)
        gdn_hist = qkv[:, :, GM + SEQ:GLEN].rearrange("p c (b s) -> p c b s", s=GM + DT)
        for u in range(2):
            for half in range(2):
                in_jobs.append(("conf", [(st_conf[0:120, u, P * (4 * half + i):P * (4 * half + i + 1)], 120)
                                         for i in range(4)],
                                conf_hist[:, 4 * half:4 * half + 4, 4 * u:4 * u + 4, 0:CM], (4, 4, CM)))
        for u in range(2):
            in_jobs.append(("gdn", [(st_gdn[0:NB * GM, P * (12 * u + i):P * (12 * u + i + 1)], NB * GM)
                                    for i in range(12)],
                            gdn_hist[:, 12 * u:12 * u + 12, :, 0:GM], (12, NB, GM)))
        loads = {"x": (ld_x, 16 * 2), "par": (ld_par, 16 * 15), "conf": (ld_conf, 16 * 2), "gdn": (ld_gdn, 16)}

        conf_tail = at(A_SA + QC * P + QC * 27, KC, CM + NS)
        gdn_tail = at(A_SA + QC * P, QC, GM + NB * GM)
        conf_rows = at(A_Z, D)
        gdn_rows = at(A_SA, QC * P)
        N_IN_JOBS = len(in_jobs)
        N_CONF_JOBS, N_GDN_JOBS = 2, 6

        def view(b, rows, n, shape):
            v = bank[b][0:rows, 0:n]
            if shape is None:
                return v
            if len(shape) == 2:
                return v.rearrange("p (a b) -> p a b", a=shape[0])
            return v.rearrange("p (a b c) -> p a b c", a=shape[0], b=shape[1])

        J_GLU, J_QKV, J_Z, J_GATE, J_PW2, J_O, J_OUT, J_KV, J_XQ, J_XO = 0, 16, 40, 48, 64, 72, 80, 88, 96, 104
        NP_GLU, NP_QKV, NP_Z, NP_GATE, NP_PW2, NP_O, NP_OUT = 0, 8, 20, 24, 32, 36, 40
        NP_KV, NP_XQ, NP_CACHE, NP_XO = 44, 52, 56, 72

        def job_ready(eng, j):
            eng.wait_ge(proj_done, j + 1)

        def job_left(eng, j):
            eng.wait_ge(proj_free[j % 4], j // 4 + 1)

        def proj_bank(j):
            return bank[j % 4][:, 0:T]

        def s4(ap):
            return ap.rearrange("p (b s) -> p b s", s=DT)

        def conf_new(c):
            return conf_hist[:, c, :, CM:CM + DT]


        hflat = hT[:, :, :].rearrange("p k t -> p (k t)")
        w3 = TT * P
        G = {}
        for n, name in enumerate(["decay", "mt", "pt", "x", "y", "ct0"]):
            G[name] = hflat[:, n * w3:(n + 1) * w3].rearrange("p (a b) -> p a b", a=TT)
        v_wide = hflat[0:NS, 3 * w3:3 * w3 + NB * P].rearrange("p (b n) -> p b n", b=NB)
        for n, name in enumerate(["ct1", "kbg", "kd", "vb", "nwt", "qg", "eg", "xt"]):
            G[name] = at(A_CV + n * w3, TT, P)
        states = at(A_CV + 8 * w3, NB, P)
        rest = at(A_CV + 8 * w3 + NB * P, 368)
        assert 8 * w3 + NB * P + 368 <= KC * CLEN
        w_q = rest[:, 0:64].rearrange("p (b i s) -> p b i s", b=NB, i=2)
        w_q_s = rest[:, 64:128].rearrange("p (b i s) -> p b i s", b=NB, i=2)
        vnT_s = rest[:, 128:160]
        vn_s = rest[0:NS, 160:288]
        k_last = rest[0:NS, 288:289]
        k_last_p = rest[0:NS, 292:324]
        s_one, vn0, vn1 = sg[:, 0, 0:P], sg[:, 0, P:2 * P], sg[:, 1, 0:P]
        s_fin = sg[:, 1, P:2 * P]
        small = at(A_SB + KC * T, 264)

        def small3(i):
            return small[:, i:i + 24].rearrange("p (t n) -> p t n", t=TT)
        ab = small[:, 0:48].rearrange("p (t n) -> p t n", t=TT)
        beta, gl, gc, kb_s, tmp_a, tmp_b = [small3(48 + 24 * i) for i in range(6)]
        ea = small[:, 192:200]
        conf_acc = at(A_Z + D, KC * NS).rearrange("p (c b s) -> p c b s", c=KC, b=NB)
        conf_tmp = at(A_Z + D + KC * NS, KC * NS).rearrange("p (c b s) -> p c b s", c=KC, b=NB)

        mem_rows = at(0, 2, D)
        memT = at(2048, KC, ML)
        mem_k, mem_v = at(4096, 2, D), at(6144, 2, D)
        mem_kT = at(8192, KC, ML)
        xq, xo = at(10240, KC, T), at(12544, KC, T)
        kT_b = at(14848, 2 * KC * ML).rearrange("p (i c m) -> p i c m", i=2, c=KC)
        probs = at(0, 2, ML)
        probsT = at(512, 2 * ML).rearrange("p (i m n) -> p i m n", i=2, m=2)
        stat = at(1024, 48)

        def half(off, *shape):
            n = 1
            for x in shape:
                n *= x
            v = arena[:, off:off + (n + 1) // 2].bitcast(BF16)[:, 0:n]
            if len(shape) == 2:
                return v.rearrange("p (a b) -> p a b", a=shape[0])
            return v
        tok_hi, tok_lo = half(0, TT, D), half(1536, TT, D)
        logits, gates_, chosen, ties, run_a, run_b, place = [at(3072 + 96 * i, TT, E) for i in range(7)]
        top = at(3744, TT, 8)
        need = at(3768, 3)
        rounds_f = at(3776, 4, E)[0:1]
        ex_off = at(3904, E)
        ex_place = at(3936, TT)
        xg_hi, xg_lo = half(4096, KC, CAP), half(4352, KC, CAP)
        gate_, lin_, sig_ = at(4608, 512), at(5120, 512), at(5632, 512)
        act_ = at(6144, FC, CAP)
        y_hi, y_lo = half(6656, D)[0:CAP], half(7168, D)[0:CAP]
        cg_hi, cg_lo = half(7680, T)[0:CAP], half(7824, T)[0:CAP]
        onehot, pg = half(7968, TT, CAP), at(8064, TT, CAP)
        ex_xg_hi, ex_xg_lo = half(8256, KC, CAP), half(8512, KC, CAP)
        ex_act = at(8768, FC, CAP)
        ex_y_hi, ex_y_lo = half(9280, D)[0:CAP], half(9792, D)[0:CAP]
        ex_cg_hi, ex_cg_lo = half(10304, T)[0:CAP], half(10448, T)[0:CAP]
        ex_onehot, ex_pg = half(10592, TT, CAP), at(10688, TT, CAP)
        b2_rows = at(10880, D)[0:E]
        gates_T = at(11904, T)[0:E]
        w_lo = [half(12544 + 1024 * i, 2 * D) for i in range(6)] + [
            hflat[:, 1024 * i:1024 * (i + 1)].bitcast(BF16) for i in range(2)]
        y_rows = at(0, TT, D)

        sg_reader = ([(proj_free[j % 4], j // 4 + 1) for j in [J_GLU + 4 * (c // 2) + c % 2 for c in range(KC)]]
                     + [(proj_free[j % 4], j // 4 + 1) for j in range(J_Z, J_Z + KC)]
                     + [(conv_made, c + 1) for c in range(QC)] + [(silu_made, k + 1) for k in range(KC)])

        XPE = {"gather": 1, "hidden": 2, "gates": 3, "output": 4, "scatter": 5}
        XDVE = {"onehot": 4, "xg": 9, "gate": 11, "act": 15, "cg": 16, "y": 18, "add": 19}
        XACT = {"xg": 1, "sig": 2, "cg": 3, "y": 4}
        XP, XD, XA = 4 + KC, 18 + KC, 4

        def at_least(eng, s, v):
            if not isinstance(v, int) or v > 0:
                eng.wait_ge(s, v)

        def w_slot(i):
            return (PRE + i) % RING

        def w_count(i):
            return 16 * ((PRE + i) // RING + 1)

        def high(ap):
            n = ap.shape[-1]
            return ap.bitcast(BF16)[:, 1:2 * n:2]

        def flat3(ap):
            return ap.rearrange("p k n -> p (k n)")

        def load_rounds(eng, e):
            return (eng.value_load(rounds[0:1, 0, bass.ds(e, 1)], min_val=0, max_val=(T - 1) // CAP),
                    eng.value_load(rounds[0:1, 1, bass.ds(e, 1)], min_val=0, max_val=E * (T - 1) // CAP))

        def bank_rows(eng, n, rows):
            eng.wait_ge(tr_done, n + 1)
            return bank[4 + n % 2][0:rows, :]

        PE_STEPS = (["rows", "turned"] + [f"{s}{l}" for l in range(1, LEVELS) for s in ("y", "z")]
                    + ["w", "vn0", "s1", "vn1", "sample", "vnt", "out"])
        DVE_STEPS = (["spread", "decay_in", "decayed", "xt0", "columns"] + [f"x{l}" for l in range(1, LEVELS)]
                     + ["qg", "vn0", "vn1", "vnT", "vn_s", "wide", "head"])
        ACT_STEPS = (["eg", "exp", "x0"] + [f"y{l}" for l in range(1, LEVELS)]
                     + ["nwt", "s1", "ws"])

        def step(eng, s, steps, h, name):
            eng.wait_ge(s, len(steps) * h + steps.index(name) + 1)

        tile_cols = [slice(0, P), slice(P, 2 * P), slice(2 * P, T)]

        def piece_read(n):
            if n >= NP_XO:
                return proj_done, J_XO + 2 * (n - NP_XO) + 2
            if n >= NP_CACHE + NB:
                return v_used, n - NP_CACHE - NB + 1
            if n >= NP_CACHE:
                return tr_done, 38 + 4 * (n - NP_CACHE + 1)
            if n >= NP_XQ:
                return proj_done, J_XQ + 2 * (n - NP_XQ) + 2
            if n >= NP_KV:
                return proj_done, J_KV + (n - NP_KV) + 1
            return proj_done, 2 * n + 2

        block = ctx.enter_context(nc.Block())

        @block.sync
        def _(sp):
            for n, src in enumerate(pieces):
                if n >= RING:
                    sp.wait_ge(*piece_read(n - RING))
                dst = ring[:, n % RING, :]
                sp.dma_start(dst.rearrange("p (k n) -> p k n", k=src.shape[1]), src).then_inc(w_here[n % RING], 16)
            w1 = d["moe_w1"][0].rearrange("e (k p) n -> p e k n", p=P)
            w2 = d["moe_w2"][0].rearrange("e (k p) n -> p e k n", p=P)

            def expert_in(e, ready):
                for i in range(EPI):
                    ready(i)
                    dst = ring[:, (PRE + i) % RING, :]
                    if i < KC:
                        sp.dma_start(dst, w1[:, e, i, :]).then_inc(w_here[(PRE + i) % RING], 16)
                    else:
                        f = 2 * (i - KC)
                        sp.dma_start(dst.rearrange("p (k n) -> p k n", k=2),
                                     w2[:, e, f:f + 2, :]).then_inc(w_here[(PRE + i) % RING], 16)

            expert_in(0, lambda i: sp.wait_ge(*piece_read(PRE + i - RING)))
            with sp.Fori(1, E) as e:
                expert_in(e, lambda i: sp.wait_ge(w_free, e * EPI - EPI + (i + 1)))

        @block.gpsimd
        def _(pool):
            own = chain(pool, pool_self)
            own(pool.memset(ident[:, :], 0.0))
            own(pool.affine_select(out=ident[:, :], in_=ident[:, :], compare_op=ALU.not_equal, fill=1.0,
                                   base=0, pattern=[[-1, P]], channel_multiplier=1))
            own(pool.memset(ones[:, :], 1.0), masks_made)
            own(pool.memset(level_mask[:, :, :], 0.0))
            for l in range(LEVELS):
                s = 1 << l
                m = level_mask[:, l, :].rearrange("p (b h i) -> p b h i", h=2, i=s)[:, :, 1, :]
                own(pool.memset(m, 1.0))
                own(pool.affine_select(out=m, in_=m, compare_op=ALU.is_ge, fill=0.0, base=0,
                                       pattern=[[-2 * s, P // (2 * s)], [0, s]], channel_multiplier=1))
                own(pool.affine_select(out=m, in_=m, compare_op=ALU.is_ge, fill=0.0, base=s - 1,
                                       pattern=[[2 * s, P // (2 * s)], [0, s]], channel_multiplier=-1))
            own(pool.memset(causal[:, :, :], 0.0))
            own(pool.memset(causal[:, 0, :], 1.0))
            own(pool.affine_select(out=causal[:, 0, :], in_=causal[:, 0, :], compare_op=ALU.is_ge, fill=0.0,
                                   base=0, pattern=[[1, P]], channel_multiplier=-1))
            own(pool.tensor_tensor(causal[0:NS, 1, 0:NS], level_mask[0:NS, 0, 0:NS], level_mask[0:NS, 1, 0:NS], ALU.add))
            own(pool.tensor_tensor(causal[0:NS, 1, 0:NS], causal[0:NS, 1, 0:NS], ident[0:NS, 0:NS], ALU.add))
            own(pool.memset(batch_of[:, :], 1.0))
            own(pool.affine_select(out=batch_of[:, :], in_=batch_of[:, :], compare_op=ALU.is_ge, fill=0.0,
                                   base=0, pattern=[[-DT, NB]], channel_multiplier=1))
            own(pool.affine_select(out=batch_of[:, :], in_=batch_of[:, :], compare_op=ALU.is_ge, fill=0.0,
                                   base=DT - 1, pattern=[[DT, NB]], channel_multiplier=-1))
            own(pool.memset(last_of[:, :], 0.0))
            own(pool.tensor_copy(last_of[:, DT - 1:NS:DT], batch_of[:, :]))
            own(pool.iota(slot_int[:, :], pattern=[[1, CAP]], base=0, channel_multiplier=0))
            own(pool.tensor_copy(slot_id[:, :], slot_int[:, :]))
            own(pool.memset(small[:, :], 0.0), masks_made)
            own(pool.memset(cvx[:, :, 0:CM], 0.0), pads_made)
            pool.wait_ge(tr_free[0], 3)
            pool.wait_ge(tr_free[1], 3)
            own(pool.memset(qkv[:, :, 0:GM], 0.0), pads_made)

            pool.wait_ge(conf_tail_made, KC)
            for j in range(CW):
                wj = []
                for lo, hi in ((0, KC),):
                    c0 = CWO + KC * j + (0 if KC * j < 124 else 4)
                    if KC * j < 124 < KC * j + KC:
                        half = 124 - KC * j
                        wj = [(0, half, CWO + KC * j), (half, KC, CWO + KC * j + half + 4)]
                    else:
                        wj = [(0, KC, c0)]
                for lo, hi, c0 in wj:
                    w = prm[:, c0:c0 + hi - lo].unsqueeze(2).unsqueeze(3).to_broadcast((P, hi - lo, NB, DT))
                    x = conf_hist[:, lo:hi, :, j:j + DT]
                    out = conf_acc if j == 0 else conf_tmp
                    last = own(pool.tensor_tensor(out[:, lo:hi], x, w, ALU.mult))
                if j:
                    a = conf_acc.rearrange("p c b s -> p (c b s)")
                    t = conf_tmp.rearrange("p c b s -> p (c b s)")
                    own(pool.tensor_tensor(a, a, t, ALU.add), conf_s_made if j == CW - 1 else pool_self)

            def load_states(h):
                pool.dma_start(states, d["state_gdn"][0, :, h].rearrange("b k v -> k b v")).then_inc(ld_state, 16)

            for h in range(H):
                step(pool, g_dve, DVE_STEPS, h, "xt0")
                for l in range(1, LEVELS):
                    if l >= 3:
                        step(pool, g_pe, PE_STEPS, h, f"y{l - 2}")
                    n = TT if l == 1 else 2
                    ct = G["ct0"] if l % 2 else G["ct1"]
                    m = level_mask[:, l:l + 1, :].to_broadcast((P, n, P))
                    own(pool.tensor_tensor(ct[:, 0:n, :], G["mt"][:, 0:n, :], m, ALU.mult), g_pool)
                if h == 0:
                    load_states(0)
                step(pool, g_dve, DVE_STEPS, h, "head")
                pool.dma_start(d["out_state_p"][0, 0, h], s_fin).then_inc(st_out, 16)
                pool.dma_start(d["out_state_s"][0, :, h].rearrange("b k v -> k b v"), states).then_inc(st_out, 16)
                pool.wait_ge(st_out, 32 * (h + 1))
                if h + 1 < H:
                    load_states(h + 1)

        @block.tensor
        def _(pe):
            mm, tp = nc.tensor.matmul, nc.tensor.transpose
            tr = [0]

            def turn(srcs, rows=None, step_=None):
                n = tr[0]
                tr[0] += 1
                if n >= 2:
                    pe.wait_ge(tr_free[n % 2], n // 2)
                c = 0
                for src, r in srcs:
                    m_ = src.shape[1]
                    last = tp(bank[4 + n % 2][0:m_, c:c + r], src, ident[0:r, 0:r])
                    c += r
                last.then_inc(tr_done, 1)

            sq = [0]

            def sum_squares(b, n=KC, cols_=T, lag=0):
                for k in range(n):
                    pe.wait_ge(sq_made, sq[0] + 1)
                    mm(bank[b][:, 0:cols_], ones[:, :], SC[:, sq[0] % 2, 0:cols_],
                       start=(k == 0), stop=(k == n - 1)).then_inc(sq_used, 1)
                    sq[0] += 1

            def piece(n):
                pe.wait_ge(w_here[n % RING], 16 * (n // RING + 1))

            def project(job, n0, pieces_, rhs):
                for p_ in range(pieces_):
                    piece(n0 + p_)
                    w = dense(n0 + p_)
                    for half in range(2):
                        j = job + 2 * p_ + half
                        if j >= 4:
                            job_left(pe, j - 4)
                        for k in range(KC):
                            last = mm(proj_bank(j), w[:, k, P * half:P * (half + 1)], rhs(k),
                                      start=(k == 0), stop=(k == KC - 1))
                        last.then_inc(proj_done, 1)
            pe.wait_ge(masks_made, 1)
            seen_load = set()
            for kind, srcs, dst, shape in in_jobs:
                if kind not in seen_load:
                    pe.wait_ge(*loads[kind])
                    seen_load.add(kind)
                turn(srcs)
            sum_squares(6)
            pe.wait_ge(norm_made, 1)
            x = lambda k: hT[:, k, :]
            project(J_GLU, NP_GLU, 8, x)
            project(J_QKV, NP_QKV, 2, x)
            pe.wait_ge(conf_tail_made, KC)
            for half in range(2):
                turn([(conf_tail[:, 4 * half + i, :], P) for i in range(4)])
            project(J_QKV + 4, NP_QKV + 2, 10, x)
            project(J_Z, NP_Z, 4, x)
            for g_ in range(N_GDN_JOBS):
                pe.wait_ge(gdn_tail_made, 4 * g_ + 4)
                turn([(gdn_tail[:, 4 * g_ + i, :], P) for i in range(4)])
            project(J_GATE, NP_GATE, 8, x)
            pe.wait_ge(ld_small, 16 * 5)
            pe.wait_ge(tr_free[0], 15)
            pe.wait_ge(tr_free[1], 15)
            for t in range(TT):
                for k in range(KC):
                    last = mm(bank[4][0:TROWS[t], 16 * t:16 * t + 16], hT[:, k, tile_cols[t]], w_ab[:, k, :],
                              start=(k == 0), stop=(k == KC - 1))
            last.then_inc(ab_done, 1)
            pe.wait_ge(conf_made, KC)
            pe.wait_ge(conv_made, QC)
            for k in range(KC):
                last = mm(bank[6][:, 0:T], ones[:, :], cvx[:, k, 0:T], start=(k == 0), stop=(k == KC - 1))
            last.then_inc(mean_done, 1)
            pe.wait_ge(mean_read, 1)
            sum_squares(6)
            pe.wait_ge(norm_made, 2)
            project(J_PW2, NP_PW2, 4, lambda k: cvx[:, k, 0:T])
            pe.wait_ge(ab_dve, 1)
            def l2_sums(n0, count):
                for n in range(n0, n0 + count):
                    if n >= 2:
                        pe.wait_ge(l2_read, n - 1)
                    sum_squares(4 + n % 2, 1)
            l2_sums(0, 2 * H)
            pe.wait_ge(gl_made, 1)
            pe.wait_ge(banks_clear, 1)
            for t in range(TT):
                last = mm(bank[7][:, 8 * t:8 * t + 8], causal[:, t // 2, :], gl[:, t, :], start=True, stop=True)
            last.then_inc(gc_done, 1)

            def tiles(b, lhsT, rhs, n=TT, small=True):
                for t in range(n):
                    r = P if t < 2 or not small else NS
                    last = mm(bank[b][0:r, P * t:P * t + r], lhsT(t), rhs(t), start=True, stop=True)
                return last

            for h in range(H):
                D_ = lambda name: step(pe, g_dve, DVE_STEPS, h, name)
                A_ = lambda name: step(pe, g_act, ACT_STEPS, h, name)
                if h:
                    step(pe, g_dve, DVE_STEPS, h - 1, "head")
                q_ = lambda t: qkv[:, h, tile_cols[t]]
                k_ = lambda t: qkv[:, H + h, tile_cols[t]]
                v_ = lambda t: qkv[:, 2 * H + h, tile_cols[t]]
                r_ = lambda t: P if t < 2 else NS
                D_("spread")
                tiles(0, lambda t: G["kbg"][:, t, :], lambda t: causal[:, t // 2, :], small=False)
                tiles(1, lambda t: G["kd"][:, t, :], lambda t: ident[:, :], small=False)
                tiles(2, k_, k_)
                tiles(3, k_, q_).then_inc(g_pe, 1)
                for t in range(TT):
                    tp(bank[4][0:r_(t), P * t:P * (t + 1)], k_(t), ident[:, :])
                    tp(bank[5][0:r_(t), P * t:P * (t + 1)], v_(t), ident[:, :])
                D_("xt0")
                for t in range(TT):
                    last = tp(bank[6][:, P * t:P * (t + 1)], G["xt"][:, t, :], ident[:, :])
                last.then_inc(g_pe, 1)
                for l in range(1, LEVELS):
                    n = TT if l == 1 else 2
                    ct = G["ct0"] if l % 2 else G["ct1"]
                    pe.wait_ge(g_pool, (LEVELS - 1) * h + l)
                    if l == 1:
                        A_("x0")
                    else:
                        D_(f"x{l - 1}")
                    tiles(7, lambda t: ct[:, t, :], lambda t: G["x"][:, t, :], n, False).then_inc(g_pe, 1)
                    A_(f"y{l}")
                    if l < LEVELS - 1:
                        tiles(6, lambda t: G["xt"][:, t, :], lambda t: G["y"][:, t, :], n, False)
                    tiles(2, lambda t: G["y"][:, t, :], lambda t: G["xt"][:, t, :], n, False).then_inc(g_pe, 1)
                D_(f"x{LEVELS - 1}")
                D_("columns")
                for t in range(TT):
                    last = mm(bank[3][:, P * t:P * t + r_(t)], G["kbg"][0:r_(t), t, :], G["xt"][0:r_(t), t, 0:r_(t)],
                              start=True, stop=True)
                last.then_inc(g_pe, 1)
                mm(bank[7][:, 0:P], G["xt"][:, 0, :], G["vb"][:, 0, :], start=True, stop=True).then_inc(g_pe, 1)
                D_("vn0")
                mm(bank[7][:, P:2 * P], G["kd"][:, 0, :], vn0, start=True, stop=True).then_inc(g_pe, 1)
                A_("nwt")
                A_("s1")
                mm(bank[7][:, 2 * P:3 * P], G["xt"][:, 1, :], G["vb"][:, 1, :], start=True, stop=False)
                mm(bank[7][:, 2 * P:3 * P], G["nwt"][:, 1, :], s_one, start=False, stop=True).then_inc(g_pe, 1)
                D_("qg")
                pe.wait_ge(ld_state, 16 * (h + 1))
                for b in range(NB):
                    mm(bank[4][:, 8 * b:8 * b + 8], states[:, b, :], w_q[:, b, :, :].rearrange("p i s -> p (i s)"),
                       start=True, stop=True)
                mm(bank[5][:, 0:NS], G["vb"][0:NS, 2, :], G["xt"][0:NS, 2, 0:NS],
                   start=True, stop=True).then_inc(g_pe, 1)
                D_("vnT")
                tp(bank[5][0:NS, P:2 * P], vnT_s, ident[:, :]).then_inc(g_pe, 1)
                D_("vn1")
                D_("wide")
                mm(bank[6][:, 0:P], vn0, G["pt"][:, 0, :], start=True, stop=True)
                mm(bank[6][:, P:2 * P], s_one, G["qg"][:, 1, :], start=True, stop=False)
                mm(bank[6][:, P:2 * P], vn1, G["pt"][:, 1, :], start=False, stop=True)
                mm(bank[6][:, 2 * P:2 * P + NS], vn_s, G["pt"][0:NS, 2, 0:NS], start=True, stop=True)
                mm(bank[3][:, 0:P], G["kd"][:, 1, :], vn1, start=True, stop=True)
                for i in range(2):
                    last = mm(bank[i][:, :], G["kd"][0:NS, 2, :],
                              v_wide[:, 4 * i:4 * i + 4, :].rearrange("p b n -> p (b n)"), start=True, stop=True)
                last.then_inc(g_pe, 1)
            l2_sums(2 * H, H)
            pe.wait_ge(o_made, H)
            project(J_O, NP_O, 4, lambda k: qkv[:, 2 * H + k, 0:T])
            job_left(pe, J_OUT - 4), job_left(pe, J_OUT - 3), job_left(pe, J_OUT - 2), job_left(pe, J_OUT - 1)
            project(J_OUT, NP_OUT, 4, lambda k: gate_a[:, k, :])
            pe.wait_ge(ld_mem, 16)
            for t in range(2):
                for half in range(2):
                    turn([(mem_rows[:, t, P * (4 * half + i):P * (4 * half + i + 1)], P) for i in range(4)])
            sum_squares(7, KC, ML)
            pe.wait_ge(norm_made, 3)
            sum_squares(6)
            for p_ in range(8):
                j = J_KV + p_
                piece(NP_KV + p_)
                job_left(pe, j - 4)
                for t in range(2):
                    for k in range(KC):
                        last = mm(bank[j % 4][:, PCOL * t:PCOL * (t + 1)], memT[:, k, P * t:P * (t + 1)],
                                  dense(NP_KV + p_)[:, k, :], start=(k == 0), stop=(k == KC - 1))
                last.then_inc(proj_done, 1)
            for p_ in range(4):
                job_left(pe, J_KV + p_)
            for t in range(2):
                for half in range(2):
                    turn([(mem_k[:, t, P * (4 * half + i):P * (4 * half + i + 1)], P) for i in range(4)])
            pe.wait_ge(norm_made, 4)
            project(J_XQ, NP_XQ, 4, lambda k: hT[:, k, :])
            for j in range(J_XQ, J_XQ + 8):
                job_left(pe, j)
            for p_ in range(4, 8):
                job_left(pe, J_KV + p_)
            pe.wait_ge(tr_free[0], 19)
            pe.wait_ge(tr_free[1], 19)

            def scores(u):
                h, t = u // 2, u % 2
                if u >= 2:
                    pe.wait_ge(xo_made, u - 1)
                for c in range(XC):
                    last = mm(bank[4 + u % 2][:, 0:ML], xq[:, XC * h + c, P * t:P * (t + 1)],
                              mem_kT[:, XC * h + c, :], start=(c == 0), stop=(c == XC - 1))
                last.then_inc(scores_done, 1)

            def attend(u):
                h, t = u // 2, u % 2
                pe.wait_ge(probs_made, u + 1)
                if u >= 2:
                    pe.wait_ge(pt_made, u - 1)
                for m in range(2):
                    last = tp(bank[6 + u % 2][:, P * m:P * (m + 1)], probs[:, u % 2, P * m:P * (m + 1)], ident[:, :])
                last.then_inc(pt_done, 1)
                pe.wait_ge(pt_made, u + 1)
                for c in range(XC):
                    for m in range(2):
                        last = mm(bank[4 + u % 2][:, ML + P * c:ML + P * (c + 1)],
                                  mem_v[:, m, P * (XC * h + c):P * (XC * h + c + 1)], probsT[:, u % 2, m, :],
                                  start=(m == 0), stop=(m == 1))
                last.then_inc(xo_done, 1)

            NU = 2 * XH
            for u in range(NU + 1):
                if u < NU:
                    scores(u)
                if u:
                    attend(u - 1)
            pe.wait_ge(xo_made, NU)
            for b in range(NB):
                n = NP_CACHE + b
                piece(n)
                for t in range(2):
                    for half in range(2):
                        turn([(wide(n)[:, t, P * (4 * half + i):P * (4 * half + i + 1)], P) for i in range(4)])
                pe.wait_ge(tr_free[0], 19 + 2 * (b + 1))
                pe.wait_ge(tr_free[1], 19 + 2 * (b + 1))
                for m in range(2):
                    for h in range(XH):
                        for c in range(XC):
                            col = P * m + 16 * b + DT * h
                            last = mm(bank[6][:, col:col + DT], kT_b[:, b % 2, XC * h + c, P * m:P * (m + 1)],
                                      xq[:, XC * h + c, SEQ + DT * b:SEQ + DT * (b + 1)],
                                      start=(c == 0), stop=(c == XC - 1))
                last.then_inc(s_scores, 1)
            pe.wait_ge(sT_made, 1)
            for m in range(2):
                last = tp(bank[7][:, P * m:P * (m + 1)], probs[:, 0, P * m:P * (m + 1)], ident[:, :])
            last.then_inc(scores_done, 1)
            pe.wait_ge(probs_made, NU + 1)
            for m in range(2):
                last = tp(bank[6][:, P * m:P * (m + 1)], probs[:, 1, P * m:P * (m + 1)], ident[:, :])
            last.then_inc(pt_done, 1)
            pe.wait_ge(pt_made, NU + 1)
            for b in range(NB):
                n = NP_CACHE + NB + b
                piece(n)
                for c in range(KC):
                    for m in range(2):
                        last = mm(bank[5][:, NS * c + DT * b:NS * c + DT * (b + 1)],
                                  wide(n)[:, m, P * c:P * (c + 1)],
                                  probsT[:, 0, m, 16 * b + DT * (c // XC):16 * b + DT * (c // XC + 1)],
                                  start=(m == 0), stop=(m == 1))
                last.then_inc(v_used, 1)
            pe.wait_ge(xo_made, NU + 1)
            project(J_XO, NP_XO, 4, lambda k: xo[:, k, :])
            sum_squares(6)
            pe.wait_ge(norm_made, 5)
            for t in range(TT):
                for hf in range(2):
                    turn([(hT[:, 4 * hf + i, tile_cols[t]], P) for i in range(4)])
            for t in range(TT):
                for k in range(KC):
                    last = mm(bank[6][0:TROWS[t], E * t:E * (t + 1)], hT[:, k, tile_cols[t]], w_router[:, k, :],
                              start=(k == 0), stop=(k == KC - 1))
            last.then_inc(logits_done, 1)
            pe.wait_ge(chosen_made, 1)
            for t in range(TT):
                r = TROWS[t]
                for i in range(t):
                    mm(bank[7][0:r, E * t:E * (t + 1)], ones[:, 0:r], chosen[:, i, :], start=(i == 0), stop=False)
                mm(bank[7][0:r, E * t:E * (t + 1)], causal[0:r, 0, 0:r], chosen[0:r, t, :], start=(t == 0), stop=True)
            for t in range(TT):
                last = mm(bank[7][0:1, E * TT:E * (TT + 1)], ones[0:TROWS[t], 0:1], chosen[0:TROWS[t], t, :],
                          start=(t == 0), stop=(t == TT - 1))
            last.then_inc(counts_done, 1)
            pe.wait_ge(gates_made, 1)
            for t in range(TT):
                last = tp(bank[0][0:E, P * t:P * t + TROWS[t]], gates_[0:TROWS[t], t, :], ident[0:TROWS[t], 0:TROWS[t]])
            last.then_inc(gates_T_done, 1)
            pe.wait_ge(tr_free[0], 38)
            pe.wait_ge(tr_free[1], 38)

            def w_wait(e, i):
                pe.wait_ge(w_here[w_slot(i)], e * 16 + w_count(i))

            pe.wait_ge(gates_T_made, 1)
            pe.wait_ge(ld_b2, 16)
            for c in range(KC):
                if c >= 2:
                    pe.wait_ge(b2_added, c - 1)
                mm(bank[4 + c % 2][:, 0:T], b2_rows[:, P * c:P * (c + 1)], gates_T, start=True, stop=True).then_inc(b2_done, 1)

            def gather(hot, signal):
                for b, part in ((0, tok_hi), (3, tok_lo)):
                    for k in range(KC):
                        for t in range(TT):
                            r = TROWS[t]
                            last = mm(bank[b][:, CAP * k:CAP * (k + 1)], part[0:r, t, P * k:P * (k + 1)], hot[0:r, t, :],
                                      start=(k == 0 and t == 0), stop=(k == KC - 1 and t == TT - 1),
                                      skip_group_check=True)
                last.then_inc(signal, 1)

            def hidden(hi, lo, e, signal):
                for k in range(KC):
                    w_wait(e, k)
                    pe.wait_ge(lo_made, e * KC + (k + 1))
                    for f in range(2 * FC):
                        out = bank[1 + f // FC][:, CAP * (f % FC):CAP * (f % FC + 1)]
                        w_hi = high(ring[:, w_slot(k), P * f:P * (f + 1)])
                        mm(out, w_hi, hi[:, k, :], start=(k == 0 and f % FC == 0), stop=False, skip_group_check=True)
                        mm(out, w_hi, lo[:, k, :], start=False, stop=False, skip_group_check=True)
                        last = mm(out, w_lo[k][:, P * f:P * (f + 1)], hi[:, k, :], start=False,
                                  stop=(k == KC - 1 and f % FC == FC - 1), skip_group_check=True)
                    if signal is w_free or k == KC - 1:
                        last.then_inc(signal, 1)

            def output(a, e, signal):
                for i in range(4):
                    w_wait(e, KC + i)
                    for f in range(2 * i, 2 * i + 2):
                        for n in range(2):
                            o = 1024 * (f % 2) + 512 * n
                            last = mm(bank[6 + n][0:CAP, :], a[:, f, :], ring[:, w_slot(KC + i), o:o + 512],
                                      start=(f == 0), stop=(f == FC - 1))
                    if signal is w_free or i == 3:
                        last.then_inc(signal, 1)

            def turn_gates(pg_, signal):
                for t in range(TT):
                    r = TROWS[t]
                    last = (tp if t else mm)(bank[5][0:CAP, P * t:P * t + r], pg_[0:r, t, :], ident[0:r, 0:r])
                last.then_inc(signal, 1)

            def scatter(c, y, g_, signal):
                out = bank[4 + c % 2][:, 0:T]
                f_ = slice(P * c, P * (c + 1))
                mm(out, y[0][:, f_], g_[0], start=True, stop=False)
                mm(out, y[0][:, f_], g_[1], start=False, stop=False)
                mm(out, y[1][:, f_], g_[0], start=False, stop=True).then_inc(signal, 1)

            def extra(e, first):
                n, r0 = load_rounds(pe, e)
                with pe.If(n > 0):
                    with pe.Fori(0, n) as j:
                        r = pe.snap(r0 + j)
                        pe.wait_ge(xg_evac, e + 1)
                        pe.wait_ge(xlo_evac, e + 1)
                        if not first:
                            at_least(pe, scat_add, e * 8 - 8)
                            pe.wait_ge(ylo_made, e)
                        pe.wait_ge(ex_dve, r * XD + XDVE["onehot"])
                        gather(ex_onehot, ex_pe)
                        pe.wait_ge(ex_dve, r * XD + XDVE["xg"])
                        pe.wait_ge(ex_actv, r * XA + XACT["xg"])
                        hidden(ex_xg_hi, ex_xg_lo, e, ex_pe)
                        turn_gates(ex_pg, ex_pe)
                        pe.wait_ge(ex_dve, r * XD + XDVE["act"])
                        output(ex_act, e, ex_pe)
                        pe.wait_ge(ex_dve, r * XD + XDVE["y"])
                        for c in range(KC):
                            if c >= 2:
                                pe.wait_ge(ex_dve, r * XD + XDVE["add"] + c - 2)
                            scatter(c, (ex_y_hi, ex_y_lo), (ex_cg_hi, ex_cg_lo), ex_pe)
                        pe.wait_ge(ex_dve, r * XD + XD)

            def scatter_last(e):
                pe.wait_ge(cgl_made, e)
                pe.wait_ge(ylo_made, e)
                for c in range(KC):
                    if c >= 2:
                        pe.wait_ge(scat_add, e * 8 - 8 + (c - 1))
                    scatter(c, (y_hi, y_lo), (cg_hi, cg_lo), scat_done)

            def gates_last(e):
                pe.wait_ge(pg_made, e)
                at_least(pe, scat_add, e * 8 - 8)
                turn_gates(pg, cg_done)

            def expert(e, first, last_one):
                pe.wait_ge(xg_evac, e + 1)
                pe.wait_ge(xlo_evac, e + 1)
                hidden(xg_hi, xg_lo, e, w_free)
                if not first:
                    gates_last(e)
                if not last_one:
                    pe.wait_ge(p_made, e + 2)
                    gather(onehot, xg_done)
                if not first:
                    scatter_last(e)
                pe.wait_ge(act_made, e + 1)
                output(act_, e, w_free)

            pe.wait_ge(rounds_made, 1)
            pe.wait_ge(b2_added, KC)
            pe.wait_ge(p_made, 1)
            gather(onehot, xg_done)
            for e in (0, 1):
                extra(e, e == 0)
                expert(e, e == 0, False)
            with pe.Fori(2, E - 1) as e:
                extra(e, False)
                expert(e, False, False)
            extra(E - 1, False)
            expert(E - 1, False, True)
            gates_last(E)
            scatter_last(E)
            sum_squares(6)
            pe.wait_ge(norm_made, 6)
            for t in range(TT):
                for half in range(2):
                    turn([(hT[:, 4 * half + i, tile_cols[t]], P) for i in range(4)])

        @block.scalar
        def _(act):
            own = chain(act, act_self)
            A = nc.scalar.activation
            sq, root = [0], [0]

            def squares(src, n=KC, cols_=T):
                for k in range(n):
                    if sq[0] >= 2:
                        act.wait_ge(sq_used, sq[0] - 1)
                    A(SC[:, sq[0] % 2, 0:cols_], src(k), ACT.Square).then_inc(sq_made, 1)
                    sq[0] += 1

            def take_root(cols_=T):
                root[0] += 1
                act.wait_ge(root_in, root[0])
                A(SC[:, 2, 0:cols_], SC[:, 2, 0:cols_], ACT.Sqrt).then_inc(root_made, 1)

            def sigmoid(n, src, **kw):
                if n >= 2:
                    act.wait_ge(*sg_reader[n - 2])
                A(sg[:, n % 2, :], src, ACT.Sigmoid, **kw).then_inc(sig_made, 1)

            def read_bank(n, dst, shape, rows=P, w=512):
                act.wait_ge(tr_done, n + 1)
                A(dst, view(4 + n % 2, rows, w, shape), ACT.Copy).then_inc(tr_free[n % 2], 1)

            act.dma_start(st_x[:, 0:2, :], d["x_prompt"][0].rearrange("(t p) n -> p t n", p=P)).then_inc(ld_x, 16)
            act.dma_start(st_x[0:NS, 2, :], d["x_sample"].rearrange("b s n -> (b s) n")).then_inc(ld_x, 16)
            for name, c in VEC.items():
                v = d[name] if name == "norm_final" else d[name][0]
                r = 1 if name == "gdn_norm" else KC
                act.dma_start(st_par[c:c + r, 0, :], v.rearrange("(r n) -> r n", n=P)).then_inc(ld_par, 16)
            act.dma_start(st_par[0:96, 1, :], d["gdn_conv_w"][0].rearrange("j (c n) -> (j c) n", n=P)).then_inc(ld_par, 16)
            cw = d["conf_conv_w"][0].rearrange("j (c n) -> (j c) n", n=P)
            for i in range(2):
                act.dma_start(st_par[0:124, 2 + i, :], cw[124 * i:124 * i + 124, :]).then_inc(ld_par, 16)
            b1 = d["moe_b1"][0].rearrange("e (c n) -> (e c) n", n=P)
            act.dma_start(st_par[:, 4:8, :], b1.rearrange("(t p) n -> p t n", p=P)).then_inc(ld_par, 16)
            b2 = d["moe_b2"][0].rearrange("e (c n) -> (e c) n", n=P)
            act.dma_start(st_par[:, 8:10, :], b2.rearrange("(t p) n -> p t n", p=P)).then_inc(ld_par, 16)
            hist = d["state_conf_conv"][0].rearrange("b s n -> (b s) n")
            for u in range(2):
                act.dma_start(st_conf[0:120, u, :], hist[120 * u:120 * u + 120, :]).then_inc(ld_conf, 16)
            act.dma_start(st_gdn[0:NB * GM, :], d["state_gdn_conv"][0].rearrange("b s n -> (b s) n")).then_inc(ld_gdn, 16)
            win = d["w_in"][0].rearrange("(k p) n -> p k n", p=P)
            act.dma_start(w_ab[:, :, :], win[:, :, C_A:C_A + 2 * H]).then_inc(ld_small, 16)
            act.dma_start(w_router[:, :, :], d["router_w"][0].rearrange("(k p) n -> p k n", p=P)).then_inc(ld_small, 16)
            act.dma_start(rbias[:, :], d["router_b"].to_broadcast((P, E))).then_inc(ld_small, 16)
            act.dma_start(abias[:, 0, :], d["gdn_dt_bias"].to_broadcast((P, H))).then_inc(ld_small, 16)
            act.dma_start(abias[:, 1, :], d["gdn_a_log"].to_broadcast((P, H))).then_inc(ld_small, 16)
            act.dma_start(d["out_conf_s"][0][:, 0:CM - DT, :], d["state_conf_conv"][0][:, DT:CM, :]).then_inc(stores, 16)

            act.wait_ge(tr_free[0], 3)
            act.wait_ge(tr_free[1], 3)
            squares(lambda k: xT[:, k, :])
            take_root()
            for c in range(KC):
                j = J_GLU + 4 * (c // 2) + 2 + c % 2
                job_ready(act, j)
                sigmoid(c, proj_bank(j))

            def q_raw(c):
                j = J_QKV + c
                job_ready(act, j)
                if c == 0:
                    act.wait_ge(pads_made, 2)
                    act.wait_ge(tr_free[0], 11)
                A(qkv[:, c, GM:GM + SEQ], proj_bank(j)[:, 0:SEQ], ACT.Copy)
                A(gdn_hist[:, c, :, GM:GM + DT], s4(proj_bank(j)[:, SEQ:T]), ACT.Copy).then_inc(proj_free[j % 4], 1)

            for c in range(4):
                q_raw(c)
            for i in range(2):
                own(A(conf_rows[0:CM + NS, 512 * i:512 * i + 512], bank_rows(act, N_IN_JOBS + i, CM + NS), ACT.Copy),
                    tr_free[(N_IN_JOBS + i) % 2], (N_IN_JOBS + i) // 2 + 1)
            act.dma_start(d["out_conf_p"][0, 0], conf_rows[0:CM, :]).then_inc(st_conf_rows, 16)
            for b in range(NB):
                act.dma_start(d["out_conf_s"][0, b, CM - DT:CM, :],
                              conf_rows[CM + DT * b:CM + DT * (b + 1), :]).then_inc(st_conf_rows, 16)
            for c in range(4, QC):
                q_raw(c)
            for c in range(KC):
                j = J_Z + c
                job_ready(act, j)
                sigmoid(KC + c, proj_bank(j))
            n0 = N_IN_JOBS + N_CONF_JOBS
            for i in range(N_GDN_JOBS):
                own(A(gdn_rows[0:GM + NB * GM, 512 * i:512 * i + 512], bank_rows(act, n0 + i, GM + NB * GM), ACT.Copy),
                    tr_free[(n0 + i) % 2], (n0 + i) // 2 + 1)
            act.dma_start(d["out_gconv_p"][0, 0], gdn_rows[0:GM, :]).then_inc(st_gdn_rows, 16)
            act.dma_start(d["out_gconv_s"][0].rearrange("b s n -> (b s) n"),
                          gdn_rows[GM:GM + NB * GM, :]).then_inc(st_gdn_rows, 16)
            act.wait_ge(st_gdn_rows, 32)
            for i in range(16):
                j = J_GATE + i
                job_ready(act, j)
                g_ = gate_a if i < KC else gate_b
                A(g_[:, i % KC, :], proj_bank(j), ACT.Sigmoid).then_inc(proj_free[j % 4], 1)
                for c in range(QC * i // 16, QC * (i + 1) // 16):
                    act.wait_ge(acc_made, c + 1)
                    sigmoid(2 * KC + c, bank[6 + c % 2][:, 0:T])
            act.wait_ge(centred, KC)
            squares(lambda k: cvx[:, k, 0:T])
            take_root()
            for k in range(KC):
                act.wait_ge(scaled, k + 1)
                sigmoid(2 * KC + QC + k, cvx[:, k, 0:T], bias=vec("conf_ln_b", k))

            act.wait_ge(ab_dve, 1)
            own(A(beta, ab[:, :, H:2 * H], ACT.Sigmoid), ab_act)
            own(A(tmp_a, tmp_a, ACT.Exp, scale=-1.0))
            own(A(ea, abias[:, 1, :], ACT.Exp))
            own(A(tmp_a, tmp_a, ACT.Ln, bias=1.0), ab_act)
            def l2(n0, count, src):
                for n in range(n0, n0 + count + 1):
                    if n < n0 + count:
                        if n >= 2 * H:
                            pass
                        squares(lambda k: src(n), 1)
                    if n > n0:
                        act.wait_ge(l2_read, n)
                        A(sg[:, (n - 1) % 2, :], sg[:, (n - 1) % 2, :], ACT.Sqrt).then_inc(l2_root, 1)
            l2(0, 2 * H, lambda n: qkv[:, n, 0:T])
            act.wait_ge(gc_read, 1)
            own(A(tmp_a, gc, ACT.Exp), ab_act)

            for h in range(H):
                D_ = lambda name: step(act, g_dve, DVE_STEPS, h, name)
                P_ = lambda name: step(act, g_pe, PE_STEPS, h, name)
                flat = lambda n_: G[n_].rearrange("p a b -> p (a b)")
                P_("rows")
                A(flat("eg"), bank[0][:, 0:w3], ACT.Exp).then_inc(g_act, 1)
                D_("decay_in")
                A(flat("decay"), flat("decay"), ACT.Exp).then_inc(g_act, 1)
                P_("turned")
                A(flat("x"), bank[6][:, 0:w3], ACT.Copy).then_inc(g_act, 1)
                for l in range(1, LEVELS):
                    n = w3 if l == 1 else 2 * P
                    P_(f"y{l}")
                    A(flat("y")[:, 0:n], bank[7][:, 0:n], ACT.Copy).then_inc(g_act, 1)
                P_("w")
                A(flat("nwt")[:, 0:T], bank[3][:, 0:T], ACT.Copy, scale=-1.0).then_inc(g_act, 1)
                P_("s1")
                A(s_one, bank[7][:, P:2 * P], ACT.Copy).then_inc(g_act, 1)
                P_("sample")
                A(w_q_s.rearrange("p b i s -> p (b i s)"), bank[4][:, 0:64], ACT.Copy).then_inc(g_act, 1)
            step(act, g_dve, DVE_STEPS, H - 1, "head")
            l2(2 * H, H, lambda n: qkv[:, n, 0:T])

            act.wait_ge(proj_done, J_OUT)
            act.dma_start(mem_rows[:, :, :], d["mem_prompt"][0].rearrange("(t p) n -> p t n", p=P)).then_inc(ld_mem, 16)
            act.wait_ge(tr_free[0], 17)
            act.wait_ge(tr_free[1], 17)
            squares(lambda k: memT[:, k, :], KC, ML)
            take_root(ML)
            for j in range(J_OUT + 4, J_OUT + 8):
                job_left(act, j)
            squares(lambda k: xT[:, k, :])
            take_root()
            for p_ in range(8):
                j = J_KV + p_
                job_ready(act, j)
                dst = (mem_k if p_ < 4 else mem_v)[:, :, PCOL * (p_ % 4):PCOL * (p_ % 4 + 1)]
                own(A(dst, bank[j % 4][:, :].rearrange("p (t n) -> p t n", t=2), ACT.Copy), proj_free[j % 4], j // 4 + 1)
                if p_ == 3:
                    act.dma_start(d["out_mem_k"][0, 0].rearrange("(t p) h e -> p t (h e)", p=P), mem_k[:, :, :]).then_inc(stores, 16)
                if p_ == 7:
                    act.dma_start(d["out_mem_v"][0, 0].rearrange("(t p) h e -> p t (h e)", p=P), mem_v[:, :, :]).then_inc(stores, 16)
            for i in range(4):
                read_bank(34 + i, mem_kT[:, 4 * (i % 2):4 * (i % 2) + 4, P * (i // 2):P * (i // 2 + 1)], (4, P))
            for c in range(KC):
                j = J_XQ + c
                job_ready(act, j)
                A(xq[:, c, :], proj_bank(j), ACT.Copy).then_inc(proj_free[j % 4], 1)
            sc = XC ** -0.5 * P ** -0.5
            for u in range(2 * XH + 1):
                if u < 2 * XH:
                    act.wait_ge(max_made, u + 1)
                    if u >= 2:
                        act.wait_ge(pt_done, u - 1)
                    own(A(probs[:, u % 2, :], bank[4 + u % 2][:, 0:ML], ACT.Exp, bias=stat[:, u:u + 1], scale=sc,
                          accum_out=stat[:, 16 + u:17 + u]), exp_made)
                if u:
                    v = u - 1
                    h, t = v // 2, v % 2
                    act.wait_ge(xo_done, u)
                    A(xo[:, XC * h:XC * h + XC, P * t:P * (t + 1)],
                      bank[4 + v % 2][:, ML:2 * ML].rearrange("p (c n) -> p c n", c=XC), ACT.Copy).then_inc(xo_made, 1)
            for b in range(NB):
                for i in (1, 3):
                    n = 38 + 4 * b + i
                    if i == 1 and b >= 2:
                        act.wait_ge(s_scores, b - 1)
                    read_bank(n, kT_b[:, b % 2, 4 * (i % 2):4 * (i % 2) + 4, P * (i // 2):P * (i // 2 + 1)], (4, P))
            act.wait_ge(s_scores, NB)
            A(probs[:, 0, :], bank[6][:, 0:ML], ACT.Copy).then_inc(sT_made, 1)
            u = 2 * XH
            act.wait_ge(max_made, u + 1)
            own(A(probs[:, 1, :], bank[7][:, 0:ML], ACT.Exp, bias=stat[:, u:u + 1], scale=sc,
                  accum_out=stat[:, 16 + u:17 + u]), exp_made)
            act.dma_start(b2_rows, d["moe_b2"][0]).then_inc(ld_b2, 16)
            act.wait_ge(v_used, NB)
            A(xo[:, :, SEQ:T], bank[5][:, 0:KC * NS].rearrange("p (c n) -> p c n", c=KC), ACT.Copy).then_inc(xo_made, 1)
            for j in range(J_XO + 4, J_XO + 8):
                job_left(act, j)
            squares(lambda k: xT[:, k, :])
            take_root()
            for i in (1, 3, 5):
                r = TROWS[i // 2]
                act.wait_ge(tr_done, 70 + i + 1)
                own(A(tok_hi[0:r, i // 2, 512:1024], bank[4 + i % 2][0:r, :], ACT.Copy), hi_made)
            act.wait_ge(max_made, 2 * XH + 2)
            own(A(gates_, gates_, ACT.Exp), exp_made)

            def extra(e, first):
                n, r0 = load_rounds(act, e)
                with act.If(n > 0):
                    with act.Fori(0, n) as j:
                        r = act.snap(r0 + j)
                        act.wait_ge(ex_pe, r * XP + XPE["gather"])
                        A(flat3(ex_xg_lo), bank[3][:, :], ACT.Copy).then_inc(ex_actv, 1)
                        act.wait_ge(ex_dve, r * XD + XDVE["gate"])
                        A(sig_, gate_, ACT.Sigmoid, scale=1.702).then_inc(ex_actv, 1)
                        act.wait_ge(ex_pe, r * XP + XPE["gates"])
                        A(ex_cg_hi, bank[5][0:CAP, 0:T], ACT.Copy).then_inc(ex_actv, 1)
                        act.wait_ge(ex_pe, r * XP + XPE["output"])
                        for i in range(2):
                            last = A(ex_y_hi[:, 512 * i:512 * i + 512], bank[6 + i][0:CAP, :], ACT.Copy)
                        last.then_inc(ex_actv, 1)

            def results(e):
                act.wait_ge(w_free, e * EPI)
                at_least(act, scat_done, e * 8 - 8)
                for i in range(2):
                    last = A(y_hi[:, 512 * i:512 * i + 512], bank[6 + i][0:CAP, :], ACT.Copy)
                last.then_inc(yhi_evac, 1)

            def gates_in(e):
                act.wait_ge(cg_done, e)
                A(cg_hi, bank[5][0:CAP, 0:T], ACT.Copy).then_inc(cg_evac, 1)

            def expert(e, first, last_one):
                if not first:
                    results(e)
                    gates_in(e)
                act.wait_ge(gate_made, e + 1)
                A(sig_, gate_, ACT.Sigmoid, scale=1.702).then_inc(sigm_made, 1)
                if not last_one:
                    act.wait_ge(xg_done, e + 2)
                    A(flat3(xg_lo), bank[3][:, :], ACT.Copy).then_inc(xlo_evac, 1)

            act.wait_ge(rounds_made, 1)
            act.wait_ge(xg_done, 1)
            A(flat3(xg_lo), bank[3][:, :], ACT.Copy).then_inc(xlo_evac, 1)
            for e in (0, 1):
                extra(e, e == 0)
                expert(e, e == 0, False)
            with act.Fori(2, E - 1) as e:
                extra(e, False)
                expert(e, False, False)
            extra(E - 1, False)
            expert(E - 1, False, True)
            results(E)
            gates_in(E)
            act.wait_ge(scat_add, 8 * E)
            squares(lambda k: xT[:, k, :])
            take_root()
            for i in (1, 3, 5):
                r = TROWS[i // 2]
                act.wait_ge(tr_done, 76 + i + 1)
                A(y_rows[0:r, i // 2, 512:1024], bank[4 + i % 2][0:r, :], ACT.Copy).then_inc(tr_free[1], 1)
            act.wait_ge(tr_free[0], 41)
            act.wait_ge(tr_free[1], 41)
            act.dma_start(d["out_y_p"][0].rearrange("(t p) n -> p t n", p=P), y_rows[:, 0:2, :]).then_inc(stores, 16)
            act.dma_start(d["out_y_s"].rearrange("b s n -> (b s) n"), y_rows[0:NS, 2, :]).then_inc(stores, 16)
            act.wait_ge(stores, 16 * 5)
            act.wait_ge(st_conf_rows, 16 * (1 + NB))
            act.wait_ge(st_gdn_rows, 32)
            act.wait_ge(st_out, 32 * H)

        @block.vector
        def _(dve):
            own = chain(dve, dve_self)
            V = nc.vector
            tt, ts, stt, cp = V.tensor_tensor, V.tensor_scalar, V.scalar_tensor_tensor, V.tensor_copy
            sq, root, norm = [0], [0], [0]

            def norm_root(b, scale, eps, n=KC, cols_=T):
                sq[0] += n
                root[0] += 1
                dve.wait_ge(sq_used, sq[0])
                ts(SC[:, 2, 0:cols_], bank[b][:, 0:cols_], scale, eps, ALU.mult, ALU.add).then_inc(root_in, 1)
                dve.wait_ge(root_made, root[0])
                own(V.reciprocal(SC[:, 2, 0:cols_], SC[:, 2, 0:cols_]))

            def rms(src, gain, dst, b=6, cols_=T):
                norm_root(b, 1.0 / D, 1e-6, KC, cols_)
                norm[0] += 1
                for k in range(KC):
                    ins = stt(dst(k), src(k), vec(gain, k), SC[:, 2, 0:cols_], ALU.mult, ALU.mult)
                    own(ins, norm_made if k == KC - 1 else dve_self, norm[0] if k == KC - 1 else None)

            def read_bank(n, dst, shape, rows=P, w=512):
                dve.wait_ge(tr_done, n + 1)
                own(cp(dst, view(4 + n % 2, rows, w, shape)), tr_free[n % 2], n // 2 + 1)

            for n, (kind, srcs, dst, shape) in enumerate(in_jobs):
                read_bank(n, dst, shape, P, sum(r for _, r in srcs))
            rms(lambda k: xT[:, k, :], "norm_mix", lambda k: hT[:, k, :])
            for c in range(KC):
                j = J_GLU + 4 * (c // 2) + c % 2
                job_ready(dve, j)
                dve.wait_ge(sig_made, c + 1)
                if c == 0:
                    dve.wait_ge(pads_made, 1)
                own(tt(cvx[:, c, CM:CM + SEQ], proj_bank(j)[:, 0:SEQ], sg[:, c % 2, 0:SEQ], ALU.mult))
                own(tt(conf_new(c), s4(proj_bank(j)[:, SEQ:T]), s4(sg[:, c % 2, SEQ:T]), ALU.mult),
                    proj_free[j % 4], j // 4 + 1)
                own(cp(conf_tail[:, c, 0:CM], cvx[:, c, SEQ:CM + SEQ]), proj_free[(j + 2) % 4], (j + 2) // 4 + 1)
                own(cp(s4(conf_tail[:, c, CM:CM + NS]), conf_new(c)), conf_tail_made)
            for c in range(KC):
                acc = bank[6][:, 0:SEQ]
                own(ts(acc, cvx[:, c, 0:SEQ], conf_w(0, c), vec("conf_conv_b", c), ALU.mult, ALU.add))
                for j in range(1, CW):
                    own(stt(acc, cvx[:, c, j:j + SEQ], conf_w(j, c), acc, ALU.mult, ALU.add))
                own(cp(cvx[:, c, 0:SEQ], acc))
            dve.wait_ge(conf_s_made, 1)
            for c in range(KC):
                own(ts(s4(cvx[:, c, SEQ:T]), conf_acc[:, c], vec("conf_conv_b", c), None, ALU.add), conf_made)
            dve.wait_ge(st_conf_rows, 16 * (1 + NB))
            for c in range(KC):
                j = J_Z + c
                dve.wait_ge(sig_made, KC + c + 1)
                own(tt(zs[:, c, :], proj_bank(j), sg[:, c % 2, :], ALU.mult), proj_free[j % 4], j // 4 + 1)
            for c in range(QC):
                j = J_QKV + c
                job_left(dve, j)
                own(cp(gdn_tail[:, c, 0:GM], qkv[:, c, SEQ:GM + SEQ]))
                own(cp(gdn_tail[:, c, GM:GM + NB * GM].rearrange("p (b s) -> p b s", s=GM),
                       gdn_hist[:, c, :, DT:DT + GM]), gdn_tail_made)

            def swish(c):
                dve.wait_ge(sig_made, 2 * KC + c + 1)
                own(tt(qkv[:, c, 0:T], bank[6 + c % 2][:, 0:T], sg[:, c % 2, :], ALU.mult), conv_made)

            for c in range(QC):
                acc = bank[6 + c % 2][:, 0:SEQ]
                acs = s4(bank[6 + c % 2][:, SEQ:T])
                own(ts(acc, qkv[:, c, 0:SEQ], gdn_w(0, c), None, ALU.mult))
                own(ts(acs, gdn_hist[:, c, :, 0:DT], gdn_w(0, c), None, ALU.mult))
                for i in range(1, GC):
                    own(stt(acc, qkv[:, c, i:i + SEQ], gdn_w(i, c), acc, ALU.mult, ALU.add))
                    own(stt(acs, gdn_hist[:, c, :, i:i + DT], gdn_w(i, c), acs, ALU.mult, ALU.add),
                        acc_made if i == GC - 1 else dve_self)
                if c:
                    swish(c - 1)
            swish(QC - 1)
            dve.wait_ge(mean_done, 1)
            own(ts(SC[:, 2, :], bank[6][:, 0:T], 1.0 / D, None, ALU.mult), mean_read)
            for k in range(KC):
                own(tt(cvx[:, k, 0:T], cvx[:, k, 0:T], SC[:, 2, :], ALU.subtract), centred)
            norm_root(6, 1.0 / D, 1e-5)
            for k in range(KC):
                own(stt(cvx[:, k, 0:T], cvx[:, k, 0:T], vec("conf_ln_g", k), SC[:, 2, :], ALU.mult, ALU.mult), scaled)
                if k:
                    dve.wait_ge(sig_made, 2 * KC + QC + k)
                    own(stt(cvx[:, k - 1, 0:T], cvx[:, k - 1, 0:T], vec("conf_ln_b", k - 1), sg[:, (k - 1) % 2, :],
                            ALU.add, ALU.mult), silu_made)
            dve.wait_ge(sig_made, 3 * KC + QC)
            norm[0] += 1
            own(stt(cvx[:, KC - 1, 0:T], cvx[:, KC - 1, 0:T], vec("conf_ln_b", KC - 1), sg[:, (KC - 1) % 2, :],
                    ALU.add, ALU.mult), norm_made, norm[0])
            dve.wait_ge(ab_done, 1)
            dve.wait_ge(masks_made, 2)
            own(cp(ab[:, 0:2, :].rearrange("p t n -> p (t n)"), bank[4][:, 0:32]))
            own(cp(ab[0:NS, 2, :], bank[4][0:NS, 32:48]))
            own(tt(tmp_b, ab[:, :, 0:H], abias[:, 0:1, :].to_broadcast((P, TT, H)), ALU.add))
            own(stt(tmp_a, tmp_b, -1.0, tmp_b, ALU.mult, ALU.max), ab_dve)
            for c in range(KC):
                j = J_PW2 + c
                job_ready(dve, j)
                own(stt(gate_b[:, c, :], proj_bank(j), vec("conf_pw2_b", c), gate_b[:, c, :], ALU.add, ALU.mult),
                    proj_free[j % 4], j // 4 + 1)
            for b in (2, 3):
                last = own(V.memset(bank[b][:, 2 * P:3 * P], 0.0), banks_clear if b == 3 else dve_self)
            dve.wait_ge(ab_act, 2)
            own(stt(tmp_b, tmp_b, 0.0, tmp_a, ALU.max, ALU.add))
            own(stt(gl, tmp_b, -1.0, ea.unsqueeze(1).to_broadcast((P, TT, H)), ALU.mult, ALU.mult), gl_made)

            def l2(n0, count, finish, scale, eps):
                for n in range(n0, n0 + count + 1):
                    if n < n0 + count:
                        sq[0] += 1
                        dve.wait_ge(sq_used, sq[0])
                        a, b = (scale(n), eps(n))
                        own(ts(sg[:, n % 2, :], bank[4 + n % 2][:, 0:T], a, b, ALU.mult, ALU.add), l2_read)
                    if n > n0:
                        m = n - 1
                        dve.wait_ge(l2_root, n)
                        own(V.reciprocal(sg[:, m % 2, :], sg[:, m % 2, :]))
                        finish(m)

            def unit(m):
                own(tt(qkv[:, m, 0:T], qkv[:, m, 0:T], sg[:, m % 2, :], ALU.mult), unit_made)

            l2(0, 2 * H, unit, lambda n: float(P) if n < H else 1.0, lambda n: (float(P) if n < H else 1.0) * 1e-6)
            dve.wait_ge(gc_done, 1)
            own(cp(gc, bank[7][:, 0:24].rearrange("p (t n) -> p t n", t=TT)), gc_read)
            dve.wait_ge(ab_act, 3)
            own(tt(kb_s, tmp_a, beta, ALU.mult))

            def tile_rows(t):
                return slice(0, P if t < 2 else NS)

            for h in range(H):
                P_ = lambda name: step(dve, g_pe, PE_STEPS, h, name)
                A_ = lambda name: step(dve, g_act, ACT_STEPS, h, name)
                own(cp(G["kbg"], gl[:, :, h:h + 1].to_broadcast((P, TT, P))))
                own(cp(G["kd"], beta[:, :, h:h + 1].to_broadcast((P, TT, P))), g_dve)
                A_("eg")
                for t in range(TT):
                    own(ts(G["decay"][:, t, :], bank[0][:, P * t:P * (t + 1)], gc[:, t, h:h + 1], 0.0,
                           ALU.subtract, ALU.min), g_dve if t == 2 else dve_self)
                A_("exp")
                own(tt(G["decay"][:, 0:2, :], G["decay"][:, 0:2, :], causal[:, 0:1, :].to_broadcast((P, 2, P)), ALU.mult))
                own(tt(G["decay"][:, 2, :], G["decay"][:, 2, :], causal[:, 1, :], ALU.mult), g_dve)
                fl = lambda n_: G[n_].rearrange("p a b -> p (a b)")
                own(tt(fl("mt"), bank[2][:, 0:w3], fl("decay"), ALU.mult))
                own(tt(fl("mt"), bank[1][:, 0:w3], fl("mt"), ALU.mult))
                own(tt(fl("pt"), bank[3][:, 0:w3], fl("decay"), ALU.mult))
                own(tt(G["ct0"], G["mt"], level_mask[:, 0:1, :].to_broadcast((P, TT, P)), ALU.mult))
                own(tt(G["xt"], ident[:, :].unsqueeze(1).to_broadcast((P, TT, P)), G["ct0"], ALU.subtract), g_dve)
                own(tt(k_last_p, G["decay"][0:NS, 2, 0:NS], last_of[:, :], ALU.mult))
                own(V.tensor_reduce(k_last, k_last_p, AX, ALU.add))
                P_("turned")
                for t in range(TT):
                    r = tile_rows(t)
                    kd_s = G["decay"][:, t, P - 1:P] if t < 2 else k_last
                    kt, vt = bank[4][r, P * t:P * (t + 1)], bank[5][r, P * t:P * (t + 1)]
                    own(ts(G["kbg"][r, t, :], kt, kb_s[r, t, h:h + 1], None, ALU.mult))
                    own(ts(G["kd"][r, t, :], kt, kd_s, None, ALU.mult))
                    own(ts(G["vb"][r, t, :], vt, beta[r, t, h:h + 1], None, ALU.mult), g_dve if t == 2 else dve_self)
                A_("x0")
                for l in range(1, LEVELS):
                    n = w3 if l == 1 else 2 * P
                    P_(f"z{l}")
                    if l < LEVELS - 1:
                        own(tt(fl("x")[:, 0:n], fl("x")[:, 0:n], bank[6][:, 0:n], ALU.subtract))
                    own(tt(fl("xt")[:, 0:n], fl("xt")[:, 0:n], bank[2][:, 0:n], ALU.subtract), g_dve)
                own(tt(fl("qg")[:, 0:T], qkv[:, h, 0:T], fl("eg")[:, 0:T], ALU.mult))
                own(cp(w_q[:, :, 1, :], s4(fl("qg")[:, SEQ:T])))
                A_("nwt")
                own(cp(w_q[:, :, 0, :], s4(fl("nwt")[:, SEQ:T])), g_dve)
                P_("vn0")
                own(cp(vn0, bank[7][:, 0:P]), g_dve)
                P_("vn1")
                own(cp(vn1, bank[7][:, 2 * P:3 * P]), g_dve)
                P_("sample")
                A_("ws")
                own(tt(s4(vnT_s), s4(bank[5][:, 0:NS]), w_q_s[:, :, 0, :], ALU.add), g_dve)
                P_("vnt")
                own(cp(vn_s, bank[5][0:NS, P:2 * P]), g_dve)
                own(tt(v_wide, vn_s.unsqueeze(1).to_broadcast((NS, NB, P)),
                       batch_of[:, :].unsqueeze(2).to_broadcast((NS, NB, P)), ALU.mult), g_dve)
                P_("out")
                own(cp(qkv[:, 2 * H + h, 0:SEQ], bank[6][:, 0:SEQ]))
                own(tt(s4(qkv[:, 2 * H + h, SEQ:T]), s4(bank[6][:, SEQ:T]), w_q_s[:, :, 1, :], ALU.add))
                own(stt(s_fin, s_one, G["eg"][:, 1, P - 1:P], bank[3][:, 0:P], ALU.mult, ALU.add))
                own(tt(states, states, G["eg"][:, 2, DT - 1:NS:DT].unsqueeze(2).to_broadcast((P, NB, P)), ALU.mult))
                for i in range(2):
                    s_ = states[:, 4 * i:4 * i + 4, :].rearrange("p b n -> p (b n)")
                    own(tt(s_, s_, bank[i][:, :], ALU.add), g_dve if i else dve_self)

            def head_norm(m):
                h = m - 2 * H
                own(stt(qkv[:, m, 0:T], qkv[:, m, 0:T], vec("gdn_norm", 0), sg[:, m % 2, :], ALU.mult, ALU.mult))
                own(tt(qkv[:, m, 0:T], qkv[:, m, 0:T], zs[:, h, :], ALU.mult), o_made)
            dve.wait_ge(st_out, 32 * H)
            l2(2 * H, H, head_norm, lambda n: 1.0 / P, lambda n: 1e-6)
            for c in range(KC):
                j = J_O + c
                job_ready(dve, j)
                own(tt(gate_a[:, c, :], proj_bank(j), gate_a[:, c, :], ALU.mult))
                own(tt(gate_a[:, c, :], gate_a[:, c, :], gate_b[:, c, :], ALU.add), proj_free[j % 4], j // 4 + 1)

            def residual(j0):
                for c in range(KC):
                    j = j0 + c
                    job_ready(dve, j)
                    own(tt(xT[:, c, :], xT[:, c, :], proj_bank(j), ALU.add), proj_free[j % 4], j // 4 + 1)
            residual(J_OUT)
            for i in range(4):
                read_bank(30 + i, memT[:, 4 * (i % 2):4 * (i % 2) + 4, P * (i // 2):P * (i // 2 + 1)], (4, P))
            rms(lambda k: memT[:, k, :], "norm_mem", lambda k: memT[:, k, :], 7, ML)
            rms(lambda k: xT[:, k, :], "norm_xa", lambda k: hT[:, k, :])
            sc = XC ** -0.5 * P ** -0.5

            def row_max(u, b):
                own(V.tensor_reduce(stat[:, 32 + u:33 + u], bank[b][:, 0:ML], AX, ALU.max))
                own(ts(stat[:, u:u + 1], stat[:, 32 + u:33 + u], -sc, None, ALU.mult), max_made)

            def divide(u, p_):
                dve.wait_ge(exp_made, u + 1)
                own(V.reciprocal(stat[:, 16 + u:17 + u], stat[:, 16 + u:17 + u]))
                own(ts(probs[:, p_, :], probs[:, p_, :], stat[:, 16 + u:17 + u], None, ALU.mult), probs_made)

            NU = 2 * XH
            for u in range(NU + 1):
                if u < NU:
                    dve.wait_ge(scores_done, u + 1)
                    row_max(u, 4 + u % 2)
                if u:
                    v = u - 1
                    divide(v, v % 2)
                    dve.wait_ge(pt_done, v + 1)
                    if v >= 2:
                        dve.wait_ge(xo_done, v - 1)
                    own(cp(probsT[:, v % 2], bank[6 + v % 2][:, 0:ML].rearrange("p (m n) -> p m n", m=2)), pt_made)
            for b in range(NB):
                for i in (0, 2):
                    if i == 0 and b >= 2:
                        dve.wait_ge(s_scores, b - 1)
                    read_bank(38 + 4 * b + i, kT_b[:, b % 2, 0:4, P * (i // 2):P * (i // 2 + 1)], (4, P))
            dve.wait_ge(scores_done, NU + 1)
            row_max(NU, 7)
            divide(NU, 1)
            dve.wait_ge(pt_done, NU + 1)
            own(cp(probsT[:, 0], bank[6][:, 0:ML].rearrange("p (m n) -> p m n", m=2)), pt_made)
            residual(J_XO)
            rms(lambda k: xT[:, k, :], "norm_ffn", lambda k: hT[:, k, :])
            for i in (0, 2, 4):
                r = TROWS[i // 2]
                dve.wait_ge(tr_done, 70 + i + 1)
                own(cp(tok_hi[0:r, i // 2, 0:512], bank[4 + i % 2][0:r, :]))
                own(tt(tok_lo[0:r, i // 2, 0:512], bank[4 + i % 2][0:r, :], tok_hi[0:r, i // 2, 0:512], ALU.subtract),
                    tr_free[0], (70 + i) // 2 + 1)
                dve.wait_ge(hi_made, i // 2 + 1)
                own(tt(tok_lo[0:r, i // 2, 512:D], bank[5][0:r, :], tok_hi[0:r, i // 2, 512:D], ALU.subtract),
                    tr_free[1], (70 + i) // 2 + 1)
            own(V.memset(logits, 0.0))
            own(V.memset(gates_, 0.0))
            own(V.memset(top, 0.0))
            dve.wait_ge(logits_done, 1)
            for t in range(TT):
                r = TROWS[t]
                own(tt(logits[0:r, t, :], bank[6][0:r, E * t:E * (t + 1)], rbias[0:r, :], ALU.add))
                own(V.max(top[0:r, t, :], logits[0:r, t, :]))
            fourth = top[:, :, TOPK - 1:TOPK].to_broadcast((P, TT, E))
            first_ = top[:, :, 0:1].to_broadcast((P, TT, E))
            own(tt(chosen, logits, fourth, ALU.is_gt))
            own(tt(run_a, logits, fourth, ALU.is_equal))
            own(cp(ties, run_a))
            own(V.tensor_reduce(need, chosen, AX, ALU.add))
            own(ts(need, need, -1.0, float(TOPK), ALU.mult, ALU.add))

            def running(a, b, n, rows):
                s = 1
                while s < n:
                    own(cp(b[rows, :, 0:s], a[rows, :, 0:s]))
                    own(tt(b[rows, :, s:n], a[rows, :, s:n], a[rows, :, 0:n - s], ALU.add))
                    a, b = b, a
                    s *= 2
                return a
            run = running(run_a, run_b, E, slice(0, P))
            own(tt(run, run, need.unsqueeze(2).to_broadcast((P, TT, E)), ALU.is_le))
            own(tt(run, run, ties, ALU.mult))
            own(tt(chosen, chosen, run, ALU.add), chosen_made)
            own(tt(gates_, logits, first_, ALU.subtract), max_made)
            dve.wait_ge(exp_made, NU + 2)
            own(tt(gates_, gates_, chosen, ALU.mult))
            own(V.tensor_reduce(need, gates_, AX, ALU.add))
            own(V.reciprocal(need, need))
            own(tt(gates_, gates_, need.unsqueeze(2).to_broadcast((P, TT, E)), ALU.mult), gates_made)
            dve.wait_ge(gates_T_done, 1)
            own(cp(gates_T, bank[0][0:E, 0:T]), gates_T_made)
            own(V.memset(place, -1.0))
            own(V.memset(ex_off, float(CAP)))
            dve.wait_ge(stores, 48)
            dve.wait_ge(counts_done, 1)
            for t in range(TT):
                r = TROWS[t]
                own(tt(place[0:r, t, :], bank[7][0:r, E * t:E * (t + 1)], chosen[0:r, t, :], ALU.mult))
                own(ts(place[0:r, t, :], place[0:r, t, :], -1.0, None, ALU.add))
            cnt = bank[7][0:1, E * TT:E * (TT + 1)]
            own(ts(rounds_f[:, 0, :], cnt, float(CAP), None, ALU.is_gt))
            for j in range(2, (T - 1) // CAP + 1):
                own(stt(rounds_f[:, 0, :], cnt, float(CAP * j), rounds_f[:, 0, :], ALU.is_gt, ALU.add))
            own(cp(rounds_f[:, 1, :], rounds_f[:, 0, :]))
            r_ = running(rounds_f[:, 1:2, :], rounds_f[:, 2:3, :], E, slice(0, 1))
            own(tt(rounds_f[:, 3:4, :], r_, rounds_f[:, 0:1, :], ALU.subtract))
            own(cp(rounds[:, 0, :], rounds_f[:, 0, :]))
            own(cp(rounds[:, 1, :], rounds_f[:, 3, :]), rounds_made)

            for c in range(KC):
                dve.wait_ge(b2_done, c + 1)
                own(tt(xT[:, c, :], xT[:, c, :], bank[4 + c % 2][:, 0:T], ALU.add), b2_added)

            def one_hot(dst, place_, t):
                r = TROWS[t]
                return ts(dst[0:r, t, :], slot_id[0:r, :], place_(t, r), None, ALU.is_equal)

            def gate_hot(dst, place_, e, t):
                r = TROWS[t]
                return ts(dst[0:r, t, :], slot_id[0:r, :], place_(t, r), gates_[0:r, t, bass.ds(e, 1)],
                          ALU.is_equal, ALU.mult)

            def bias1(e, lin):
                return prm[:, bass.ds(e * 16 + (B1O + 8 * lin), 8)].unsqueeze(2).to_broadcast((P, FC, CAP))

            def swiglu(e, link, first_sig, sig_wait, act_out, last_sig):
                hb = lambda i: bank[1 + i][:, :].rearrange("p (f n) -> p f n", f=FC)
                g3, l3 = gate_.rearrange("p (f n) -> p f n", f=FC), lin_.rearrange("p (f n) -> p f n", f=FC)
                link(tt(g3, hb(0), bias1(e, 0), ALU.add))
                link(ts(gate_, gate_, 7.0, None, ALU.min), first_sig)
                link(tt(l3, hb(1), bias1(e, 1), ALU.add))
                link(ts(lin_, lin_, 7.0, -7.0, ALU.min, ALU.max))
                link(stt(lin_, lin_, 1.0, gate_, ALU.add, ALU.mult))
                sig_wait()
                link(tt(act_out.rearrange("p f n -> p (f n)"), lin_, sig_, ALU.mult), last_sig)

            def low(e, k):
                w = ring[:, w_slot(k), :]
                dve.wait_ge(w_here[w_slot(k)], e * 16 + w_count(k))
                tt(w_lo[k], w, high(w), ALU.subtract).then_inc(lo_made, 1)

            def extra(e, first):
                n, r0 = load_rounds(dve, e)
                with dve.If(n > 0):
                    pc = lambda t, r: ex_place[0:r, t:t + 1]
                    c0 = [0]
                    with dve.Fori(0, n) as j:
                        r = dve.snap(r0 + j)

                        def link(ins, *_):
                            c0[0] += 1
                            ins.then_inc(ex_dve, 1)
                            dve.wait_ge(ex_dve, r * XD + c0[0])
                        link(ts(ex_place, place[:, :, bass.ds(e, 1)].rearrange("p t o -> p (t o)"),
                                ex_off[:, bass.ds(e, 1)], None, ALU.subtract))
                        for t in range(TT):
                            link(one_hot(ex_onehot, pc, t))
                        assert c0[0] == XDVE["onehot"]
                        for t in range(TT):
                            link(gate_hot(ex_pg, pc, e, t))
                        link(ts(ex_off[:, bass.ds(e, 1)], ex_off[:, bass.ds(e, 1)], float(CAP), None, ALU.add))
                        dve.wait_ge(ex_pe, r * XP + XPE["gather"])
                        link(cp(flat3(ex_xg_hi), bank[0][:, :]))
                        assert c0[0] == XDVE["xg"]
                        dve.wait_ge(ex_pe, r * XP + XPE["hidden"])
                        swiglu(e, link, None, lambda: dve.wait_ge(ex_actv, r * XA + XACT["sig"]), ex_act, None)
                        assert c0[0] == XDVE["act"] and XDVE["gate"] == XDVE["act"] - 4
                        dve.wait_ge(ex_actv, r * XA + XACT["cg"])
                        link(tt(ex_cg_lo, bank[5][0:CAP, 0:T], ex_cg_hi, ALU.subtract))
                        dve.wait_ge(ex_actv, r * XA + XACT["y"])
                        for i in range(2):
                            c_ = slice(512 * i, 512 * i + 512)
                            link(tt(ex_y_lo[:, c_], bank[6 + i][0:CAP, :], ex_y_hi[:, c_], ALU.subtract))
                        assert c0[0] == XDVE["y"]
                        for c in range(KC):
                            dve.wait_ge(ex_pe, r * XP + XPE["scatter"] + c)
                            link(tt(xT[:, c, :], xT[:, c, :], bank[4 + c % 2][:, 0:T], ALU.add))
                        assert c0[0] == XD

            N_E = 4

            def hot_gates(e):
                at_least(dve, cg_done, e - 1)
                for t in range(TT):
                    last = gate_hot(pg, lambda t, r: place[0:r, t, bass.ds(e - 1, 1)], e - 1, t)
                last.then_inc(pg_made, 1)

            def y_low(e):
                dve.wait_ge(yhi_evac, e)
                for i in range(2):
                    c_ = slice(512 * i, 512 * i + 512)
                    last = tt(y_lo[:, c_], bank[6 + i][0:CAP, :], y_hi[:, c_], ALU.subtract)
                last.then_inc(ylo_made, 1)

            def cg_low(e):
                dve.wait_ge(cg_evac, e)
                tt(cg_lo, bank[5][0:CAP, 0:T], cg_hi, ALU.subtract).then_inc(cgl_made, 1)

            def add_in(e):
                for c in range(KC):
                    dve.wait_ge(scat_done, e * 8 - 8 + (c + 1))
                    tt(xT[:, c, :], xT[:, c, :], bank[4 + c % 2][:, 0:T], ALU.add).then_inc(scat_add, 1)

            def expert(e, first, last_one, at_):
                n = [0]

                def link(ins, s=None, v=None):
                    if s is None:
                        n[0] += 1
                        ins.then_inc(ex_self, 1)
                        dve.wait_ge(ex_self, at_ + n[0])
                    else:
                        ins.then_inc(s, 1)
                        dve.wait_ge(s, v)
                if not first:
                    hot_gates(e)
                if not last_one:
                    dve.wait_ge(xg_done, e + 1)
                    for t in range(TT):
                        last = one_hot(onehot, lambda t, r: place[0:r, t, bass.ds(e + 1, 1)], t)
                    last.then_inc(p_made, 1)
                if not first:
                    y_low(e)
                dve.wait_ge(w_free, e * EPI + KC)

                def swi_link(ins, s=None):
                    link(ins, s, None if s is None else e + 1)
                swiglu(e, swi_link, gate_made, lambda: dve.wait_ge(sigm_made, e + 1), act_, act_made)
                if not first:
                    cg_low(e)
                if not last_one:
                    dve.wait_ge(xg_done, e + 2)
                    cp(flat3(xg_hi), bank[0][:, :]).then_inc(xg_evac, 1)
                if not first:
                    add_in(e)
                if not last_one:
                    for k in range(KC):
                        low(e + 1, k)
                assert n[0] == N_E, n[0]

            for t in range(TT):
                ins = one_hot(onehot, lambda t, r: place[0:r, t, 0:1], t)
                own(ins, p_made if t == 2 else dve_self)
            for k in range(KC):
                low(0, k)
            dve.wait_ge(xg_done, 1)
            own(cp(flat3(xg_hi), bank[0][:, :]), xg_evac)
            for e in (0, 1):
                extra(e, e == 0)
                expert(e, e == 0, False, e * N_E)
            with dve.Fori(2, E - 1) as e:
                extra(e, False)
                expert(e, False, False, e * N_E)
            extra(E - 1, False)
            expert(E - 1, False, True, (E - 1) * N_E)
            hot_gates(E)
            y_low(E)
            cg_low(E)
            add_in(E)
            rms(lambda k: xT[:, k, :], "norm_final", lambda k: hT[:, k, :])
            for i in (0, 2, 4):
                r = TROWS[i // 2]
                dve.wait_ge(tr_done, 76 + i + 1)
                own(cp(y_rows[0:r, i // 2, 0:512], bank[4 + i % 2][0:r, :]), tr_free[0], (76 + i) // 2 + 1)


INS = ["x_prompt", "x_sample", "mem_prompt", "state_gdn", "state_gdn_conv", "state_conf_conv", "cache_mem_k",
       "cache_mem_v", "norm_mix", "w_in", "gdn_conv_w", "gdn_a_log", "gdn_dt_bias", "gdn_norm", "gdn_o",
       "conf_conv_w", "conf_conv_b", "conf_ln_g", "conf_ln_b", "conf_pw2", "conf_pw2_b", "w_out", "norm_xa",
       "norm_mem", "xa_q", "xa_kv", "xa_o", "norm_ffn", "router_w", "router_b", "moe_w1", "moe_b1", "moe_w2",
       "moe_b2", "norm_final"]
OUTS = [("y_p", (1, SEQ, D)), ("y_s", (NB, DT, D)), ("state_p", (1, 1, H, P, P)), ("gconv_p", (1, 1, GM, QC * P)),
        ("conf_p", (1, 1, CM, D)), ("mem_k", (1, 1, ML, XH, XC * P)), ("mem_v", (1, 1, ML, XH, XC * P)),
        ("state_s", (1, NB, H, P, P)), ("gconv_s", (1, NB, GM, QC * P)), ("conf_s", (1, NB, CM, D))]


def kernel(**inputs):
    import numpy as np
    import concourse.bacc as bacc
    from concourse.bass_utils import run_bass_kernel_spmd

    nc = bacc.Bacc("TRN2", target_bir_lowering=False, num_devices=1)
    arrays, d = {}, {}
    for name in INS:
        arrays[f"in_{name}"] = np.ascontiguousarray(inputs[name])
        d[name] = nc.dram_tensor(f"in_{name}", arrays[f"in_{name}"].shape, F32, kind="ExternalInput").ap()
    for name, shape in OUTS:
        d[f"out_{name}"] = nc.dram_tensor(f"out_{name}", shape, F32, kind="ExternalOutput").ap()
    build(nc, d)
    r = run_bass_kernel_spmd(nc, [arrays], core_ids=[0])
    return tuple(r.results[0][f"out_{name}"] for name, _ in OUTS)
```

```python
from contextlib import ExitStack

import concourse.bass as bass
from concourse import mybir

F32 = mybir.dt.float32
I32 = mybir.dt.int32
BF16 = mybir.dt.bfloat16
ALU = mybir.AluOpType
ACT = mybir.ActivationFunctionType
AX = mybir.AxisListType.X

P = 128
D = 1024
KC = D // P
SEQ, NB, DT = 256, 8, 4
NS = NB * DT
T = SEQ + NS
TT = (T + P - 1) // P
TROWS = [P, P, NS]
H = 8
GC = 4
QC = 3 * H
GM = GC - 1
GLEN = GM + SEQ + NB * (GM + DT)
CW = 31
CM = CW - 1
CLEN = CM + SEQ + NB * (CM + DT)
ML = 256
XH, XC = 4, 2
E, TOPK = 32, 4
FC = D // P
CAP = 64
LEVELS = 7
RING = 12
PCOL = 256
EPI = 12


def build(nc, d):
    with ExitStack() as ctx:
        def sb(name, shape, dt=F32):
            return ctx.enter_context(nc.sbuf_tensor(name, shape, dt))

        def sem(name):
            return ctx.enter_context(nc.semaphore(name))

        bank = [ctx.enter_context(nc.psum_tensor(f"bank{i}", [P, 512], F32)) for i in range(8)]

        ident = sb("ident", [P, P])
        ones = sb("ones", [P, P])
        level_mask = sb("level_mask", [P, LEVELS, P])
        causal = sb("causal", [P, 2, P])
        batch_of = sb("batch_of", [NS, NB])
        last_of = sb("last_of", [NS, NS])
        pick = sb("pick", [P, 4 * H - 1])
        slot_id = sb("slot_id", [P, CAP])
        slot_int = sb("slot_int", [P, CAP], I32)
        NPT = 10
        prm = sb("prm", [P, NPT * P])
        abias = sb("abias", [P, 2, H])
        rbias = sb("rbias", [P, E])
        w_ab = sb("w_ab", [P, KC, 2 * H])
        w_router = sb("w_router", [P, KC, E])

        ring = sb("ring", [P, RING, 2048])
        xT = sb("xT", [P, KC, T])
        hT = sb("hT", [P, KC, T])
        arena = sb("arena", [P, 19200])
        SC = sb("SC", [P, 3, T])
        sg = sb("sg", [P, 2, T])
        rounds = sb("rounds", [1, 2, E], I32)

        A_QKV, A_Z = 0, QC * GLEN
        A_CV = A_Z + KC * T
        A_SA = A_CV + KC * CLEN
        A_SB = A_SA + KC * T
        assert A_SB + KC * T <= 19200

        def at(off, *shape):
            n = 1
            for s in shape:
                n *= s
            v = arena[:, off:off + n]
            if len(shape) == 2:
                return v.rearrange("p (a b) -> p a b", a=shape[0])
            if len(shape) == 3:
                return v.rearrange("p (a b c) -> p a b c", a=shape[0], b=shape[1])
            return v

        qkv = at(A_QKV, QC, GLEN)
        zs = at(A_Z, KC, T)
        cvx = at(A_CV, KC, CLEN)
        gate_a = at(A_SA, KC, T)
        gate_b = at(A_SB, KC, T)
        st_x = at(A_QKV, TT, D)
        st_conf = at(A_Z, 2, D)
        st_gdn = at(A_SA, QC * P)
        st_par = at(A_SA + QC * P, NPT, P)
        assert QC * P + NPT * P <= 2 * KC * T

        VEC = {}
        for n, name in enumerate(["norm_mix", "norm_xa", "norm_mem", "norm_ffn", "norm_final",
                                  "conf_conv_b", "conf_ln_g", "conf_ln_b", "conf_pw2_b"]):
            VEC[name] = 8 * n
        VEC["gdn_norm"] = 72
        GW, CWO, B1O, B2O = P, 2 * P, 4 * P, 8 * P

        def vec(name, k):
            return prm[:, VEC[name] + k:VEC[name] + k + 1]

        def gdn_w(j, c):
            return prm[:, GW + QC * j + c:GW + QC * j + c + 1]

        def conf_w(j, c):
            r = KC * j + c
            r = r if r < 124 else r + 4
            return prm[:, CWO + r:CWO + r + 1]

        def cols(w, j):
            return w[0].rearrange("(k p) n -> p k n", p=P)[:, :, PCOL * j:PCOL * (j + 1)]

        def cols_at(w, c0):
            return w[0].rearrange("(k p) n -> p k n", p=P)[:, :, c0:c0 + PCOL]

        NQKV, NV = QC * P, H * P
        C_Z, C_A = NQKV, NQKV + NV
        C_GLU = C_A + 2 * H
        C_GATE = C_GLU + 2 * D
        W = d["w_in"]
        pieces = []
        for j in range(4):
            pieces += [cols_at(W, C_GLU + PCOL * j), cols_at(W, C_GLU + D + PCOL * j)]
        pieces += [cols(W, j) for j in range(NQKV // PCOL)]
        pieces += [cols_at(W, C_Z + PCOL * j) for j in range(4)]
        pieces += [cols_at(W, C_GATE + PCOL * j) for j in range(8)]
        for name in ("conf_pw2", "gdn_o", "w_out"):
            pieces += [cols(d[name], j) for j in range(4)]
        pieces += [cols(d["xa_kv"], j) for j in range(8)]
        pieces += [cols(d["xa_q"], j) for j in range(4)]
        for name in ("cache_mem_k", "cache_mem_v"):
            for b in range(NB):
                pieces.append(d[name][0, b].rearrange("(m p) h e -> p m (h e)", p=P))
        pieces += [cols(d["xa_o"], j) for j in range(4)]
        PRE = len(pieces)

        def dense(n):
            return ring[:, n % RING, :].rearrange("p (k n) -> p k n", k=KC)

        def wide(n):
            return ring[:, n % RING, :].rearrange("p (k n) -> p k n", k=2)

        w_here = [sem(f"w_here{i}") for i in range(RING)]
        w_free = sem("w_free")

        ld_x, ld_par, ld_conf, ld_gdn, ld_small = [sem(f"ld_{n}") for n in ("x", "par", "conf", "gdn", "small")]
        ld_mem, ld_state, masks_made, pads_made, tr_done, proj_done = [
            sem(n) for n in ["ld_mem", "ld_state", "masks_made", "pads_made", "tr_done", "proj_done"]]
        sq_made, sq_used, root_in, root_made, norm_made, act_self = [
            sem(n) for n in ["sq_made", "sq_used", "root_in", "root_made", "norm_made", "act_self"]]
        dve_self, pool_self, sig_made, acc_made, ab_done, ab_dve = [
            sem(n) for n in ["dve_self", "pool_self", "sig_made", "acc_made", "ab_done", "ab_dve"]]
        ab_act, g_pe, g_dve, g_act, g_pool, st_out = [
            sem(n) for n in ["ab_act", "g_pe", "g_dve", "g_act", "g_pool", "st_out"]]
        stores, conf_tail_made, conf_s_made, conf_made, conv_made = [
            sem(n) for n in ["stores", "conf_tail_made", "conf_s_made", "conf_made", "conv_made"]]
        mean_done, mean_read, centred, scaled, silu_made, st_conf_rows = [
            sem(n) for n in ["mean_done", "mean_read", "centred", "scaled", "silu_made", "st_conf_rows"]]
        st_gdn_rows, l2_read, gl_made, banks_clear, gc_done = [
            sem(n) for n in ["st_gdn_rows", "l2_read", "gl_made", "banks_clear", "gc_done"]]
        gc_read, o_made, scores_done, max_made, exp_made = [
            sem(n) for n in ["gc_read", "o_made", "scores_done", "max_made", "exp_made"]]
        probs_made, pt_done, pt_made, xo_done, xo_made, s_scores = [
            sem(n) for n in ["probs_made", "pt_done", "pt_made", "xo_done", "xo_made", "s_scores"]]
        sT_made, v_used, logits_done, chosen_made, counts_done, rounds_made = [
            sem(n) for n in ["sT_made", "v_used", "logits_done", "chosen_made", "counts_done", "rounds_made"]]
        p_made, pg_made, xg_done, xg_evac, gate_made, sigm_made = [
            sem(n) for n in ["p_made", "pg_made", "xg_done", "xg_evac", "gate_made", "sigm_made"]]
        act_made, cg_done, cg_evac = [
            sem(n) for n in ["act_made", "cg_done", "cg_evac"]]
        scat_done, scat_add, ex_self, ex_pe, ex_dve, ex_actv = [
            sem(n) for n in ["scat_done", "scat_add", "ex_self", "ex_pe", "ex_dve", "ex_actv"]]
        lo_made, hi_made, gates_made, gates_T_done, gates_T_made, b2_done = [
            sem(n) for n in ["lo_made", "hi_made", "gates_made", "gates_T_done", "gates_T_made", "b2_done"]]
        b2_added, ld_b2, xlo_evac, yhi_evac, ylo_made, cgl_made = [
            sem(n) for n in ["b2_added", "ld_b2", "xlo_evac", "yhi_evac", "ylo_made", "cgl_made"]]
        scores_rows, decay_in, decay_exp, xt_start = [sem(n) for n in ["scores_rows", "decay_in", "decay_exp", "xt_start"]]
        rows_done, kv_turned, spread_made, decayed_states, st_prompt = [
            sem(n) for n in ["rows_done", "kv_turned", "spread_made", "decayed_states", "st_prompt"]]
        v_lo_made = sem("v_lo_made")
        z_made, l2_done, l2_inv = [sem(n) for n in ["z_made", "l2_done", "l2_inv"]]
        tr_free = [sem(f"tr_free{i}") for i in range(2)]
        proj_free = [sem(f"proj_free{i}") for i in range(4)]

        def chain(eng, s):
            n = {}

            def link(ins, signal=None, value=None, wait=True, lag=0):
                to = s if signal is None else signal
                n[to.name] = n.get(to.name, 0) + 1
                ins.then_inc(to, 1)
                if wait:
                    eng.wait_ge(to, n[to.name] - lag if value is None else value)
            return link

        in_jobs = []
        for t in range(TT):
            for half in range(2):
                r = TROWS[t]
                in_jobs.append(("x", [(st_x[0:r, t, P * (4 * half + i):P * (4 * half + i + 1)], r) for i in range(4)],
                                xT[:, 4 * half:4 * half + 4, P * t:P * t + r], (4, r)))
        PAR_ROWS = [73, 96, 124, 124] + [128] * 6
        for i, r in enumerate(PAR_ROWS):
            in_jobs.append(("par", [(st_par[0:r, i, :], r)], prm[:, P * i:P * i + r], None))
        conf_hist = cvx[:, :, CM + SEQ:CLEN].rearrange("p c (b s) -> p c b s", s=CM + DT)
        gdn_hist = qkv[:, :, GM + SEQ:GLEN].rearrange("p c (b s) -> p c b s", s=GM + DT)
        for u in range(2):
            for half in range(2):
                in_jobs.append(("conf", [(st_conf[0:120, u, P * (4 * half + i):P * (4 * half + i + 1)], 120)
                                         for i in range(4)],
                                conf_hist[:, 4 * half:4 * half + 4, 4 * u:4 * u + 4, 0:CM], (4, 4, CM)))
        for u in range(2):
            in_jobs.append(("gdn", [(st_gdn[0:NB * GM, P * (12 * u + i):P * (12 * u + i + 1)], NB * GM)
                                    for i in range(12)],
                            gdn_hist[:, 12 * u:12 * u + 12, :, 0:GM], (12, NB, GM)))
        loads = {"x": (ld_x, 16 * 2), "par": (ld_par, 16 * 15), "conf": (ld_conf, 16 * 2), "gdn": (ld_gdn, 16)}

        conf_tail = at(A_SA + QC * P + QC * 27, KC, CM + NS)
        gdn_tail = at(A_SA + QC * P, QC, GM + NB * GM)
        conf_rows = at(A_Z, D)
        gdn_rows = at(A_SA, QC * P)
        N_IN_JOBS = len(in_jobs)
        N_CONF_JOBS, N_GDN_JOBS = 2, 6

        def view(b, rows, n, shape):
            v = bank[b][0:rows, 0:n]
            if shape is None:
                return v
            if len(shape) == 2:
                return v.rearrange("p (a b) -> p a b", a=shape[0])
            return v.rearrange("p (a b c) -> p a b c", a=shape[0], b=shape[1])

        J_GLU, J_QKV, J_Z, J_GATE, J_PW2, J_O, J_OUT, J_KV, J_XQ, J_XO = 0, 16, 40, 48, 64, 72, 80, 88, 96, 104
        NP_GLU, NP_QKV, NP_Z, NP_GATE, NP_PW2, NP_O, NP_OUT = 0, 8, 20, 24, 32, 36, 40
        NP_KV, NP_XQ, NP_CACHE, NP_XO = 44, 52, 56, 72

        def job_ready(eng, j):
            eng.wait_ge(proj_done, j + 1)

        def job_left(eng, j):
            eng.wait_ge(proj_free[j % 4], j // 4 + 1)

        def proj_bank(j):
            return bank[j % 4][:, 0:T]

        def s4(ap):
            return ap.rearrange("p (b s) -> p b s", s=DT)

        def conf_new(c):
            return conf_hist[:, c, :, CM:CM + DT]


        hflat = hT[:, :, :].rearrange("p k t -> p (k t)")
        w3 = TT * P
        G = {}
        for n, name in enumerate(["decay", "mt", "pt", "x", "y", "ct0"]):
            G[name] = hflat[:, n * w3:(n + 1) * w3].rearrange("p (a b) -> p a b", a=TT)
        N_HELD = NP_O + RING - 1
        v_wide = ring[0:NS, N_HELD % RING, 0:NB * P].rearrange("p (b n) -> p b n", b=NB)
        row_sel = hflat[0:2 * H, 0:2 * H * P].rearrange("p (n m) -> p n m", n=2 * H)
        SC_flat = SC[:, :, :].rearrange("p a t -> p (a t)")
        gl_wide, beta_wide = [SC_flat[:, w3 * i:w3 * (i + 1)].rearrange("p (a b) -> p a b", a=TT) for i in range(2)]
        for n, name in enumerate(["ct1", "kbg", "kd", "vb", "nwt", "qg", "eg", "xt"]):
            G[name] = at(A_CV + n * w3, TT, P)
        states = at(A_CV + 8 * w3, NB, P)
        rest = at(A_CV + 8 * w3 + NB * P, 368)
        assert 8 * w3 + NB * P + 368 <= KC * CLEN
        w_q = rest[:, 0:64].rearrange("p (b i s) -> p b i s", b=NB, i=2)
        w_q_s = rest[:, 64:128].rearrange("p (b i s) -> p b i s", b=NB, i=2)
        vnT_s = rest[:, 128:160]
        vn_s = rest[0:NS, 160:288]
        k_last = rest[0:NS, 288:289]
        k_last_p = rest[0:NS, 292:324]
        s_one, vn0, vn1 = sg[:, 0, 0:P], sg[:, 0, P:2 * P], sg[:, 1, 0:P]
        s_fin = sg[:, 1, P:2 * P]
        small = at(A_SB + KC * T, 264)

        def small3(i):
            return small[:, i:i + 24].rearrange("p (t n) -> p t n", t=TT)
        ab = small[:, 0:48].rearrange("p (t n) -> p t n", t=TT)
        beta, gl, gc, kb_s, tmp_a, tmp_b = [small3(48 + 24 * i) for i in range(6)]
        ea = small[:, 192:200]
        conf_acc = at(A_SA, KC * NS).rearrange("p (c b s) -> p c b s", c=KC, b=NB)
        conf_tmp = at(A_SA + KC * NS, KC * NS).rearrange("p (c b s) -> p c b s", c=KC, b=NB)

        def bf16_at(off, *shape):
            n = 1
            for x in shape:
                n *= x
            v = arena[:, off:off + (n + 1) // 2].bitcast(BF16)[:, 0:n]
            if len(shape) == 2:
                return v.rearrange("p (a b) -> p a b", a=shape[0])
            return v

        def high(ap):
            n = ap.shape[-1]
            return ap.bitcast(BF16)[:, 1:2 * n:2]

        mem_rows = at(0, 2, D)
        memT = at(2048, KC, ML)
        mem_k, mem_v = at(4096, 2, D), at(6144, 2, D)
        mem_kT = at(8192, KC, ML)
        xq, xo = at(10240, KC, T), at(12544, KC, T)
        probs = at(0, 2, ML)
        probsT = at(512, 2 * ML).rearrange("p (i m n) -> p i m n", i=2, m=2)
        stat = at(1024, 48)

        kT_b = at(14848, 2 * KC * ML).rearrange("p (i c m) -> p i c m", i=2, c=KC)
        pT_hi, pT_lo = bf16_at(1344, 2, P), bf16_at(1472, 2, P)
        v_lo = [bf16_at(2048 + 1024 * i, 2 * D) for i in range(2)]

        tok_hi, tok_lo = bf16_at(0, TT, D), bf16_at(1536, TT, D)
        logits, gates_, chosen, ties, run_a, run_b, place = [at(3072 + 96 * i, TT, E) for i in range(7)]
        top = at(3744, TT, 8)
        need = at(3768, 3)
        rounds_f = at(3776, 4, E)[0:1]
        ex_off = at(3904, E)
        ex_place = at(3936, TT)
        xg_hi, xg_lo = bf16_at(4096, KC, CAP), bf16_at(4352, KC, CAP)
        gate_, lin_, sig_ = at(4608, FC * CAP), at(5120, FC * CAP), at(5632, FC * CAP)
        act_ = at(6144, FC, CAP)
        y_hi, y_lo = bf16_at(6656, D)[0:CAP], bf16_at(7168, D)[0:CAP]
        cg_hi, cg_lo = bf16_at(7680, T)[0:CAP], bf16_at(7824, T)[0:CAP]
        onehot, pg = bf16_at(7968, TT, CAP), at(8064, TT, CAP)
        ex_xg_hi, ex_xg_lo = bf16_at(8256, KC, CAP), bf16_at(8512, KC, CAP)
        ex_act = at(8768, FC, CAP)
        ex_y_hi, ex_y_lo = bf16_at(9280, D)[0:CAP], bf16_at(9792, D)[0:CAP]
        ex_cg_hi, ex_cg_lo = bf16_at(10304, T)[0:CAP], bf16_at(10448, T)[0:CAP]
        ex_onehot, ex_pg = bf16_at(10592, TT, CAP), at(10688, TT, CAP)
        b2_rows = at(10880, D)[0:E]
        gates_T = at(11904, T)[0:E]
        W_LO_ARENA = 6
        w_lo = [bf16_at(12544 + 1024 * i, 2 * D) for i in range(W_LO_ARENA)] + [
            hflat[:, 1024 * i:1024 * (i + 1)].bitcast(BF16) for i in range(KC - W_LO_ARENA)]
        y_rows = at(0, TT, D)

        sg_reader = ([(proj_free[j % 4], j // 4 + 1) for j in [J_GLU + 4 * (c // 2) + c % 2 for c in range(KC)]]
                     + [(z_made, c + 1) for c in range(KC)]
                     + [(silu_made, k + 1) for k in range(KC - 1)] + [(norm_made, 2)]
                     + [(conv_made, c + 1) for c in range(QC)])

        XPE = {"gather": 1, "hidden": 2, "gates": 3, "output": 4, "scatter": 5}
        XDVE = {"onehot": 4, "xg": 9, "gate": 11, "act": 15, "cg": 16, "y": 18, "add": 19}
        XACT = {"xg": 1, "sig": 2, "cg": 3, "y": 4}
        XP, XD, XA = 4 + KC, 18 + KC, 4

        def at_least(eng, s, v):
            if not isinstance(v, int) or v > 0:
                eng.wait_ge(s, v)

        def w_slot(i):
            return (PRE + i) % RING

        def w_count(i):
            return 16 * ((PRE + i) // RING + 1)

        def flat3(ap):
            return ap.rearrange("p k n -> p (k n)")

        def load_rounds(eng, e):
            return (eng.value_load(rounds[0:1, 0, bass.ds(e, 1)], min_val=0, max_val=(T - 1) // CAP),
                    eng.value_load(rounds[0:1, 1, bass.ds(e, 1)], min_val=0, max_val=E * (T - 1) // CAP))

        def bank_rows(eng, n, rows):
            eng.wait_ge(tr_done, n + 1)
            return bank[4 + n % 2][0:rows, :]

        PE_STEPS = (["turned", "ya1", "yb1", "za1", "zb1", "ya2", "yb2", "w_s", "za2", "zb2", "ya3", "yb3", "za3", "zb3",
                     "ya4", "yb4", "sample", "za4", "zb4", "ya5", "yb5", "vnt", "za5", "zb5", "ya6", "yb6", "wide_out",
                     "za6", "zb6", "w", "vn0", "s1", "vn1", "out"])
        DVE_STEPS = (["pt", "columns", "xa1", "xta1", "xb1", "xtb1", "xa2", "xta2", "xb2", "xtb2",
                      "wq", "xa3", "xta3", "xb3", "xtb3", "xa4", "xta4", "xb4", "xtb4", "vnT", "xa5", "xta5", "xb5",
                      "xtb5", "vn_s", "wide", "xta6", "xtb6", "vn0", "vn1", "head", "states"])
        ACT_STEPS = (["eg", "x0", "ya1", "yb1", "ya2", "yb2", "nwt_s", "ya3", "yb3", "ya4", "yb4", "ws",
                      "ya5", "yb5", "ya6", "yb6", "nwt", "s1"])
        Y_BANK, X_BANK, Z_BANK = {"a": 7, "b": 0}, {"a": 6, "b": 1}, {"a": 2, "b": 3}

        def chain_tiles(ab_, l):
            return range(0, 1) if ab_ == "a" else range(1, TT if l == 1 else 2)

        def step(eng, s, steps, h, name):
            eng.wait_ge(s, len(steps) * h + steps.index(name) + 1)

        tile_cols = [slice(0, P), slice(P, 2 * P), slice(2 * P, T)]

        def piece_read(n):
            if n >= NP_XO:
                return proj_done, J_XO + 2 * (n - NP_XO) + 2
            if n >= NP_CACHE + NB:
                return v_used, n - NP_CACHE - NB + 1
            if n >= NP_CACHE:
                return tr_done, 38 + 4 * (n - NP_CACHE + 1)
            if n >= NP_XQ:
                return proj_done, J_XQ + 2 * (n - NP_XQ) + 2
            if n >= NP_KV:
                return proj_done, J_KV + (n - NP_KV) + 1
            return proj_done, 2 * n + 2

        block = ctx.enter_context(nc.Block())

        @block.sync
        def _(sp):
            for n, src in enumerate(pieces):
                if n >= RING:
                    sp.wait_ge(*piece_read(n - RING))
                if n == 2:
                    sp.wait_ge(ld_par, 16 * 15)
                    sp.wait_ge(ld_conf, 16 * 2)
                    sp.wait_ge(ld_gdn, 16)
                if n == N_HELD:
                    step(sp, g_pe, PE_STEPS, H - 1, "wide_out")
                dst = ring[:, n % RING, :]
                sp.dma_start(dst.rearrange("p (k n) -> p k n", k=src.shape[1]), src).then_inc(w_here[n % RING], 16)
            w1 = d["moe_w1"][0].rearrange("e (k p) n -> p e k n", p=P)
            w2 = d["moe_w2"][0].rearrange("e (k p) n -> p e k n", p=P)

            def expert_in(e, ready):
                for i in range(EPI):
                    ready(i)
                    dst = ring[:, (PRE + i) % RING, :]
                    if i < KC:
                        sp.dma_start(dst, w1[:, e, i, :]).then_inc(w_here[(PRE + i) % RING], 16)
                    else:
                        f = 2 * (i - KC)
                        sp.dma_start(dst.rearrange("p (k n) -> p k n", k=2),
                                     w2[:, e, f:f + 2, :]).then_inc(w_here[(PRE + i) % RING], 16)

            expert_in(0, lambda i: sp.wait_ge(*piece_read(PRE + i - RING)))
            with sp.Fori(1, E) as e:
                expert_in(e, lambda i: sp.wait_ge(w_free, e * EPI - EPI + (i + 1)))

        @block.gpsimd
        def _(pool):
            own = chain(pool, pool_self)
            own(pool.memset(ident[:, :], 0.0))
            own(pool.affine_select(out=ident[:, :], in_=ident[:, :], compare_op=ALU.not_equal, fill=1.0,
                                   base=0, pattern=[[-1, P]], channel_multiplier=1))
            own(pool.memset(ones[:, :], 1.0), masks_made)
            own(pool.memset(level_mask[:, :, :], 0.0))
            for l in range(LEVELS):
                s = 1 << l
                m = level_mask[:, l, :].rearrange("p (b h i) -> p b h i", h=2, i=s)[:, :, 1, :]
                own(pool.memset(m, 1.0))
                own(pool.affine_select(out=m, in_=m, compare_op=ALU.is_ge, fill=0.0, base=0,
                                       pattern=[[-2 * s, P // (2 * s)], [0, s]], channel_multiplier=1))
                own(pool.affine_select(out=m, in_=m, compare_op=ALU.is_ge, fill=0.0, base=s - 1,
                                       pattern=[[2 * s, P // (2 * s)], [0, s]], channel_multiplier=-1))
            own(pool.memset(causal[:, :, :], 0.0))
            own(pool.memset(causal[:, 0, :], 1.0))
            own(pool.affine_select(out=causal[:, 0, :], in_=causal[:, 0, :], compare_op=ALU.is_ge, fill=0.0,
                                   base=0, pattern=[[1, P]], channel_multiplier=-1))
            own(pool.tensor_tensor(causal[0:NS, 1, 0:NS], level_mask[0:NS, 0, 0:NS], level_mask[0:NS, 1, 0:NS], ALU.add))
            own(pool.tensor_tensor(causal[0:NS, 1, 0:NS], causal[0:NS, 1, 0:NS], ident[0:NS, 0:NS], ALU.add))
            own(pool.memset(batch_of[:, :], 1.0))
            own(pool.affine_select(out=batch_of[:, :], in_=batch_of[:, :], compare_op=ALU.is_ge, fill=0.0,
                                   base=0, pattern=[[-DT, NB]], channel_multiplier=1))
            own(pool.affine_select(out=batch_of[:, :], in_=batch_of[:, :], compare_op=ALU.is_ge, fill=0.0,
                                   base=DT - 1, pattern=[[DT, NB]], channel_multiplier=-1))
            own(pool.memset(last_of[:, :], 0.0))
            own(pool.tensor_copy(last_of[:, DT - 1:NS:DT], batch_of[:, :]))
            own(pool.iota(slot_int[:, :], pattern=[[1, CAP]], base=0, channel_multiplier=0))
            own(pool.tensor_copy(slot_id[:, :], slot_int[:, :]))
            own(pool.memset(pick[:, :], 0.0))
            own(pool.memset(pick[:, 2 * H - 1:2 * H], 1.0))
            own(pool.memset(small[:, :], 0.0), masks_made)
            own(pool.memset(cvx[:, :, 0:CM], 0.0), pads_made)
            pool.wait_ge(tr_free[0], 3)
            pool.wait_ge(tr_free[1], 3)
            own(pool.memset(qkv[:, :, 0:GM], 0.0), pads_made)

            pool.wait_ge(conf_tail_made, KC)
            for j in range(CW):
                wj = []
                for lo, hi in ((0, KC),):
                    c0 = CWO + KC * j + (0 if KC * j < 124 else 4)
                    if KC * j < 124 < KC * j + KC:
                        half = 124 - KC * j
                        wj = [(0, half, CWO + KC * j), (half, KC, CWO + KC * j + half + 4)]
                    else:
                        wj = [(0, KC, c0)]
                for lo, hi, c0 in wj:
                    w = prm[:, c0:c0 + hi - lo].unsqueeze(2).unsqueeze(3).to_broadcast((P, hi - lo, NB, DT))
                    x = conf_hist[:, lo:hi, :, j:j + DT]
                    out = conf_acc if j == 0 else conf_tmp
                    last = own(pool.tensor_tensor(out[:, lo:hi], x, w, ALU.mult))
                if j:
                    a = conf_acc.rearrange("p c b s -> p (c b s)")
                    t = conf_tmp.rearrange("p c b s -> p (c b s)")
                    own(pool.tensor_tensor(a, a, t, ALU.add), conf_s_made if j == CW - 1 else pool_self)

            for c in range(KC):
                pool.wait_ge(sig_made, KC + c + 1)
                job_left(pool, J_Z + c)
                own(pool.tensor_tensor(zs[:, c, :], zs[:, c, :], sg[:, c % 2, :], ALU.mult), z_made)

            def load_states(h):
                pool.dma_start(states, d["state_gdn"][0, :, h].rearrange("b k v -> k b v")).then_inc(ld_state, 16)

            def spread(h):
                own(pool.tensor_copy(gl_wide, gl[:, :, h:h + 1].to_broadcast((P, TT, P))))
                own(pool.tensor_copy(beta_wide, beta[:, :, h:h + 1].to_broadcast((P, TT, P))), spread_made)

            def states_out(h):
                step(pool, g_dve, DVE_STEPS, h, "head")
                pool.dma_start(d["out_state_p"][0, 0, h], s_fin).then_inc(st_prompt, 16)
                step(pool, g_dve, DVE_STEPS, h, "states")
                pool.dma_start(d["out_state_s"][0, :, h].rearrange("b k v -> k b v"), states).then_inc(st_out, 16)

            pool.wait_ge(ab_act, 1)
            pool.wait_ge(gl_made, 1)
            pool.wait_ge(l2_read, 2 * H)
            spread(0)
            load_states(0)
            for h in range(H):
                pool.wait_ge(xt_start, h + 1)
                for l in range(1, LEVELS):
                    if l == 3 and h:
                        states_out(h - 1)
                    if l >= 3:
                        step(pool, g_pe, PE_STEPS, h, f"yb{l - 2}")
                    n = TT if l == 1 else 2
                    ct = G["ct0"] if l % 2 else G["ct1"]
                    m = level_mask[:, l:l + 1, :].to_broadcast((P, n, P))
                    own(pool.tensor_tensor(ct[:, 0:n, :], G["mt"][:, 0:n, :], m, ALU.mult), g_pool)
                    if l == 3 and h:
                        pool.wait_ge(st_out, 16 * h)
                        load_states(h)
                step(pool, g_pe, PE_STEPS, h, "sample")
                own(pool.tensor_tensor(states, states, G["eg"][:, 2, DT - 1:NS:DT].unsqueeze(2).to_broadcast((P, NB, P)),
                                       ALU.mult), decayed_states)
                if h + 1 < H:
                    spread(h + 1)
            states_out(H - 1)
            pool.wait_ge(proj_done, J_XO + 8)
            for k in range(KC):
                if k == W_LO_ARENA:
                    pool.wait_ge(logits_done, 1)
                pool.wait_ge(w_here[w_slot(k)], w_count(k))
                w = ring[:, w_slot(k), :]
                pool.tensor_tensor(w_lo[k], w, high(w), ALU.subtract).then_inc(lo_made, 1)

        @block.tensor
        def _(pe):
            mm, tp = nc.tensor.matmul, nc.tensor.transpose
            tr = [0]

            def turn(srcs, rows=None, step_=None):
                n = tr[0]
                tr[0] += 1
                if n >= 2:
                    pe.wait_ge(tr_free[n % 2], n // 2)
                c = 0
                for src, r in srcs:
                    m_ = src.shape[1]
                    last = tp(bank[4 + n % 2][0:m_, c:c + r], src, ident[0:r, 0:r])
                    c += r
                last.then_inc(tr_done, 1)

            sq = [0]

            def sum_squares(b, n=KC, cols_=T, lag=0):
                for k in range(n):
                    pe.wait_ge(sq_made, sq[0] + 1)
                    mm(bank[b][:, 0:cols_], ones[:, :], SC[:, sq[0] % 2, 0:cols_],
                       start=(k == 0), stop=(k == n - 1)).then_inc(sq_used, 1)
                    sq[0] += 1

            def piece(n):
                pe.wait_ge(w_here[n % RING], 16 * (n // RING + 1))

            def project(job, n0, pieces_, rhs):
                for p_ in range(pieces_):
                    piece(n0 + p_)
                    w = dense(n0 + p_)
                    for half in range(2):
                        j = job + 2 * p_ + half
                        if j >= 4:
                            job_left(pe, j - 4)
                        for k in range(KC):
                            last = mm(proj_bank(j), w[:, k, P * half:P * (half + 1)], rhs(k),
                                      start=(k == 0), stop=(k == KC - 1))
                        last.then_inc(proj_done, 1)
            pe.wait_ge(masks_made, 1)
            seen_load = set()
            for kind, srcs, dst, shape in in_jobs:
                if kind not in seen_load:
                    pe.wait_ge(*loads[kind])
                    seen_load.add(kind)
                turn(srcs)
            sum_squares(6)
            pe.wait_ge(norm_made, 1)
            x = lambda k: hT[:, k, :]
            project(J_GLU, NP_GLU, 8, x)
            project(J_QKV, NP_QKV, 2, x)
            pe.wait_ge(conf_tail_made, KC)
            for half in range(2):
                turn([(conf_tail[:, 4 * half + i, :], P) for i in range(4)])
            project(J_QKV + 4, NP_QKV + 2, 10, x)
            project(J_Z, NP_Z, 2, x)
            pe.wait_ge(conf_made, KC)
            for k in range(KC):
                last = mm(bank[6][:, 0:T], ones[:, :], cvx[:, k, 0:T], start=(k == 0), stop=(k == KC - 1))
            last.then_inc(mean_done, 1)
            project(J_Z + 4, NP_Z + 2, 2, x)
            pe.wait_ge(mean_read, 1)
            sum_squares(6)
            for g_ in range(N_GDN_JOBS):
                for j in range(J_QKV + 4 * g_, J_QKV + 4 * g_ + 4):
                    job_left(pe, j)
                turn([(gdn_tail[:, 4 * g_ + i, :], P) for i in range(4)])
            project(J_GATE, NP_GATE, 8, x)
            pe.wait_ge(ld_small, 16 * 5)
            pe.wait_ge(tr_free[0], 15)
            pe.wait_ge(tr_free[1], 15)
            for t in range(TT):
                for k in range(KC):
                    last = mm(bank[4][0:TROWS[t], 16 * t:16 * t + 16], hT[:, k, tile_cols[t]], w_ab[:, k, :],
                              start=(k == 0), stop=(k == KC - 1))
            last.then_inc(ab_done, 1)
            pe.wait_ge(norm_made, 2)
            project(J_PW2, NP_PW2, 4, lambda k: cvx[:, k, 0:T])

            def l2_sums(count):
                for n in range(count):
                    pe.wait_ge(sq_made, sq[0] + 1)
                    mm(bank[6][0:count, 0:T], pick[:, 2 * H - 1 - n:2 * H - 1 - n + count], SC[:, sq[0] % 2, :],
                       start=(n == 0), stop=(n == count - 1)).then_inc(sq_used, 1)
                    sq[0] += 1

            def l2_spread(n0, count):
                pe.wait_ge(l2_inv, 1 if n0 == 0 else 2)
                for n in range(count):
                    if n >= 2:
                        pe.wait_ge(l2_read, n0 + n - 1)
                    mm(bank[4 + n % 2][:, 0:T], row_sel[0:count, n, :], SC[0:count, 2, :],
                       start=True, stop=True).then_inc(l2_done, 1)

            pe.wait_ge(ab_dve, 1)
            pe.wait_ge(conv_made, QC)
            pe.wait_ge(masks_made, 2)
            l2_sums(2 * H)
            l2_spread(0, 2 * H)
            pe.wait_ge(gl_made, 1)
            pe.wait_ge(banks_clear, 1)
            for t in range(TT):
                last = mm(bank[7][:, 8 * t:8 * t + 8], causal[:, t // 2, :], gl[:, t, :], start=True, stop=True)
            last.then_inc(gc_done, 1)

            def tiles(b, lhsT, rhs, n=TT, small=True):
                for t in range(n):
                    r = P if t < 2 or not small else NS
                    last = mm(bank[b][0:r, P * t:P * t + r], lhsT(t), rhs(t), start=True, stop=True)
                return last

            r_ = lambda t: P if t < 2 else NS

            def head_rows(h):
                pe.wait_ge(spread_made, h + 1)
                tiles(0, lambda t: gl_wide[:, t, :], lambda t: causal[:, t // 2, :], small=False)
                tiles(1, lambda t: beta_wide[:, t, :], lambda t: ident[:, :], small=False).then_inc(rows_done, 1)

            def head_scores(h):
                q_ = lambda t: qkv[:, h, tile_cols[t]]
                k_ = lambda t: qkv[:, H + h, tile_cols[t]]
                tiles(2, k_, k_)
                tiles(3, k_, q_).then_inc(scores_rows, 1)

            def head_columns(h):
                for t in range(TT):
                    tp(bank[4][0:r_(t), P * t:P * (t + 1)], qkv[:, H + h, tile_cols[t]], ident[:, :])
                    last = tp(bank[5][0:r_(t), P * t:P * (t + 1)], qkv[:, 2 * H + h, tile_cols[t]], ident[:, :])
                last.then_inc(kv_turned, 1)

            head_rows(0)
            head_scores(0)
            for h in range(H):
                D_ = lambda name: step(pe, g_dve, DVE_STEPS, h, name)
                A_ = lambda name: step(pe, g_act, ACT_STEPS, h, name)
                if h:
                    step(pe, g_dve, DVE_STEPS, h - 1, "head")
                pe.wait_ge(xt_start, h + 1)
                for t in range(TT):
                    last = tp(bank[6][:, P * t:P * (t + 1)], G["xt"][:, t, :], ident[:, :])
                last.then_inc(g_pe, 1)
                if h:
                    step(pe, g_dve, DVE_STEPS, h - 1, "states")
                head_columns(h)
                for l in range(1, LEVELS):
                    ct = G["ct0"] if l % 2 else G["ct1"]
                    pe.wait_ge(g_pool, (LEVELS - 1) * h + l)
                    if l == 1:
                        A_("x0")
                    for c in "ab":
                        if l > 1:
                            D_(f"x{c}{l - 1}")
                        for t in chain_tiles(c, l):
                            last = mm(bank[Y_BANK[c]][:, P * t:P * (t + 1)], ct[:, t, :], G["x"][:, t, :], start=True, stop=True)
                        last.then_inc(g_pe, 1)
                    if l == 2:
                        D_("columns")
                        D_("xtb1")
                        mm(bank[5][:, 3 * P:3 * P + NS], G["kbg"][0:NS, 2, :], G["xt"][0:NS, 2, 0:NS], start=True, stop=True)
                        mm(bank[5][:, 0:NS], G["vb"][0:NS, 2, :], G["xt"][0:NS, 2, 0:NS],
                           start=True, stop=True).then_inc(g_pe, 1)
                    if l == 3:
                        D_("wq")
                        pe.wait_ge(ld_state, 16 * (h + 1))
                    if l in (3, 4):
                        for b in range(4 * (l - 3), 4 * (l - 2)):
                            last = mm(bank[4][:, 8 * b:8 * b + 8], states[:, b, :],
                                      w_q[:, b, :, :].rearrange("p i s -> p (i s)"), start=True, stop=True)
                        if l == 4:
                            last.then_inc(g_pe, 1)
                    if l == 5:
                        D_("vnT")
                        tp(bank[5][0:NS, P:2 * P], vnT_s, ident[:, :]).then_inc(g_pe, 1)
                    if l == 6:
                        D_("wide")
                        for i in range(2):
                            last = mm(bank[4 + i][:, :], G["kd"][0:NS, 2, :],
                                      v_wide[:, 4 * i:4 * i + 4, :].rearrange("p b n -> p (b n)"), start=True, stop=True)
                        last.then_inc(g_pe, 1)
                    for c in "ab":
                        A_(f"y{c}{l}")
                        if l == 1:
                            D_("pt")
                        if l > 1:
                            D_(f"xt{c}{l - 1}")
                        if l < LEVELS - 1:
                            for t in chain_tiles(c, l):
                                mm(bank[X_BANK[c]][:, P * t:P * (t + 1)], G["xt"][:, t, :], G["y"][:, t, :], start=True, stop=True)
                        for t in chain_tiles(c, l):
                            last = mm(bank[Z_BANK[c]][:, P * t:P * (t + 1)], G["y"][:, t, :], G["xt"][:, t, :],
                                      start=True, stop=True)
                        last.then_inc(g_pe, 1)
                D_(f"xtb{LEVELS - 1}")
                mm(bank[6][:, 3 * P:4 * P], G["kbg"][:, 1, :], G["xt"][:, 1, :], start=True, stop=True).then_inc(g_pe, 1)
                mm(bank[7][:, 0:P], G["xt"][:, 0, :], G["vb"][:, 0, :], start=True, stop=True).then_inc(g_pe, 1)
                if h + 1 < H:
                    head_rows(h + 1)
                D_("vn0")
                mm(bank[7][:, P:2 * P], G["kd"][:, 0, :], vn0, start=True, stop=True).then_inc(g_pe, 1)
                if h + 1 < H:
                    head_scores(h + 1)
                A_("nwt")
                A_("s1")
                mm(bank[7][:, 2 * P:3 * P], G["xt"][:, 1, :], G["vb"][:, 1, :], start=True, stop=False)
                mm(bank[7][:, 2 * P:3 * P], G["nwt"][:, 1, :], s_one, start=False, stop=True).then_inc(g_pe, 1)
                D_("vn1")
                mm(bank[6][:, 0:P], vn0, G["pt"][:, 0, :], start=True, stop=True)
                mm(bank[6][:, P:2 * P], s_one, G["qg"][:, 1, :], start=True, stop=False)
                mm(bank[6][:, P:2 * P], vn1, G["pt"][:, 1, :], start=False, stop=True)
                mm(bank[6][:, 2 * P:2 * P + NS], vn_s, G["pt"][0:NS, 2, 0:NS], start=True, stop=True)
                mm(bank[7][:, 3 * P:4 * P], G["kd"][:, 1, :], vn1, start=True, stop=True).then_inc(g_pe, 1)
            step(pe, g_dve, DVE_STEPS, H - 1, "states")
            l2_sums(H)
            l2_spread(2 * H, H)
            pe.wait_ge(o_made, H)
            project(J_O, NP_O, 4, lambda k: qkv[:, 2 * H + k, 0:T])
            job_left(pe, J_OUT - 4), job_left(pe, J_OUT - 3), job_left(pe, J_OUT - 2), job_left(pe, J_OUT - 1)
            project(J_OUT, NP_OUT, 4, lambda k: gate_a[:, k, :])
            pe.wait_ge(ld_mem, 16)
            for t in range(2):
                for half in range(2):
                    turn([(mem_rows[:, t, P * (4 * half + i):P * (4 * half + i + 1)], P) for i in range(4)])
            sum_squares(7, KC, ML)
            pe.wait_ge(norm_made, 3)
            sum_squares(6)
            for p_ in range(8):
                j = J_KV + p_
                piece(NP_KV + p_)
                job_left(pe, j - 4)
                for t in range(2):
                    for k in range(KC):
                        last = mm(bank[j % 4][:, PCOL * t:PCOL * (t + 1)], memT[:, k, P * t:P * (t + 1)],
                                  dense(NP_KV + p_)[:, k, :], start=(k == 0), stop=(k == KC - 1))
                last.then_inc(proj_done, 1)
            for p_ in range(4):
                job_left(pe, J_KV + p_)
            for t in range(2):
                for half in range(2):
                    turn([(mem_k[:, t, P * (4 * half + i):P * (4 * half + i + 1)], P) for i in range(4)])
            pe.wait_ge(norm_made, 4)
            project(J_XQ, NP_XQ, 4, lambda k: hT[:, k, :])
            for j in range(J_XQ, J_XQ + 8):
                job_left(pe, j)
            for p_ in range(4, 8):
                job_left(pe, J_KV + p_)
            pe.wait_ge(tr_free[0], 19)
            pe.wait_ge(tr_free[1], 19)

            def scores(u):
                h, t = u // 2, u % 2
                if u >= 2:
                    pe.wait_ge(xo_made, u - 1)
                for c in range(XC):
                    last = mm(bank[u % 2][:, 0:ML], xq[:, XC * h + c, P * t:P * (t + 1)],
                              mem_kT[:, XC * h + c, :], start=(c == 0), stop=(c == XC - 1))
                last.then_inc(scores_done, 1)

            def attend(u):
                h, t = u // 2, u % 2
                pe.wait_ge(probs_made, u + 1)
                if u >= 2:
                    pe.wait_ge(pt_made, u - 1)
                for m in range(2):
                    last = tp(bank[2 + u % 2][:, P * m:P * (m + 1)], probs[:, u % 2, P * m:P * (m + 1)], ident[:, :])
                last.then_inc(pt_done, 1)
                pe.wait_ge(pt_made, u + 1)
                for c in range(XC):
                    for m in range(2):
                        last = mm(bank[u % 2][:, ML + P * c:ML + P * (c + 1)],
                                  mem_v[:, m, P * (XC * h + c):P * (XC * h + c + 1)], probsT[:, u % 2, m, :],
                                  start=(m == 0), stop=(m == 1))
                last.then_inc(xo_done, 1)

            def turn_keys(b):
                piece(NP_CACHE + b)
                for t in range(2):
                    for half in range(2):
                        turn([(wide(NP_CACHE + b)[:, t, P * (4 * half + i):P * (4 * half + i + 1)], P) for i in range(4)])

            def sample_scores(b):
                pe.wait_ge(tr_free[0], 19 + 2 * (b + 1))
                pe.wait_ge(tr_free[1], 19 + 2 * (b + 1))
                for m in range(2):
                    for h in range(XH):
                        for c in range(XC):
                            col = P * m + 16 * b + DT * h
                            last = mm(bank[6][:, col:col + DT], kT_b[:, b % 2, XC * h + c, P * m:P * (m + 1)],
                                      xq[:, XC * h + c, SEQ + DT * b:SEQ + DT * (b + 1)],
                                      start=(c == 0), stop=(c == XC - 1))
                last.then_inc(s_scores, 1)

            NU = 2 * XH
            assert NU == NB
            for u in range(NU + 1):
                if u < NU:
                    scores(u)
                    turn_keys(u)
                if u:
                    sample_scores(u - 1)
                    attend(u - 1)
            pe.wait_ge(sT_made, 1)
            for m in range(2):
                last = tp(bank[7][:, P * m:P * (m + 1)], probs[:, 0, P * m:P * (m + 1)], ident[:, :])
            last.then_inc(scores_done, 1)
            pe.wait_ge(probs_made, NU + 1)
            for m in range(2):
                last = tp(bank[6][:, P * m:P * (m + 1)], probs[:, 1, P * m:P * (m + 1)], ident[:, :])
            last.then_inc(pt_done, 1)
            pe.wait_ge(pt_made, NU + 1)
            for b in range(NB):
                n = NP_CACHE + NB + b
                piece(n)
                pe.wait_ge(v_lo_made, b + 1)
                for c in range(KC):
                    for m in range(2):
                        out = bank[5][:, NS * c + DT * b:NS * c + DT * (b + 1)]
                        v_ = slice(D * m + P * c, D * m + P * (c + 1))
                        v_hi = high(ring[:, n % RING, v_])
                        p_hi, p_lo = [p_[:, m, 16 * b + DT * (c // XC):16 * b + DT * (c // XC + 1)] for p_ in (pT_hi, pT_lo)]
                        mm(out, v_hi, p_hi, start=(m == 0), stop=False)
                        mm(out, v_hi, p_lo, start=False, stop=False)
                        mm(out, v_lo[b % 2][:, v_], p_hi, start=False, stop=False)
                        last = mm(out, v_lo[b % 2][:, v_], p_lo, start=False, stop=(m == 1))
                last.then_inc(v_used, 1)
            pe.wait_ge(xo_made, NU + 1)
            project(J_XO, NP_XO, 4, lambda k: xo[:, k, :])
            sum_squares(6)
            pe.wait_ge(norm_made, 5)
            for t in range(TT):
                for hf in range(2):
                    turn([(hT[:, 4 * hf + i, tile_cols[t]], P) for i in range(4)])
            for t in range(TT):
                for k in range(KC):
                    last = mm(bank[6][0:TROWS[t], E * t:E * (t + 1)], hT[:, k, tile_cols[t]], w_router[:, k, :],
                              start=(k == 0), stop=(k == KC - 1))
            last.then_inc(logits_done, 1)
            pe.wait_ge(chosen_made, 1)
            for t in range(TT):
                r = TROWS[t]
                for i in range(t):
                    mm(bank[7][0:r, E * t:E * (t + 1)], ones[:, 0:r], chosen[:, i, :], start=(i == 0), stop=False)
                mm(bank[7][0:r, E * t:E * (t + 1)], causal[0:r, 0, 0:r], chosen[0:r, t, :], start=(t == 0), stop=True)
            for t in range(TT):
                last = mm(bank[7][0:1, E * TT:E * (TT + 1)], ones[0:TROWS[t], 0:1], chosen[0:TROWS[t], t, :],
                          start=(t == 0), stop=(t == TT - 1))
            last.then_inc(counts_done, 1)
            pe.wait_ge(gates_made, 1)
            for t in range(TT):
                last = tp(bank[0][0:E, P * t:P * t + TROWS[t]], gates_[0:TROWS[t], t, :], ident[0:TROWS[t], 0:TROWS[t]])
            last.then_inc(gates_T_done, 1)
            pe.wait_ge(tr_free[0], 38)
            pe.wait_ge(tr_free[1], 38)

            def w_wait(e, i):
                pe.wait_ge(w_here[w_slot(i)], e * 16 + w_count(i))

            pe.wait_ge(gates_T_made, 1)
            pe.wait_ge(ld_b2, 16)
            for c in range(KC):
                if c >= 2:
                    pe.wait_ge(b2_added, c - 1)
                mm(bank[4 + c % 2][:, 0:T], b2_rows[:, P * c:P * (c + 1)], gates_T, start=True, stop=True).then_inc(b2_done, 1)

            def gather(hot, signal):
                for b, part in ((0, tok_hi), (3, tok_lo)):
                    for k in range(KC):
                        for t in range(TT):
                            r = TROWS[t]
                            last = mm(bank[b][:, CAP * k:CAP * (k + 1)], part[0:r, t, P * k:P * (k + 1)], hot[0:r, t, :],
                                      start=(k == 0 and t == 0), stop=(k == KC - 1 and t == TT - 1),
                                      skip_group_check=True)
                last.then_inc(signal, 1)

            def hidden(hi, lo, e, signal):
                for k in range(KC):
                    w_wait(e, k)
                    pe.wait_ge(lo_made, e * KC + (k + 1))
                    for f in range(2 * FC):
                        out = bank[1 + f // FC][:, CAP * (f % FC):CAP * (f % FC + 1)]
                        w_hi = high(ring[:, w_slot(k), P * f:P * (f + 1)])
                        mm(out, w_hi, hi[:, k, :], start=(k == 0 and f % FC == 0), stop=False, skip_group_check=True)
                        mm(out, w_hi, lo[:, k, :], start=False, stop=False, skip_group_check=True)
                        last = mm(out, w_lo[k][:, P * f:P * (f + 1)], hi[:, k, :], start=False,
                                  stop=(k == KC - 1 and f % FC == FC - 1), skip_group_check=True)
                    if signal is w_free or k == KC - 1:
                        last.then_inc(signal, 1)

            def output(a, e, signal, to):
                for i in range(4):
                    w_wait(e, KC + i)
                    for f in range(2 * i, 2 * i + 2):
                        for n in range(2):
                            o = 1024 * (f % 2) + 512 * n
                            last = mm(bank[to[n]][0:CAP, :], a[:, f, :], ring[:, w_slot(KC + i), o:o + 512],
                                      start=(f == 0), stop=(f == FC - 1))
                    if signal is w_free or i == 3:
                        last.then_inc(signal, 1)

            def turn_gates(pg_, signal):
                for t in range(TT):
                    r = TROWS[t]
                    last = (tp if t else mm)(bank[5][0:CAP, P * t:P * t + r], pg_[0:r, t, :], ident[0:r, 0:r])
                last.then_inc(signal, 1)

            def scatter(c, y, g_, signal):
                out = bank[4 + c % 2][:, 0:T]
                f_ = slice(P * c, P * (c + 1))
                mm(out, y[0][:, f_], g_[0], start=True, stop=False)
                mm(out, y[0][:, f_], g_[1], start=False, stop=False)
                mm(out, y[1][:, f_], g_[0], start=False, stop=True).then_inc(signal, 1)

            def extra(e, first):
                n, r0 = load_rounds(pe, e)
                with pe.If(n > 0):
                    with pe.Fori(0, n) as j:
                        r = pe.snap(r0 + j)
                        pe.wait_ge(xg_evac, e + 1)
                        pe.wait_ge(xlo_evac, e + 1)
                        if not first:
                            at_least(pe, scat_add, e * 8 - 8)
                        pe.wait_ge(ex_dve, r * XD + XDVE["onehot"])
                        gather(ex_onehot, ex_pe)
                        pe.wait_ge(ex_dve, r * XD + XDVE["xg"])
                        pe.wait_ge(ex_actv, r * XA + XACT["xg"])
                        hidden(ex_xg_hi, ex_xg_lo, e, ex_pe)
                        turn_gates(ex_pg, ex_pe)
                        pe.wait_ge(ex_dve, r * XD + XDVE["act"])
                        output(ex_act, e, ex_pe, (0, 3))
                        pe.wait_ge(ex_dve, r * XD + XDVE["y"])
                        for c in range(KC):
                            if c >= 2:
                                pe.wait_ge(ex_dve, r * XD + XDVE["add"] + c - 2)
                            scatter(c, (ex_y_hi, ex_y_lo), (ex_cg_hi, ex_cg_lo), ex_pe)
                        pe.wait_ge(ex_dve, r * XD + XD)

            def scatter_last(e):
                pe.wait_ge(cgl_made, e)
                pe.wait_ge(ylo_made, e)
                for c in range(KC):
                    if c >= 2:
                        pe.wait_ge(scat_add, e * 8 - 8 + (c - 1))
                    scatter(c, (y_hi, y_lo), (cg_hi, cg_lo), scat_done)

            def gates_last(e):
                pe.wait_ge(pg_made, e)
                at_least(pe, scat_add, e * 8 - 8)
                turn_gates(pg, cg_done)

            def expert(e, first, last_one):
                pe.wait_ge(xg_evac, e + 1)
                pe.wait_ge(xlo_evac, e + 1)
                hidden(xg_hi, xg_lo, e, w_free)
                if not first:
                    gates_last(e)
                if not last_one:
                    pe.wait_ge(p_made, e + 2)
                    gather(onehot, xg_done)
                if not first:
                    scatter_last(e)
                pe.wait_ge(act_made, e + 1)
                output(act_, e, w_free, (6, 7))

            pe.wait_ge(rounds_made, 1)
            pe.wait_ge(b2_added, KC)
            pe.wait_ge(p_made, 1)
            gather(onehot, xg_done)
            for e in (0, 1):
                extra(e, e == 0)
                expert(e, e == 0, False)
            with pe.Fori(2, E - 1) as e:
                extra(e, False)
                expert(e, False, False)
            extra(E - 1, False)
            expert(E - 1, False, True)
            gates_last(E)
            scatter_last(E)
            sum_squares(6)
            pe.wait_ge(norm_made, 6)
            for t in range(TT):
                for half in range(2):
                    turn([(hT[:, 4 * half + i, tile_cols[t]], P) for i in range(4)])

        @block.scalar
        def _(act):
            own = chain(act, act_self)
            A = nc.scalar.activation
            sq, root = [0], [0]

            def squares(src, n=KC, cols_=T):
                for k in range(n):
                    if sq[0] >= 2:
                        act.wait_ge(sq_used, sq[0] - 1)
                    A(SC[:, sq[0] % 2, 0:cols_], src(k), ACT.Square).then_inc(sq_made, 1)
                    sq[0] += 1

            def take_root(cols_=T):
                root[0] += 1
                act.wait_ge(root_in, root[0])
                A(SC[:, 2, 0:cols_], SC[:, 2, 0:cols_], ACT.Sqrt).then_inc(root_made, 1)

            def sigmoid(n, src, **kw):
                if n >= 2:
                    act.wait_ge(*sg_reader[n - 2])
                A(sg[:, n % 2, :], src, ACT.Sigmoid, **kw).then_inc(sig_made, 1)

            def read_bank(n, dst, shape, rows=P, w=512):
                act.wait_ge(tr_done, n + 1)
                A(dst, view(4 + n % 2, rows, w, shape), ACT.Copy).then_inc(tr_free[n % 2], 1)

            act.dma_start(st_x[:, 0:2, :], d["x_prompt"][0].rearrange("(t p) n -> p t n", p=P)).then_inc(ld_x, 16)
            act.dma_start(st_x[0:NS, 2, :], d["x_sample"].rearrange("b s n -> (b s) n")).then_inc(ld_x, 16)
            for name, c in VEC.items():
                v = d[name] if name == "norm_final" else d[name][0]
                r = 1 if name == "gdn_norm" else KC
                act.dma_start(st_par[c:c + r, 0, :], v.rearrange("(r n) -> r n", n=P)).then_inc(ld_par, 16)
            act.dma_start(st_par[0:96, 1, :], d["gdn_conv_w"][0].rearrange("j (c n) -> (j c) n", n=P)).then_inc(ld_par, 16)
            cw = d["conf_conv_w"][0].rearrange("j (c n) -> (j c) n", n=P)
            for i in range(2):
                act.dma_start(st_par[0:124, 2 + i, :], cw[124 * i:124 * i + 124, :]).then_inc(ld_par, 16)
            b1 = d["moe_b1"][0].rearrange("e (c n) -> (e c) n", n=P)
            act.dma_start(st_par[:, 4:8, :], b1.rearrange("(t p) n -> p t n", p=P)).then_inc(ld_par, 16)
            b2 = d["moe_b2"][0].rearrange("e (c n) -> (e c) n", n=P)
            act.dma_start(st_par[:, 8:10, :], b2.rearrange("(t p) n -> p t n", p=P)).then_inc(ld_par, 16)
            hist = d["state_conf_conv"][0].rearrange("b s n -> (b s) n")
            for u in range(2):
                act.dma_start(st_conf[0:120, u, :], hist[120 * u:120 * u + 120, :]).then_inc(ld_conf, 16)
            act.dma_start(st_gdn[0:NB * GM, :], d["state_gdn_conv"][0].rearrange("b s n -> (b s) n")).then_inc(ld_gdn, 16)
            win = d["w_in"][0].rearrange("(k p) n -> p k n", p=P)
            act.dma_start(w_ab[:, :, :], win[:, :, C_A:C_A + 2 * H]).then_inc(ld_small, 16)
            act.dma_start(w_router[:, :, :], d["router_w"][0].rearrange("(k p) n -> p k n", p=P)).then_inc(ld_small, 16)
            act.dma_start(rbias[:, :], d["router_b"].to_broadcast((P, E))).then_inc(ld_small, 16)
            act.dma_start(abias[:, 0, :], d["gdn_dt_bias"].to_broadcast((P, H))).then_inc(ld_small, 16)
            act.dma_start(abias[:, 1, :], d["gdn_a_log"].to_broadcast((P, H))).then_inc(ld_small, 16)
            act.dma_start(d["out_conf_s"][0][:, 0:CM - DT, :], d["state_conf_conv"][0][:, DT:CM, :]).then_inc(stores, 16)

            act.wait_ge(tr_free[0], 3)
            act.wait_ge(tr_free[1], 3)
            squares(lambda k: xT[:, k, :])
            take_root()
            for c in range(KC):
                j = J_GLU + 4 * (c // 2) + 2 + c % 2
                job_ready(act, j)
                sigmoid(c, proj_bank(j))

            def q_raw(c):
                j = J_QKV + c
                job_ready(act, j)
                if c == 0:
                    act.wait_ge(pads_made, 2)
                    act.wait_ge(tr_free[0], 11)
                A(qkv[:, c, GM:GM + SEQ], proj_bank(j)[:, 0:SEQ], ACT.Copy)
                A(gdn_hist[:, c, :, GM:GM + DT], s4(proj_bank(j)[:, SEQ:T]), ACT.Copy)
                A(gdn_tail[:, c, 0:GM], proj_bank(j)[:, SEQ - GM:SEQ], ACT.Copy)
                A(gdn_tail[:, c, GM:GM + NB * GM].rearrange("p (b s) -> p b s", s=GM),
                  s4(proj_bank(j)[:, SEQ:T])[:, :, DT - GM:DT], ACT.Copy).then_inc(proj_free[j % 4], 1)

            for c in range(4):
                q_raw(c)
            for i in range(2):
                own(A(conf_rows[0:CM + NS, 512 * i:512 * i + 512], bank_rows(act, N_IN_JOBS + i, CM + NS), ACT.Copy),
                    tr_free[(N_IN_JOBS + i) % 2], (N_IN_JOBS + i) // 2 + 1)
            act.dma_start(d["out_conf_p"][0, 0], conf_rows[0:CM, :]).then_inc(st_conf_rows, 16)
            for b in range(NB):
                act.dma_start(d["out_conf_s"][0, b, CM - DT:CM, :],
                              conf_rows[CM + DT * b:CM + DT * (b + 1), :]).then_inc(st_conf_rows, 16)
            for c in range(4, QC):
                q_raw(c)
            act.wait_ge(st_conf_rows, 16 * (1 + NB))

            def z_in(c):
                j = J_Z + c
                job_ready(act, j)
                sigmoid(KC + c, proj_bank(j))
                A(zs[:, c, :], proj_bank(j), ACT.Copy).then_inc(proj_free[j % 4], 1)
            for c in range(6):
                z_in(c)
            act.wait_ge(centred, KC)
            squares(lambda k: cvx[:, k, 0:T])
            for c in range(6, KC):
                z_in(c)
            take_root()
            n0 = N_IN_JOBS + N_CONF_JOBS
            act.wait_ge(conf_made, KC)
            for i in range(N_GDN_JOBS):
                own(A(gdn_rows[0:GM + NB * GM, 512 * i:512 * i + 512], bank_rows(act, n0 + i, GM + NB * GM), ACT.Copy),
                    tr_free[(n0 + i) % 2], (n0 + i) // 2 + 1)
            act.dma_start(d["out_gconv_p"][0, 0], gdn_rows[0:GM, :]).then_inc(st_gdn_rows, 16)
            act.dma_start(d["out_gconv_s"][0].rearrange("b s n -> (b s) n"),
                          gdn_rows[GM:GM + NB * GM, :]).then_inc(st_gdn_rows, 16)
            for k in range(KC):
                act.wait_ge(scaled, k + 1)
                sigmoid(2 * KC + k, cvx[:, k, 0:T], bias=vec("conf_ln_b", k))
            act.wait_ge(st_gdn_rows, 32)
            def qkv_sigmoid(c):
                act.wait_ge(acc_made, c + 1)
                sigmoid(3 * KC + c, bank[6 + c % 2][:, 0:T])
            for i in range(16):
                j = J_GATE + i
                job_ready(act, j)
                g_ = gate_a if i < KC else gate_b
                A(g_[:, i % KC, :], proj_bank(j), ACT.Sigmoid).then_inc(proj_free[j % 4], 1)
                if i:
                    qkv_sigmoid(i - 1)
            for c in range(15, QC):
                qkv_sigmoid(c)

            act.wait_ge(ab_dve, 1)
            own(A(beta, ab[:, :, H:2 * H], ACT.Sigmoid), ab_act)
            own(A(tmp_a, tmp_a, ACT.Exp, scale=-1.0))
            own(A(ea, abias[:, 1, :], ACT.Exp))
            own(A(tmp_a, tmp_a, ACT.Ln, bias=1.0), ab_act)
            def l2(n0, count):
                for n in range(n0, n0 + count):
                    squares(lambda k: qkv[:, n, 0:T], 1)
                root[0] += 1
                act.wait_ge(root_in, root[0])
                A(SC[0:count, 2, :], SC[0:count, 2, :], ACT.Sqrt).then_inc(root_made, 1)
            act.wait_ge(conv_made, QC)
            l2(0, 2 * H)
            act.wait_ge(gc_read, 1)
            own(A(tmp_a, gc, ACT.Exp), ab_act)

            for h in range(H):
                D_ = lambda name: step(act, g_dve, DVE_STEPS, h, name)
                P_ = lambda name: step(act, g_pe, PE_STEPS, h, name)
                flat = lambda n_: G[n_].rearrange("p a b -> p (a b)")
                act.wait_ge(decay_in, h + 1)
                A(flat("decay"), flat("decay"), ACT.Exp).then_inc(decay_exp, 1)
                if h:
                    step(act, g_dve, DVE_STEPS, h - 1, "states")
                A(flat("eg"), bank[0][:, 0:w3], ACT.Exp).then_inc(g_act, 1)
                P_("turned")
                A(flat("x"), bank[6][:, 0:w3], ACT.Copy).then_inc(g_act, 1)
                for l in range(1, LEVELS):
                    for c in "ab":
                        t_ = chain_tiles(c, l)
                        P_(f"y{c}{l}")
                        A(flat("y")[:, P * t_[0]:P * (t_[-1] + 1)], bank[Y_BANK[c]][:, P * t_[0]:P * (t_[-1] + 1)],
                          ACT.Copy).then_inc(g_act, 1)
                    if l == 2:
                        P_("w_s")
                        A(flat("nwt")[:, SEQ:T], bank[5][:, 3 * P:3 * P + NS], ACT.Copy, scale=-1.0).then_inc(g_act, 1)
                    if l == 4:
                        P_("sample")
                        A(w_q_s.rearrange("p b i s -> p (b i s)"), bank[4][:, 0:64], ACT.Copy).then_inc(g_act, 1)
                P_("w")
                A(flat("nwt")[:, P:2 * P], bank[6][:, 3 * P:4 * P], ACT.Copy, scale=-1.0).then_inc(g_act, 1)
                P_("s1")
                A(s_one, bank[7][:, P:2 * P], ACT.Copy).then_inc(g_act, 1)
            step(act, g_dve, DVE_STEPS, H - 1, "states")
            l2(2 * H, H)

            act.wait_ge(proj_done, J_OUT)
            act.dma_start(mem_rows[:, :, :], d["mem_prompt"][0].rearrange("(t p) n -> p t n", p=P)).then_inc(ld_mem, 16)
            act.wait_ge(tr_free[0], 17)
            act.wait_ge(tr_free[1], 17)
            squares(lambda k: memT[:, k, :], KC, ML)
            take_root(ML)
            for j in range(J_OUT + 4, J_OUT + 8):
                job_left(act, j)
            squares(lambda k: xT[:, k, :])
            take_root()
            for p_ in range(8):
                j = J_KV + p_
                job_ready(act, j)
                dst = (mem_k if p_ < 4 else mem_v)[:, :, PCOL * (p_ % 4):PCOL * (p_ % 4 + 1)]
                own(A(dst, bank[j % 4][:, :].rearrange("p (t n) -> p t n", t=2), ACT.Copy), proj_free[j % 4], j // 4 + 1)
                if p_ == 3:
                    act.dma_start(d["out_mem_k"][0, 0].rearrange("(t p) h e -> p t (h e)", p=P), mem_k[:, :, :]).then_inc(stores, 16)
                if p_ == 7:
                    act.dma_start(d["out_mem_v"][0, 0].rearrange("(t p) h e -> p t (h e)", p=P), mem_v[:, :, :]).then_inc(stores, 16)
            for i in range(4):
                read_bank(34 + i, mem_kT[:, 4 * (i % 2):4 * (i % 2) + 4, P * (i // 2):P * (i // 2 + 1)], (4, P))
            for c in range(KC):
                j = J_XQ + c
                job_ready(act, j)
                A(xq[:, c, :], proj_bank(j), ACT.Copy).then_inc(proj_free[j % 4], 1)
            sc = XC ** -0.5 * P ** -0.5
            for u in range(2 * XH + 1):
                if u < 2 * XH:
                    act.wait_ge(max_made, u + 1)
                    if u >= 2:
                        act.wait_ge(pt_done, u - 1)
                    own(A(probs[:, u % 2, :], bank[u % 2][:, 0:ML], ACT.Exp, bias=stat[:, u:u + 1], scale=sc,
                          accum_out=stat[:, 16 + u:17 + u]), exp_made)
                    b = u
                    for i in (1, 3):
                        n = 38 + 4 * b + i
                        if i == 1 and b >= 2:
                            act.wait_ge(s_scores, b - 1)
                        read_bank(n, kT_b[:, b % 2, 4 * (i % 2):4 * (i % 2) + 4, P * (i // 2):P * (i // 2 + 1)], (4, P))
                if u:
                    v = u - 1
                    h, t = v // 2, v % 2
                    act.wait_ge(xo_done, u)
                    A(xo[:, XC * h:XC * h + XC, P * t:P * (t + 1)],
                      bank[v % 2][:, ML:2 * ML].rearrange("p (c n) -> p c n", c=XC), ACT.Copy).then_inc(xo_made, 1)
            act.wait_ge(s_scores, NB)
            A(probs[:, 0, :], bank[6][:, 0:ML], ACT.Copy).then_inc(sT_made, 1)
            u = 2 * XH
            act.wait_ge(max_made, u + 1)
            own(A(probs[:, 1, :], bank[7][:, 0:ML], ACT.Exp, bias=stat[:, u:u + 1], scale=sc,
                  accum_out=stat[:, 16 + u:17 + u]), exp_made)
            act.dma_start(b2_rows, d["moe_b2"][0]).then_inc(ld_b2, 16)
            act.wait_ge(v_used, NB)
            A(xo[:, :, SEQ:T], bank[5][:, 0:KC * NS].rearrange("p (c n) -> p c n", c=KC), ACT.Copy).then_inc(xo_made, 1)
            for j in range(J_XO + 4, J_XO + 8):
                job_left(act, j)
            squares(lambda k: xT[:, k, :])
            take_root()
            for i in (1, 3, 5):
                r = TROWS[i // 2]
                act.wait_ge(tr_done, 70 + i + 1)
                own(A(tok_hi[0:r, i // 2, 512:1024], bank[4 + i % 2][0:r, :], ACT.Copy), hi_made)
            act.wait_ge(max_made, 2 * XH + 2)
            own(A(gates_, gates_, ACT.Exp), exp_made)

            def extra(e, first):
                n, r0 = load_rounds(act, e)
                with act.If(n > 0):
                    with act.Fori(0, n) as j:
                        r = act.snap(r0 + j)
                        act.wait_ge(ex_pe, r * XP + XPE["gather"])
                        A(flat3(ex_xg_lo), bank[3][:, 0:KC * CAP], ACT.Copy).then_inc(ex_actv, 1)
                        act.wait_ge(ex_dve, r * XD + XDVE["gate"])
                        A(sig_, gate_, ACT.Sigmoid, scale=1.702).then_inc(ex_actv, 1)
                        act.wait_ge(ex_pe, r * XP + XPE["gates"])
                        A(ex_cg_hi, bank[5][0:CAP, 0:T], ACT.Copy).then_inc(ex_actv, 1)
                        act.wait_ge(ex_pe, r * XP + XPE["output"])
                        for i in range(2):
                            last = A(ex_y_hi[:, 512 * i:512 * i + 512], bank[3 * i][0:CAP, :], ACT.Copy)
                        last.then_inc(ex_actv, 1)

            def results(e):
                act.wait_ge(w_free, e * EPI)
                at_least(act, scat_done, e * 8 - 8)
                for i in range(2):
                    last = A(y_hi[:, 512 * i:512 * i + 512], bank[6 + i][0:CAP, :], ACT.Copy)
                last.then_inc(yhi_evac, 1)

            def gates_in(e):
                act.wait_ge(cg_done, e)
                A(cg_hi, bank[5][0:CAP, 0:T], ACT.Copy).then_inc(cg_evac, 1)

            def expert(e, first, last_one):
                if not first:
                    results(e)
                    gates_in(e)
                act.wait_ge(gate_made, e + 1)
                A(sig_, gate_, ACT.Sigmoid, scale=1.702).then_inc(sigm_made, 1)
                if not last_one:
                    act.wait_ge(xg_done, e + 2)
                    A(flat3(xg_lo), bank[3][:, 0:KC * CAP], ACT.Copy).then_inc(xlo_evac, 1)

            act.wait_ge(rounds_made, 1)
            act.wait_ge(xg_done, 1)
            A(flat3(xg_lo), bank[3][:, 0:KC * CAP], ACT.Copy).then_inc(xlo_evac, 1)
            for e in (0, 1):
                extra(e, e == 0)
                expert(e, e == 0, False)
            with act.Fori(2, E - 1) as e:
                extra(e, False)
                expert(e, False, False)
            extra(E - 1, False)
            expert(E - 1, False, True)
            results(E)
            gates_in(E)
            act.wait_ge(scat_add, 8 * E)
            squares(lambda k: xT[:, k, :])
            take_root()
            for i in (1, 3, 5):
                r = TROWS[i // 2]
                act.wait_ge(tr_done, 76 + i + 1)
                A(y_rows[0:r, i // 2, 512:1024], bank[4 + i % 2][0:r, :], ACT.Copy).then_inc(tr_free[1], 1)
            act.wait_ge(tr_free[0], 41)
            act.wait_ge(tr_free[1], 41)
            act.dma_start(d["out_y_p"][0].rearrange("(t p) n -> p t n", p=P), y_rows[:, 0:2, :]).then_inc(stores, 16)
            act.dma_start(d["out_y_s"].rearrange("b s n -> (b s) n"), y_rows[0:NS, 2, :]).then_inc(stores, 16)
            act.wait_ge(stores, 16 * 5)
            act.wait_ge(st_conf_rows, 16 * (1 + NB))
            act.wait_ge(st_gdn_rows, 32)
            act.wait_ge(st_out, 16 * H)
            act.wait_ge(st_prompt, 16 * H)

        @block.vector
        def _(dve):
            own = chain(dve, dve_self)
            V = nc.vector
            tt, ts, stt, cp = V.tensor_tensor, V.tensor_scalar, V.scalar_tensor_tensor, V.tensor_copy
            sq, root, norm = [0], [0], [0]

            def norm_root(b, scale, eps, n=KC, cols_=T):
                sq[0] += n
                root[0] += 1
                dve.wait_ge(sq_used, sq[0])
                ts(SC[:, 2, 0:cols_], bank[b][:, 0:cols_], scale, eps, ALU.mult, ALU.add).then_inc(root_in, 1)
                dve.wait_ge(root_made, root[0])
                own(V.reciprocal(SC[:, 2, 0:cols_], SC[:, 2, 0:cols_]))

            def rms(src, gain, dst, b=6, cols_=T):
                norm_root(b, 1.0 / D, 1e-6, KC, cols_)
                norm[0] += 1
                for k in range(KC):
                    ins = stt(dst(k), src(k), vec(gain, k), SC[:, 2, 0:cols_], ALU.mult, ALU.mult)
                    if k == KC - 1:
                        own(ins, norm_made, norm[0])

            def read_bank(n, dst, shape, rows=P, w=512):
                dve.wait_ge(tr_done, n + 1)
                own(cp(dst, view(4 + n % 2, rows, w, shape)), tr_free[n % 2], n // 2 + 1)

            for n, (kind, srcs, dst, shape) in enumerate(in_jobs):
                read_bank(n, dst, shape, P, sum(r for _, r in srcs))
            rms(lambda k: xT[:, k, :], "norm_mix", lambda k: hT[:, k, :])
            for c in range(KC):
                j = J_GLU + 4 * (c // 2) + c % 2
                job_ready(dve, j)
                dve.wait_ge(sig_made, c + 1)
                if c == 0:
                    dve.wait_ge(pads_made, 1)
                own(tt(cvx[:, c, CM:CM + SEQ], proj_bank(j)[:, 0:SEQ], sg[:, c % 2, 0:SEQ], ALU.mult))
                own(tt(conf_new(c), s4(proj_bank(j)[:, SEQ:T]), s4(sg[:, c % 2, SEQ:T]), ALU.mult),
                    proj_free[j % 4], j // 4 + 1)
                own(cp(conf_tail[:, c, 0:CM], cvx[:, c, SEQ:CM + SEQ]), proj_free[(j + 2) % 4], (j + 2) // 4 + 1)
                own(cp(s4(conf_tail[:, c, CM:CM + NS]), conf_new(c)), conf_tail_made)
            for c in range(0, KC, 2):
                pair = [(c + i, bank[6 + i][:, 0:SEQ]) for i in range(2)]
                for k, acc in pair:
                    own(ts(acc, cvx[:, k, 0:SEQ], conf_w(0, k), vec("conf_conv_b", k), ALU.mult, ALU.add), lag=1)
                for j in range(1, CW):
                    for k, acc in pair:
                        own(stt(acc, cvx[:, k, j:j + SEQ], conf_w(j, k), acc, ALU.mult, ALU.add), lag=1)
                for k, acc in pair:
                    own(cp(cvx[:, k, 0:SEQ], acc))
            dve.wait_ge(conf_s_made, 1)
            for c in range(KC):
                own(ts(s4(cvx[:, c, SEQ:T]), conf_acc[:, c], vec("conf_conv_b", c), None, ALU.add), conf_made)
            dve.wait_ge(mean_done, 1)
            own(ts(SC[:, 2, :], bank[6][:, 0:T], 1.0 / D, None, ALU.mult), mean_read)
            for k in range(KC):
                own(tt(cvx[:, k, 0:T], cvx[:, k, 0:T], SC[:, 2, :], ALU.subtract), centred, wait=False)
            norm_root(6, 1.0 / D, 1e-5)

            def silu(k):
                dve.wait_ge(sig_made, 2 * KC + k + 1)
                if k == KC - 1:
                    norm[0] += 1
                own(stt(cvx[:, k, 0:T], cvx[:, k, 0:T], vec("conf_ln_b", k), sg[:, k % 2, :], ALU.add, ALU.mult),
                    silu_made if k < KC - 1 else norm_made, norm[0] if k == KC - 1 else None, wait=(k == KC - 1))
            for k in range(KC):
                own(stt(cvx[:, k, 0:T], cvx[:, k, 0:T], vec("conf_ln_g", k), SC[:, 2, :], ALU.mult, ALU.mult), scaled,
                    wait=False)
                if k:
                    silu(k - 1)
            silu(KC - 1)

            for j in range(J_QKV + QC - 4, J_QKV + QC):
                job_left(dve, j)

            def swish(c):
                dve.wait_ge(sig_made, 3 * KC + c + 1)
                own(tt(qkv[:, c, 0:T], bank[6 + c % 2][:, 0:T], sg[:, c % 2, :], ALU.mult), conv_made)

            def gate_conf(c):
                j = J_PW2 + c
                job_ready(dve, j)
                own(stt(gate_b[:, c, :], proj_bank(j), vec("conf_pw2_b", c), gate_b[:, c, :], ALU.add, ALU.mult),
                    proj_free[j % 4], j // 4 + 1)

            for c in range(QC):
                acc = bank[6 + c % 2][:, 0:SEQ]
                acs = s4(bank[6 + c % 2][:, SEQ:T])
                own(ts(acc, qkv[:, c, 0:SEQ], gdn_w(0, c), None, ALU.mult), lag=1)
                own(ts(acs, gdn_hist[:, c, :, 0:DT], gdn_w(0, c), None, ALU.mult), lag=1)
                for i in range(1, GC):
                    own(stt(acc, qkv[:, c, i:i + SEQ], gdn_w(i, c), acc, ALU.mult, ALU.add), lag=1)
                    if i < GC - 1:
                        own(stt(acs, gdn_hist[:, c, :, i:i + DT], gdn_w(i, c), acs, ALU.mult, ALU.add), lag=1)
                    else:
                        own(stt(acs, gdn_hist[:, c, :, i:i + DT], gdn_w(i, c), acs, ALU.mult, ALU.add), acc_made, wait=False)
                if c:
                    swish(c - 1)
                if c > QC - KC:
                    gate_conf(c - 1 - (QC - KC))
                if c == QC - KC:
                    dve.wait_ge(ab_done, 1)
                    dve.wait_ge(masks_made, 2)
                    own(cp(ab[:, 0:2, :].rearrange("p t n -> p (t n)"), bank[4][:, 0:32]))
                    own(cp(ab[0:NS, 2, :], bank[4][0:NS, 32:48]))
                    own(tt(tmp_b, ab[:, :, 0:H], abias[:, 0:1, :].to_broadcast((P, TT, H)), ALU.add))
                    own(stt(tmp_a, tmp_b, -1.0, tmp_b, ALU.mult, ALU.max), ab_dve)
            swish(QC - 1)
            gate_conf(KC - 1)

            def l2(n0, count, scale, eps, spread_to):
                sq[0] += count
                root[0] += 1
                for r, f in spread_to:
                    own(ts(row_sel[0:count, r, :], ident[0:count, r].unsqueeze(2).to_broadcast((count, r.stop - r.start, P)),
                           f, None, ALU.mult))
                dve.wait_ge(sq_used, sq[0])
                ts(SC[0:count, 2, :], bank[6][0:count, 0:T], scale, eps, ALU.mult, ALU.add).then_inc(root_in, 1)
                dve.wait_ge(root_made, root[0])
                own(V.reciprocal(SC[0:count, 2, :], SC[0:count, 2, :]), l2_inv)

            l2(0, 2 * H, 1.0, 1e-6, ((slice(0, H), P ** -0.5), (slice(H, 2 * H), 1.0)))
            for n in range(2 * H):
                dve.wait_ge(l2_done, n + 1)
                own(tt(qkv[:, n, 0:T], qkv[:, n, 0:T], bank[4 + n % 2][:, 0:T], ALU.mult), l2_read, wait=False)
            for b in (2, 3):
                own(V.memset(bank[b][:, 2 * P:3 * P], 0.0), banks_clear if b == 3 else dve_self)
            dve.wait_ge(ab_act, 2)
            own(stt(tmp_b, tmp_b, 0.0, tmp_a, ALU.max, ALU.add))
            own(stt(gl, tmp_b, -1.0, ea.unsqueeze(1).to_broadcast((P, TT, H)), ALU.mult, ALU.mult), gl_made)
            dve.wait_ge(gc_done, 1)
            own(cp(gc, bank[7][:, 0:24].rearrange("p (t n) -> p t n", t=TT)), gc_read)
            dve.wait_ge(ab_act, 3)
            own(tt(kb_s, tmp_a, beta, ALU.mult))

            def tile_rows(t):
                return slice(0, P if t < 2 else NS)

            fl = lambda n_: G[n_].rearrange("p a b -> p (a b)")

            def decay_start(h):
                dve.wait_ge(rows_done, h + 1)
                for t in range(TT):
                    last = ts(G["decay"][:, t, :], bank[0][:, P * t:P * (t + 1)], gc[:, t, h:h + 1], 0.0, ALU.subtract, ALU.min)
                own(last, decay_in)

            def key_products(h):
                dve.wait_ge(scores_rows, h + 1)
                own(cp(fl("mt"), bank[2][:, 0:w3]))
                own(tt(fl("mt"), bank[1][:, 0:w3], fl("mt"), ALU.mult))

            def inverse_start(h):
                dve.wait_ge(decay_exp, h + 1)
                own(tt(fl("mt"), fl("mt"), fl("decay"), ALU.mult))
                own(tt(G["ct0"], G["mt"], level_mask[:, 0:1, :].to_broadcast((P, TT, P)), ALU.mult))
                own(tt(G["xt"], ident[:, :].unsqueeze(1).to_broadcast((P, TT, P)), G["ct0"], ALU.subtract), xt_start)

            def columns(h, t):
                r = tile_rows(t)
                kd_s = G["decay"][:, t, P - 1:P] if t < 2 else k_last
                kt, vt = bank[4][r, P * t:P * (t + 1)], bank[5][r, P * t:P * (t + 1)]
                ts(G["kbg"][r, t, :], kt, kb_s[r, t, h:h + 1], None, ALU.mult)
                ts(G["kd"][r, t, :], kt, kd_s, None, ALU.mult)
                return ts(G["vb"][r, t, :], vt, beta[r, t, h:h + 1], None, ALU.mult)

            decay_start(0)
            key_products(0)
            inverse_start(0)
            for h in range(H):
                P_ = lambda name: step(dve, g_pe, PE_STEPS, h, name)
                A_ = lambda name: step(dve, g_act, ACT_STEPS, h, name)
                own(tt(G["decay"][:, 0:2, :], G["decay"][:, 0:2, :], causal[:, 0:1, :].to_broadcast((P, 2, P)), ALU.mult),
                    wait=False)
                own(tt(G["decay"][:, 2, :], G["decay"][:, 2, :], causal[:, 1, :], ALU.mult))
                own(tt(fl("pt"), bank[3][:, 0:w3], fl("decay"), ALU.mult), g_dve, wait=False)
                own(tt(k_last_p, G["decay"][0:NS, 2, 0:NS], last_of[:, :], ALU.mult))
                own(V.tensor_reduce(k_last, k_last_p, AX, ALU.add))
                dve.wait_ge(kv_turned, h + 1)
                for t in range(TT):
                    last = columns(h, t)
                own(last, g_dve, wait=False)
                for l in range(1, LEVELS):
                    for c in "ab":
                        t_ = chain_tiles(c, l)
                        s_ = slice(P * t_[0], P * (t_[-1] + 1))
                        P_(f"z{c}{l}")
                        if l < LEVELS - 1:
                            own(tt(fl("x")[:, s_], fl("x")[:, s_], bank[X_BANK[c]][:, s_], ALU.subtract),
                                g_dve, wait=False)
                        own(tt(fl("xt")[:, s_], fl("xt")[:, s_], bank[Z_BANK[c]][:, s_], ALU.subtract),
                            g_dve, wait=False)
                    if l == 2:
                        own(tt(fl("qg")[:, 0:T], qkv[:, h, 0:T], fl("eg")[:, 0:T], ALU.mult))
                        own(cp(w_q[:, :, 1, :], s4(fl("qg")[:, SEQ:T])))
                        A_("nwt_s")
                        own(cp(w_q[:, :, 0, :], s4(fl("nwt")[:, SEQ:T])), g_dve)
                    if l == 4:
                        A_("ws")
                        own(tt(s4(vnT_s), s4(bank[5][:, 0:NS]), w_q_s[:, :, 0, :], ALU.add), g_dve)
                    if l == 5:
                        P_("vnt")
                        own(cp(vn_s, bank[5][0:NS, P:2 * P]), g_dve)
                        own(tt(v_wide, vn_s.unsqueeze(1).to_broadcast((NS, NB, P)),
                               batch_of[:, :].unsqueeze(2).to_broadcast((NS, NB, P)), ALU.mult), g_dve)
                P_("vn0")
                own(cp(vn0, bank[7][:, 0:P]), g_dve)
                if h + 1 < H:
                    decay_start(h + 1)
                    key_products(h + 1)
                P_("vn1")
                own(cp(vn1, bank[7][:, 2 * P:3 * P]), g_dve)
                if h + 1 < H:
                    inverse_start(h + 1)
                P_("out")
                own(cp(qkv[:, 2 * H + h, 0:SEQ], bank[6][:, 0:SEQ]))
                own(tt(s4(qkv[:, 2 * H + h, SEQ:T]), s4(bank[6][:, SEQ:T]), w_q_s[:, :, 1, :], ALU.add))
                if h:
                    dve.wait_ge(st_prompt, 16 * h)
                own(stt(s_fin, s_one, G["eg"][:, 1, P - 1:P], bank[7][:, 3 * P:4 * P], ALU.mult, ALU.add), g_dve)
                dve.wait_ge(decayed_states, h + 1)
                for i in range(2):
                    s_ = states[:, 4 * i:4 * i + 4, :].rearrange("p b n -> p (b n)")
                    own(tt(s_, s_, bank[4 + i][:, :], ALU.add), g_dve if i else dve_self)

            dve.wait_ge(st_out, 16 * H)
            dve.wait_ge(st_prompt, 16 * H)
            dve.wait_ge(z_made, KC)
            l2(2 * H, H, 1.0 / P, 1e-6, ((slice(0, H), 1.0),))
            for n in range(H):
                m = 2 * H + n
                dve.wait_ge(l2_done, m + 1)
                own(stt(qkv[:, m, 0:T], qkv[:, m, 0:T], vec("gdn_norm", 0), bank[4 + n % 2][:, 0:T], ALU.mult, ALU.mult),
                    l2_read)
                own(tt(qkv[:, m, 0:T], qkv[:, m, 0:T], zs[:, n, :], ALU.mult), o_made, wait=False)
            for c in range(KC):
                j = J_O + c
                job_ready(dve, j)
                own(tt(gate_a[:, c, :], proj_bank(j), gate_a[:, c, :], ALU.mult))
                own(tt(gate_a[:, c, :], gate_a[:, c, :], gate_b[:, c, :], ALU.add), proj_free[j % 4], j // 4 + 1)

            def residual(j0):
                for c in range(KC):
                    j = j0 + c
                    job_ready(dve, j)
                    own(tt(xT[:, c, :], xT[:, c, :], proj_bank(j), ALU.add), proj_free[j % 4], j // 4 + 1)
            residual(J_OUT)
            for i in range(4):
                read_bank(30 + i, memT[:, 4 * (i % 2):4 * (i % 2) + 4, P * (i // 2):P * (i // 2 + 1)], (4, P))
            rms(lambda k: memT[:, k, :], "norm_mem", lambda k: memT[:, k, :], 7, ML)
            rms(lambda k: xT[:, k, :], "norm_xa", lambda k: hT[:, k, :])
            sc = XC ** -0.5 * P ** -0.5

            def row_max(u, b):
                own(V.tensor_reduce(stat[:, 32 + u:33 + u], bank[b][:, 0:ML], AX, ALU.max))
                own(ts(stat[:, u:u + 1], stat[:, 32 + u:33 + u], -sc, None, ALU.mult), max_made)

            def divide(u, p_):
                dve.wait_ge(exp_made, u + 1)
                own(V.reciprocal(stat[:, 16 + u:17 + u], stat[:, 16 + u:17 + u]))
                own(ts(probs[:, p_, :], probs[:, p_, :], stat[:, 16 + u:17 + u], None, ALU.mult), probs_made)

            def values_low(b):
                n = NP_CACHE + NB + b
                dve.wait_ge(w_here[n % RING], 16 * (n // RING + 1))
                if b >= 2:
                    dve.wait_ge(v_used, b - 1)
                tt(v_lo[b % 2], ring[:, n % RING, :], high(ring[:, n % RING, :]), ALU.subtract).then_inc(v_lo_made, 1)

            NU = 2 * XH
            for u in range(NU + 1):
                if u < NU:
                    dve.wait_ge(scores_done, u + 1)
                    row_max(u, u % 2)
                    b = u
                    for i in (0, 2):
                        if i == 0 and b >= 2:
                            dve.wait_ge(s_scores, b - 1)
                        read_bank(38 + 4 * b + i, kT_b[:, b % 2, 0:4, P * (i // 2):P * (i // 2 + 1)], (4, P))
                if u:
                    v = u - 1
                    divide(v, v % 2)
                    dve.wait_ge(pt_done, v + 1)
                    if v >= 2:
                        dve.wait_ge(xo_done, v - 1)
                    own(cp(probsT[:, v % 2], bank[2 + v % 2][:, 0:ML].rearrange("p (m n) -> p m n", m=2)), pt_made)
            values_low(0)
            values_low(1)
            dve.wait_ge(scores_done, NU + 1)
            row_max(NU, 7)
            divide(NU, 1)
            dve.wait_ge(pt_done, NU + 1)
            pT_sum = bank[6][:, 0:ML].rearrange("p (m n) -> p m n", m=2)
            own(cp(pT_hi, pT_sum))
            own(tt(pT_lo, pT_sum, pT_hi, ALU.subtract), pt_made)
            for b in range(2, NB):
                values_low(b)
            residual(J_XO)
            rms(lambda k: xT[:, k, :], "norm_ffn", lambda k: hT[:, k, :])
            for i in (0, 2, 4):
                r = TROWS[i // 2]
                dve.wait_ge(tr_done, 70 + i + 1)
                own(cp(tok_hi[0:r, i // 2, 0:512], bank[4 + i % 2][0:r, :]))
                own(tt(tok_lo[0:r, i // 2, 0:512], bank[4 + i % 2][0:r, :], tok_hi[0:r, i // 2, 0:512], ALU.subtract),
                    tr_free[0], (70 + i) // 2 + 1)
                dve.wait_ge(hi_made, i // 2 + 1)
                own(tt(tok_lo[0:r, i // 2, 512:D], bank[5][0:r, :], tok_hi[0:r, i // 2, 512:D], ALU.subtract),
                    tr_free[1], (70 + i) // 2 + 1)
            own(V.memset(logits, 0.0))
            own(V.memset(gates_, 0.0))
            own(V.memset(top, 0.0))
            dve.wait_ge(logits_done, 1)
            for t in range(TT):
                r = TROWS[t]
                own(tt(logits[0:r, t, :], bank[6][0:r, E * t:E * (t + 1)], rbias[0:r, :], ALU.add))
                own(V.max(top[0:r, t, :], logits[0:r, t, :]))
            fourth = top[:, :, TOPK - 1:TOPK].to_broadcast((P, TT, E))
            first_ = top[:, :, 0:1].to_broadcast((P, TT, E))
            own(tt(chosen, logits, fourth, ALU.is_gt))
            own(tt(run_a, logits, fourth, ALU.is_equal))
            own(cp(ties, run_a))
            own(V.tensor_reduce(need, chosen, AX, ALU.add))
            own(ts(need, need, -1.0, float(TOPK), ALU.mult, ALU.add))

            def running(a, b, n, rows):
                s = 1
                while s < n:
                    own(cp(b[rows, :, 0:s], a[rows, :, 0:s]))
                    own(tt(b[rows, :, s:n], a[rows, :, s:n], a[rows, :, 0:n - s], ALU.add))
                    a, b = b, a
                    s *= 2
                return a
            run = running(run_a, run_b, E, slice(0, P))
            own(tt(run, run, need.unsqueeze(2).to_broadcast((P, TT, E)), ALU.is_le))
            own(tt(run, run, ties, ALU.mult))
            own(tt(chosen, chosen, run, ALU.add), chosen_made)
            own(tt(gates_, logits, first_, ALU.subtract), max_made)
            dve.wait_ge(exp_made, NU + 2)
            own(tt(gates_, gates_, chosen, ALU.mult))
            own(V.tensor_reduce(need, gates_, AX, ALU.add))
            own(V.reciprocal(need, need))
            own(tt(gates_, gates_, need.unsqueeze(2).to_broadcast((P, TT, E)), ALU.mult), gates_made)
            dve.wait_ge(gates_T_done, 1)
            own(cp(gates_T, bank[0][0:E, 0:T]), gates_T_made)
            own(V.memset(place, -1.0))
            own(V.memset(ex_off, float(CAP)))
            dve.wait_ge(stores, 48)
            dve.wait_ge(counts_done, 1)
            for t in range(TT):
                r = TROWS[t]
                own(tt(place[0:r, t, :], bank[7][0:r, E * t:E * (t + 1)], chosen[0:r, t, :], ALU.mult))
                own(ts(place[0:r, t, :], place[0:r, t, :], -1.0, None, ALU.add))
            cnt = bank[7][0:1, E * TT:E * (TT + 1)]
            own(ts(rounds_f[:, 0, :], cnt, float(CAP), None, ALU.is_gt))
            for j in range(2, (T - 1) // CAP + 1):
                own(stt(rounds_f[:, 0, :], cnt, float(CAP * j), rounds_f[:, 0, :], ALU.is_gt, ALU.add))
            own(cp(rounds_f[:, 1, :], rounds_f[:, 0, :]))
            r_ = running(rounds_f[:, 1:2, :], rounds_f[:, 2:3, :], E, slice(0, 1))
            own(tt(rounds_f[:, 3:4, :], r_, rounds_f[:, 0:1, :], ALU.subtract))
            own(cp(rounds[:, 0, :], rounds_f[:, 0, :]))
            own(cp(rounds[:, 1, :], rounds_f[:, 3, :]), rounds_made)

            for c in range(KC):
                dve.wait_ge(b2_done, c + 1)
                own(tt(xT[:, c, :], xT[:, c, :], bank[4 + c % 2][:, 0:T], ALU.add), b2_added)

            def one_hot(dst, place_, t):
                r = TROWS[t]
                return ts(dst[0:r, t, :], slot_id[0:r, :], place_(t, r), None, ALU.is_equal)

            def gate_hot(dst, place_, e, t):
                r = TROWS[t]
                return ts(dst[0:r, t, :], slot_id[0:r, :], place_(t, r), gates_[0:r, t, bass.ds(e, 1)],
                          ALU.is_equal, ALU.mult)

            def bias1(e, lin):
                return prm[:, bass.ds(e * 16 + (B1O + 8 * lin), 8)].unsqueeze(2).to_broadcast((P, FC, CAP))

            def swiglu(e, link, first_sig, sig_wait, act_out, last_sig):
                hb = lambda i: bank[1 + i][:, 0:FC * CAP].rearrange("p (f n) -> p f n", f=FC)
                g3, l3 = gate_.rearrange("p (f n) -> p f n", f=FC), lin_.rearrange("p (f n) -> p f n", f=FC)
                link(tt(g3, hb(0), bias1(e, 0), ALU.add))
                link(ts(gate_, gate_, 7.0, None, ALU.min), first_sig)
                link(tt(l3, hb(1), bias1(e, 1), ALU.add))
                link(ts(lin_, lin_, 7.0, -7.0, ALU.min, ALU.max))
                link(stt(lin_, lin_, 1.0, gate_, ALU.add, ALU.mult))
                sig_wait()
                link(tt(act_out.rearrange("p f n -> p (f n)"), lin_, sig_, ALU.mult), last_sig)

            def low(e, k):
                w = ring[:, w_slot(k), :]
                dve.wait_ge(w_here[w_slot(k)], e * 16 + w_count(k))
                tt(w_lo[k], w, high(w), ALU.subtract).then_inc(lo_made, 1)

            def extra(e, first):
                n, r0 = load_rounds(dve, e)
                with dve.If(n > 0):
                    pc = lambda t, r: ex_place[0:r, t:t + 1]
                    c0 = [0]
                    with dve.Fori(0, n) as j:
                        r = dve.snap(r0 + j)

                        def link(ins, *_):
                            c0[0] += 1
                            ins.then_inc(ex_dve, 1)
                            dve.wait_ge(ex_dve, r * XD + c0[0])
                        link(ts(ex_place, place[:, :, bass.ds(e, 1)].rearrange("p t o -> p (t o)"),
                                ex_off[:, bass.ds(e, 1)], None, ALU.subtract))
                        for t in range(TT):
                            link(one_hot(ex_onehot, pc, t))
                        assert c0[0] == XDVE["onehot"]
                        for t in range(TT):
                            link(gate_hot(ex_pg, pc, e, t))
                        link(ts(ex_off[:, bass.ds(e, 1)], ex_off[:, bass.ds(e, 1)], float(CAP), None, ALU.add))
                        dve.wait_ge(ex_pe, r * XP + XPE["gather"])
                        link(cp(flat3(ex_xg_hi), bank[0][:, 0:KC * CAP]))
                        assert c0[0] == XDVE["xg"]
                        dve.wait_ge(ex_pe, r * XP + XPE["hidden"])
                        swiglu(e, link, None, lambda: dve.wait_ge(ex_actv, r * XA + XACT["sig"]), ex_act, None)
                        assert c0[0] == XDVE["act"] and XDVE["gate"] == XDVE["act"] - 4
                        dve.wait_ge(ex_actv, r * XA + XACT["cg"])
                        link(tt(ex_cg_lo, bank[5][0:CAP, 0:T], ex_cg_hi, ALU.subtract))
                        dve.wait_ge(ex_actv, r * XA + XACT["y"])
                        for i in range(2):
                            c_ = slice(512 * i, 512 * i + 512)
                            link(tt(ex_y_lo[:, c_], bank[3 * i][0:CAP, :], ex_y_hi[:, c_], ALU.subtract))
                        assert c0[0] == XDVE["y"]
                        for c in range(KC):
                            dve.wait_ge(ex_pe, r * XP + XPE["scatter"] + c)
                            link(tt(xT[:, c, :], xT[:, c, :], bank[4 + c % 2][:, 0:T], ALU.add))
                        assert c0[0] == XD

            N_E = 4

            def hot_gates(e):
                at_least(dve, cg_done, e - 1)
                for t in range(TT):
                    last = gate_hot(pg, lambda t, r: place[0:r, t, bass.ds(e - 1, 1)], e - 1, t)
                last.then_inc(pg_made, 1)

            def y_low(e):
                dve.wait_ge(yhi_evac, e)
                for i in range(2):
                    c_ = slice(512 * i, 512 * i + 512)
                    last = tt(y_lo[:, c_], bank[6 + i][0:CAP, :], y_hi[:, c_], ALU.subtract)
                last.then_inc(ylo_made, 1)

            def cg_low(e):
                dve.wait_ge(cg_evac, e)
                tt(cg_lo, bank[5][0:CAP, 0:T], cg_hi, ALU.subtract).then_inc(cgl_made, 1)

            def add_in(e):
                for c in range(KC):
                    dve.wait_ge(scat_done, e * 8 - 8 + (c + 1))
                    tt(xT[:, c, :], xT[:, c, :], bank[4 + c % 2][:, 0:T], ALU.add).then_inc(scat_add, 1)

            def expert(e, first, last_one, at_):
                n = [0]

                def link(ins, s=None, v=None):
                    if s is None:
                        n[0] += 1
                        ins.then_inc(ex_self, 1)
                        dve.wait_ge(ex_self, at_ + n[0])
                    else:
                        ins.then_inc(s, 1)
                        dve.wait_ge(s, v)
                if not first:
                    hot_gates(e)
                if not last_one:
                    dve.wait_ge(xg_done, e + 1)
                    for t in range(TT):
                        last = one_hot(onehot, lambda t, r: place[0:r, t, bass.ds(e + 1, 1)], t)
                    last.then_inc(p_made, 1)
                if not first:
                    y_low(e)
                dve.wait_ge(w_free, e * EPI + KC)

                def swi_link(ins, s=None):
                    link(ins, s, None if s is None else e + 1)
                swiglu(e, swi_link, gate_made, lambda: dve.wait_ge(sigm_made, e + 1), act_, act_made)
                if not first:
                    cg_low(e)
                if not last_one:
                    dve.wait_ge(xg_done, e + 2)
                    cp(flat3(xg_hi), bank[0][:, 0:KC * CAP]).then_inc(xg_evac, 1)
                if not first:
                    add_in(e)
                if not last_one:
                    for k in range(KC):
                        low(e + 1, k)
                assert n[0] == N_E, n[0]

            for t in range(TT):
                ins = one_hot(onehot, lambda t, r: place[0:r, t, 0:1], t)
                own(ins, p_made if t == 2 else dve_self)
            dve.wait_ge(xg_done, 1)
            own(cp(flat3(xg_hi), bank[0][:, 0:KC * CAP]), xg_evac)
            for e in (0, 1):
                extra(e, e == 0)
                expert(e, e == 0, False, e * N_E)
            with dve.Fori(2, E - 1) as e:
                extra(e, False)
                expert(e, False, False, e * N_E)
            extra(E - 1, False)
            expert(E - 1, False, True, (E - 1) * N_E)
            hot_gates(E)
            y_low(E)
            cg_low(E)
            add_in(E)
            rms(lambda k: xT[:, k, :], "norm_final", lambda k: hT[:, k, :])
            for i in (0, 2, 4):
                r = TROWS[i // 2]
                dve.wait_ge(tr_done, 76 + i + 1)
                own(cp(y_rows[0:r, i // 2, 0:512], bank[4 + i % 2][0:r, :]), tr_free[0], (76 + i) // 2 + 1)


INS = ["x_prompt", "x_sample", "mem_prompt", "state_gdn", "state_gdn_conv", "state_conf_conv", "cache_mem_k",
       "cache_mem_v", "norm_mix", "w_in", "gdn_conv_w", "gdn_a_log", "gdn_dt_bias", "gdn_norm", "gdn_o",
       "conf_conv_w", "conf_conv_b", "conf_ln_g", "conf_ln_b", "conf_pw2", "conf_pw2_b", "w_out", "norm_xa",
       "norm_mem", "xa_q", "xa_kv", "xa_o", "norm_ffn", "router_w", "router_b", "moe_w1", "moe_b1", "moe_w2",
       "moe_b2", "norm_final"]
OUTS = [("y_p", (1, SEQ, D)), ("y_s", (NB, DT, D)), ("state_p", (1, 1, H, P, P)), ("gconv_p", (1, 1, GM, QC * P)),
        ("conf_p", (1, 1, CM, D)), ("mem_k", (1, 1, ML, XH, XC * P)), ("mem_v", (1, 1, ML, XH, XC * P)),
        ("state_s", (1, NB, H, P, P)), ("gconv_s", (1, NB, GM, QC * P)), ("conf_s", (1, NB, CM, D))]


def kernel(**inputs):
    import numpy as np
    import concourse.bacc as bacc
    from concourse.bass_utils import run_bass_kernel_spmd

    nc = bacc.Bacc("TRN2", target_bir_lowering=False, num_devices=1)
    arrays, d = {}, {}
    for name in INS:
        arrays[f"in_{name}"] = np.ascontiguousarray(inputs[name])
        d[name] = nc.dram_tensor(f"in_{name}", arrays[f"in_{name}"].shape, F32, kind="ExternalInput").ap()
    for name, shape in OUTS:
        d[f"out_{name}"] = nc.dram_tensor(f"out_{name}", shape, F32, kind="ExternalOutput").ap()
    build(nc, d)
    r = run_bass_kernel_spmd(nc, [arrays], core_ids=[0])
    return tuple(r.results[0][f"out_{name}"] for name, _ in OUTS)
```
